# Optimizing a Trainium2 kernel written in Bass

```python
import math
import jax, jax.numpy as jnp
from jax import lax
import numpy as np

D_MODEL = 1024
BATCH = 1
SEQ = 512
DEPTH = 2
DEC_BATCH = 8
DEC_SEQ = 8
PAST_LEN = 4096
PAGE_SIZE = 128

N_MIXERS = 2
N_HGRN_LAYERS = (DEPTH + 1) // 2
N_S5_LAYERS = DEPTH // 2
HGRN_HEAD_DIM = 128
HGRN_HEADS = D_MODEL // HGRN_HEAD_DIM
HGRN_CHUNK = 32
S5_GROUP_CH = 16
S5_GROUPS = D_MODEL // S5_GROUP_CH
S5_STATE = 64
S5_DT_MIN = 1e-3
S5_DT_MAX = 1e-1
D_FF = 2816
MACARON_SCALE = 0.5
EPS = 1e-6
GATE_FLOOR = 1e-30

kernel_name = "hgrn2_s5_macaron_hybrid_step"

def _rmsnorm(x, gain):
    xf = x.astype(jnp.float32)
    y = xf * lax.rsqrt(jnp.mean(xf * xf, axis=-1, keepdims=True) + EPS)
    return (y * gain.astype(jnp.float32)).astype(x.dtype)

def _swiglu(h, w_in, w_out):
    a, b = jnp.split(h @ w_in, 2, axis=-1)
    return (jax.nn.silu(a) * b) @ w_out

def _hgrn_lower_bounds(lb_logits):
    p = jax.nn.softmax(lb_logits.astype(jnp.float32), axis=0)
    return jnp.clip(jnp.cumsum(p, axis=0) - p[0], 0.0, 1.0 - 1e-4)

def _hgrn2_chunk_scan(q, k, v, log_f, s0):
    bsz, T = q.shape[0], q.shape[1]
    C = min(HGRN_CHUNK, T)
    n = -(-T // C)
    pad = n * C - T

    def blocks(t):
        t = jnp.pad(t, ((0, 0), (0, pad), (0, 0), (0, 0)))
        return jnp.moveaxis(t.reshape(bsz, n, C, t.shape[2], t.shape[3]), 1, 0)

    causal = jnp.tril(jnp.ones((C, C), dtype=bool))[None, :, :, None, None]

    def step(S, blk):
        qc, kc, vc, gc = blk
        b = jnp.cumsum(gc, axis=1)
        o_inter = jnp.einsum('bthk,bhkv->bthv', qc * jnp.exp(b), S)
        diff = jnp.where(causal, b[:, :, None] - b[:, None, :], 0.0)
        decay = jnp.where(causal, jnp.exp(diff), 0.0)
        scores = jnp.einsum('bthk,btshk,bshk->bths', qc, decay, kc)
        o_intra = jnp.einsum('bths,bshv->bthv', scores, vc)
        b_end = b[:, -1]
        S_new = jnp.exp(b_end)[..., None] * S + jnp.einsum(
            'bshk,bshv->bhkv', kc * jnp.exp(b_end[:, None] - b), vc)
        return S_new, o_inter + o_intra

    s_T, o = lax.scan(step, s0, (blocks(q), blocks(k), blocks(v), blocks(log_f)))
    o = jnp.moveaxis(o, 0, 1).reshape(bsz, n * C, o.shape[3], o.shape[4])[:, :T]
    return o, s_T

def _hgrn2_mixer(h, s0, lb, w_in, gnorm, w_out):
    bsz, T, _ = h.shape
    proj = (h @ w_in).astype(jnp.float32)
    q, f, i, g = jnp.split(proj, 4, axis=-1)
    lbf = lb.astype(jnp.float32)
    fg = lbf + (1.0 - lbf) * jax.nn.sigmoid(f)
    log_f = jnp.log(jnp.maximum(fg, GATE_FLOOR))
    k = (1.0 - lbf) * jax.nn.sigmoid(-f)

    def heads(t):
        return t.reshape(bsz, T, HGRN_HEADS, HGRN_HEAD_DIM)

    o, s_T = _hgrn2_chunk_scan(heads(q), heads(k), heads(i), heads(log_f), s0.astype(jnp.float32))
    o = o * lax.rsqrt(jnp.mean(o * o, axis=-1, keepdims=True) + EPS) * gnorm.astype(jnp.float32)
    o = o.reshape(bsz, T, D_MODEL) * jax.nn.silu(g)
    return o.astype(h.dtype) @ w_out, s_T

def _s5_mixer(h, s0_re, s0_im, a_re, a_im, log_dt, b_re, b_im, c_re, c_im, d_skip, w_glu):
    f32 = jnp.float32
    bsz, T, _ = h.shape
    u = h.astype(f32)
    lam = lax.complex(a_re.astype(f32), a_im.astype(f32))
    dt = jnp.exp(log_dt.astype(f32))[:, None]
    lam_bar = jnp.exp(lam * dt)
    b_bar = ((lam_bar - 1.0) / lam)[..., None] * lax.complex(b_re.astype(f32), b_im.astype(f32))
    u_g = u.reshape(bsz, T, S5_GROUPS, S5_GROUP_CH).astype(jnp.complex64)
    bu = jnp.einsum('btgc,gpc->btgp', u_g, b_bar)
    s0 = lax.complex(s0_re.astype(f32), s0_im.astype(f32))
    bu = bu.at[:, 0].add(lam_bar * s0)

    def combine(l, r):
        return l[0] * r[0], r[0] * l[1] + r[1]

    _, s = lax.associative_scan(combine, (jnp.broadcast_to(lam_bar, bu.shape), bu), axis=1)
    c = lax.complex(c_re.astype(f32), c_im.astype(f32))
    y = jnp.einsum('btgp,gcp->btgc', s, c).real.reshape(bsz, T, D_MODEL) + d_skip.astype(f32) * u
    z = jax.nn.gelu(y).astype(h.dtype)
    a, gate = jnp.split(z @ w_glu, 2, axis=-1)
    return a * jax.nn.sigmoid(gate), s[:, -1].real, s[:, -1].imag

def _trunk(x, st_hgrn, st_re, st_im,
           ln_ffn1, ffn1_w_in, ffn1_w_out, ln_mix, ln_ffn2, ffn2_w_in, ffn2_w_out,
           hgrn_lb_logits, hgrn_w_in, hgrn_gnorm, hgrn_w_out,
           s5_a_re, s5_a_im, s5_log_dt, s5_b_re, s5_b_im, s5_c_re, s5_c_im, s5_d, s5_w_glu,
           ln_final):
    lbs = _hgrn_lower_bounds(hgrn_lb_logits)
    new_hgrn, new_re, new_im = [], [], []
    for i in range(DEPTH):
        x = x + MACARON_SCALE * _swiglu(_rmsnorm(x, ln_ffn1[i]), ffn1_w_in[i], ffn1_w_out[i])
        h = _rmsnorm(x, ln_mix[i])
        j = i // N_MIXERS
        if i % N_MIXERS == 0:
            out, s_T = _hgrn2_mixer(h, st_hgrn[j], lbs[i], hgrn_w_in[j], hgrn_gnorm[j], hgrn_w_out[j])
            new_hgrn.append(s_T)
        else:
            out, sr, si = _s5_mixer(h, st_re[j], st_im[j], s5_a_re[j], s5_a_im[j], s5_log_dt[j],
                                    s5_b_re[j], s5_b_im[j], s5_c_re[j], s5_c_im[j], s5_d[j], s5_w_glu[j])
            new_re.append(sr)
            new_im.append(si)
        x = x + out
        x = x + MACARON_SCALE * _swiglu(_rmsnorm(x, ln_ffn2[i]), ffn2_w_in[i], ffn2_w_out[i])
    return _rmsnorm(x, ln_final), jnp.stack(new_hgrn), jnp.stack(new_re), jnp.stack(new_im)

def setup_inputs(seed: int = 0) -> dict:
    key = jax.random.key(seed)
    ks = iter(jax.random.split(key, 32))
    f32 = jnp.float32

    def nrm(shape, scale):
        return jax.random.normal(next(ks), shape, f32) * scale

    def gain(shape):
        return 1.0 + nrm(shape, 0.02)

    D, F = D_MODEL, D_FF
    G, GC, P = S5_GROUPS, S5_GROUP_CH, S5_STATE
    H, K = HGRN_HEADS, HGRN_HEAD_DIM
    NA, NB = N_HGRN_LAYERS, N_S5_LAYERS
    return {
        "x_prompt": nrm((BATCH, SEQ, D), 1.0),
        "x_sample": nrm((DEC_BATCH, DEC_SEQ, D), 1.0),
        "state_hgrn": nrm((NA, DEC_BATCH, H, K, K), 0.3),
        "state_s5_re": nrm((NB, DEC_BATCH, G, P), 0.1),
        "state_s5_im": nrm((NB, DEC_BATCH, G, P), 0.1),
        "ln_ffn1": gain((DEPTH, D)),
        "ffn1_w_in": nrm((DEPTH, D, 2 * F), D ** -0.5),
        "ffn1_w_out": nrm((DEPTH, F, D), F ** -0.5),
        "ln_mix": gain((DEPTH, D)),
        "ln_ffn2": gain((DEPTH, D)),
        "ffn2_w_in": nrm((DEPTH, D, 2 * F), D ** -0.5),
        "ffn2_w_out": nrm((DEPTH, F, D), F ** -0.5),
        "hgrn_lb_logits": nrm((DEPTH, D), 0.1),
        "hgrn_w_in": nrm((NA, D, 4 * D), D ** -0.5),
        "hgrn_gnorm": gain((NA, K)),
        "hgrn_w_out": nrm((NA, D, D), D ** -0.5),
        "s5_a_re": -0.5 + nrm((NB, G, P), 0.01),
        "s5_a_im": jnp.pi * jnp.arange(P, dtype=f32) + nrm((NB, G, P), 0.01),
        "s5_log_dt": jax.random.uniform(next(ks), (NB, G), f32, math.log(S5_DT_MIN), math.log(S5_DT_MAX)),
        "s5_b_re": nrm((NB, G, P, GC), (2 * GC) ** -0.5),
        "s5_b_im": nrm((NB, G, P, GC), (2 * GC) ** -0.5),
        "s5_c_re": nrm((NB, G, GC, P), (2 * P) ** -0.5),
        "s5_c_im": nrm((NB, G, GC, P), (2 * P) ** -0.5),
        "s5_d": nrm((NB, D), 1.0),
        "s5_w_glu": nrm((NB, D, 2 * D), D ** -0.5),
        "ln_final": gain((D,)),
    }

def reference(x_prompt, x_sample, state_hgrn, state_s5_re, state_s5_im,
              ln_ffn1, ffn1_w_in, ffn1_w_out, ln_mix, ln_ffn2, ffn2_w_in, ffn2_w_out,
              hgrn_lb_logits, hgrn_w_in, hgrn_gnorm, hgrn_w_out,
              s5_a_re, s5_a_im, s5_log_dt, s5_b_re, s5_b_im, s5_c_re, s5_c_im, s5_d, s5_w_glu,
              ln_final):
    weights = (ln_ffn1, ffn1_w_in, ffn1_w_out, ln_mix, ln_ffn2, ffn2_w_in, ffn2_w_out,
               hgrn_lb_logits, hgrn_w_in, hgrn_gnorm, hgrn_w_out,
               s5_a_re, s5_a_im, s5_log_dt, s5_b_re, s5_b_im, s5_c_re, s5_c_im, s5_d, s5_w_glu,
               ln_final)
    bp = x_prompt.shape[0]
    zero_hgrn = jnp.zeros((N_HGRN_LAYERS, bp, HGRN_HEADS, HGRN_HEAD_DIM, HGRN_HEAD_DIM), jnp.float32)
    zero_s5 = jnp.zeros((N_S5_LAYERS, bp, S5_GROUPS, S5_STATE), jnp.float32)
    y_prompt, hgrn_p, re_p, im_p = _trunk(x_prompt, zero_hgrn, zero_s5, zero_s5, *weights)
    y_sample, hgrn_s, re_s, im_s = _trunk(x_sample, state_hgrn, state_s5_re, state_s5_im, *weights)
    return (y_prompt, y_sample, hgrn_p, re_p, im_p, hgrn_s, re_s, im_s)


_drawn_inputs = setup_inputs


def setup_inputs(seed=0):
    import zlib

    import numpy as np

    out = dict(_drawn_inputs(seed))
    spreads = {}
    factors = {'ln_ffn1': 3.681,
     'ln_ffn2': 5.747,
     'hgrn_gnorm': 15.982,
     's5_a_re': 16.727,
     's5_c_re': 24.504,
     's5_c_im': 24.648,
     'ln_final': 7.822}
    for name, (base, spread) in spreads.items():
        noise = np.random.default_rng([zlib.crc32(name.encode()), seed]).standard_normal(out[name].shape)
        drawn = base * np.exp(spread * noise) if base else spread * noise
        out[name] = __import__('jax').numpy.asarray(drawn.astype(out[name].dtype))
    for name, factor in factors.items():
        out[name] = (out[name] * factor).astype(out[name].dtype)
    return out
```

```python
from contextlib import ExitStack

import concourse.bass as bass
from concourse import mybir

F32 = mybir.dt.float32
F32R = mybir.dt.float32r
I32 = mybir.dt.int32
U8 = mybir.dt.uint8
ALU = mybir.AluOpType
ACT = mybir.ActivationFunctionType

D_MODEL = 1024
SEQ = 512
DEC_BATCH = 8
DEC_SEQ = 8
D_FF = 2816
HEADS = 8
GROUPS = 64
GROUP_CH = 16
STATE = 64
EPS = 1e-6
GATE_FLOOR = 1e-30

P = 128
SAMPLE = DEC_BATCH * DEC_SEQ
T = SEQ + SAMPLE
HALF = T // 2
BANK = 512
NK = D_MODEL // P
CHUNKS = SEQ // P
F_GROUPS = (12, 10)
HALVINGS = (1, 2, 4, 8, 16, 32, 64)
LEVELS = 1 + len(HALVINGS)
SAMPLE_LEVELS = 4
LIFT = 8
BLOCKS = T // LIFT
PROMPT_BLOCKS = SEQ // LIFT
ST = GROUPS // 2
ST_CT = ST // NK
G_CT = GROUPS // NK
UNIT = NK * 2 * P

VECS = ["ln_ffn1", "ln_mix", "ln_ffn2", "ln_final", "hgrn_lb_logits", "s5_d", "hgrn_gnorm"]


class Phase:

    def __init__(self, kind, name, pairs, kt, cols, at):
        self.kind, self.name, self.pairs, self.kt, self.cols = kind, name, pairs, kt, cols
        self.size = kt * cols * P
        self.pair0, self.tile0 = at["pair"], at["tile"]
        at["pair"] += pairs
        at["tile"] += pairs * cols

    def last_use(self, j):
        end = self.tile0 + self.pairs * self.cols
        return (1, end - 1 + j) if self.cols == 2 else (j, end)


def phases():
    at = {"pair": 0, "tile": NK // 2}
    out = []

    def ffn(name):
        for g, n in enumerate(F_GROUPS):
            out.append(Phase("up", (name, g), n // 2, NK, 2, at))
            out.append(Phase("down", (name, g), NK // 2, n, 1, at))

    ffn("ffn1_0")
    out.append(Phase("hgrn_in", ("hgrn", 0), HEADS, NK, 2, at))
    out.append(Phase("hgrn_out", ("hgrn", 0), NK // 2, NK, 1, at))
    ffn("ffn2_0")
    ffn("ffn1_1")
    at["tile"] += NK // 2
    out.append(Phase("glu", ("s5", 0), NK // 2, NK, 2, at))
    ffn("ffn2_1")
    return out, at


class Chain:

    def __init__(self, eng, sem):
        self.eng, self.sem, self.base, self.n = eng, sem, 0, 0

    def __call__(self, ins):
        self.n += 1
        ins.then_inc(self.sem, 1)
        self.eng.wait_ge(self.sem, self.base + self.n)

    def settle(self):
        done, self.base, self.n = self.n, self.base + self.n, 0
        return done


def build_trunk(nc, x_prompt, x_sample, state_hgrn, state_s5_re, state_s5_im, ln_ffn1, ffn1_w_in, ffn1_w_out,
                ln_mix, ln_ffn2, ffn2_w_in, ffn2_w_out, hgrn_lb_logits, hgrn_w_in, hgrn_gnorm, hgrn_w_out,
                s5_a_re, s5_a_im, s5_log_dt, s5_b_re, s5_b_im, s5_c_re, s5_c_im, s5_d, s5_w_glu, ln_final,
                y_prompt, y_sample, hgrn_p, re_p, im_p, hgrn_s, re_s, im_s):
    PH, END = phases()

    place = {"at": nc.sbuf_base + (-nc.sbuf_base) % 64}
    limit = nc.sbuf_usable_end

    def sb(name, shape, dt=F32, at=None):
        size = 1 if dt == U8 else 4
        for n in shape[1:]:
            size *= n
        size += -size % 32
        where = place["at"] if at is None else at
        if at is None:
            place["at"] += size
        assert where + size <= limit, (name, where + size, limit)
        return nc.alloc_sbuf_tensor_at(name, shape, dt, offset=where)

    x = sb("x", [P, NK, T])
    h_at = place["at"]
    h_hi = sb("h_hi", [P, NK, T], F32R)
    h_lo = sb("h_lo", [P, NK, T], F32R)
    w_raw = [sb(f"w_raw{j}", [P, UNIT]) for j in range(2)]
    w_hi = [sb(f"w_hi{j}", [P, UNIT], F32R) for j in range(2)]
    w_lo = [sb(f"w_lo{j}", [P, UNIT], F32R) for j in range(2)]
    rstd = sb("rstd", [P, T])
    ssq = sb("ssq", [P, T])
    sq = sb("sq", [P, T])
    ident = sb("ident", [P, P])
    ones = sb("ones", [P, P])
    eps_t = sb("eps_t", [P, 1])
    vec = sb("vec", [P, P])
    lb = sb("lb", [P, NK])
    lb_c = sb("lb_c", [P, NK])
    lb_t = sb("lb_t", [P, 4, NK])
    lam8 = sb("lam8", [P, 2, 2, ST])
    own_seq = sb("own_seq", [SAMPLE, DEC_BATCH])
    masks = sb("masks", [P, LEVELS, P], U8)
    masks_s = sb("masks_s", [SAMPLE, SAMPLE_LEVELS, SAMPLE], U8)
    overlay = place["at"]

    g_at = place["at"]
    g_hi = sb("g_hi", [P, F_GROUPS[0], T], F32R)
    g_lo = sb("g_lo", [P, F_GROUPS[0], T], F32R)
    t_a = sb("t_a", [P, T])
    t_b = sb("t_b", [P, T])
    t_s = sb("t_s", [P, T])
    t_g = sb("t_g", [P, T])
    dt_in = sb("dt_in", [P, 2])
    lam_c = sb("lam_c", [P, 3, ST])
    lam_sc = sb("lam_sc", [P, 24, ST])
    lam_p = sb("lam_p", [P, 2, ST, LIFT + 1])
    lam_r = sb("lam_r", [P, 2, ST, LIFT])
    b_in = sb("b_in", [P, 2, ST_CT, GROUP_CH])
    b_bar = sb("b_bar", [P, 2, ST_CT, GROUP_CH])
    b_blk = sb("b_blk", [P, 2, ST_CT, 2 * GROUP_CH])
    c_in = sb("c_in", [P, 2, 2, STATE])
    c_t = sb("c_t", [P, 2, ST_CT, GROUP_CH])
    start_at = place["at"]
    b_pow = sb("b_pow", [P, 2, ST_CT, LIFT * GROUP_CH])
    c_pow = sb("c_pow", [P, 2, ST_CT, (LIFT + 1) * GROUP_CH])
    p_t1 = sb("p_t1", [P, ST_CT * (LIFT + 1) * GROUP_CH])
    p_t2 = sb("p_t2", [P, ST_CT * (LIFT + 1) * GROUP_CH])
    mask_at = place["at"]
    wb_st = sb("wb_st", [P, 2, ST_CT, P])
    kz = sb("kz", [2 * GROUP_CH, ST_CT, (2 * LIFT - 1) * GROUP_CH])
    ffn_end = place["at"]
    assert place["at"] <= limit

    x_rows = sb("x_rows", [P, CHUNKS + 1, D_MODEL], at=g_at)

    place["at"] = overlay
    o_hi = sb("o_hi", [P, NK, T], F32R)
    o_lo = sb("o_lo", [P, NK, T], F32R)
    q_t = [sb(f"q_t{b}", [P, T]) for b in range(2)]
    k_t = [sb(f"k_t{b}", [P, T]) for b in range(2)]
    s_g = [sb(f"s_g{b}", [P, T]) for b in range(2)]
    f_t = sb("f_t", [P, T])
    v_t = sb("v_t", [P, T])
    pre = sb("pre", [P, T])
    e_t = sb("e_t", [P, 608])
    score = sb("score", [P, T])
    v_tok = sb("v_tok", [P, CHUNKS + 1, P])
    k_tok = sb("k_tok", [P, CHUNKS + 1, P])
    v_seq = sb("v_seq", [SAMPLE, DEC_BATCH, P])
    s_chunk = sb("s_chunk", [P, CHUNKS - 1, P])
    s_end = [sb(f"s_end{b}", [P, P]) for b in range(2)]
    s_in = [sb(f"s_in{b}", [P, DEC_BATCH, P]) for b in range(2)]
    s_out = [sb(f"s_out{b}", [P, DEC_BATCH, P]) for b in range(2)]
    o_rs = sb("o_rs", [P, 8])
    o_dg = sb("o_dg", [P, CHUNKS + 1, P])
    assert place["at"] <= limit

    place["at"] = overlay
    z_hi = sb("z_hi", [P, NK, T], F32R)
    v_at = place["at"]
    s5_v = sb("s5_v", [P, 2, ST, BLOCKS])
    y_lift = sb("y_lift", [P, GROUPS, BLOCKS], at=v_at)
    s_at = place["at"]
    s5_s = sb("s5_s", [P, 2, ST, BLOCKS])
    z_lo = sb("z_lo", [P, NK, T], F32R, at=s_at)
    wb_at = place["at"]
    wb = [sb(f"wb{b}", [P, 2, ST_CT, P]) for b in range(2)]
    y_f = [sb(f"y_f{b}", [P, T], at=wb_at + 4 * T * b) for b in range(2)]
    z_t = sb("z_t", [P, T], at=wb_at + 4 * T * 2)
    wc = [sb(f"wc{b}", [P, 2, ST_CT, P]) for b in range(2)]
    wi = [sb(f"wi{b}", [P, G_CT, P]) for b in range(2)]
    st_rows = sb("st_rows", [P, 2, 2, P])
    s5_t = sb("s5_t", [P, 2, 2, ST])
    s5_fp = sb("s5_fp", [P, 2, ST])
    s5_fs = sb("s5_fs", [P, 2, DEC_BATCH, ST])
    fp_rows = sb("fp_rows", [ST, 2, P])
    fs_rows = sb("fs_rows", [P, 2, 2, P])
    u_t = sb("u_t", [P, NK, T], at=h_at)
    u_lift = sb("u_lift", [P, GROUPS, BLOCKS], at=h_at + 4 * NK * T)

    y_n = sb("y_n", [P, NK, T], at=h_at)
    y_rows = sb("y_rows", [P, CHUNKS + 1, D_MODEL], at=g_at)

    vec_rows = sb("vec_rows", [P, P], at=start_at)
    lam_in = sb("lam_in", [P, P], at=start_at + 4 * P)
    m_i = [sb(f"m_i{n}", [P, P], I32, at=mask_at + 4 * P * n) for n in range(4)]
    m_f = [sb(f"m_f{n}", [P, P], F32, at=mask_at + 4 * P * (4 + n)) for n in range(4)]
    ps = nc.alloc_psum_tensor("ps", [P, 8, BANK], F32)

    wb_d = nc.dram_tensor("wb_d", (NK, P, 2, ST_CT, P), F32).ap()
    wc_d = nc.dram_tensor("wc_d", (NK, P, 2, ST_CT, P), F32).ap()
    wi_d = nc.dram_tensor("wi_d", (NK, P, G_CT, P), F32).ap()
    lu_d = nc.dram_tensor("lu_d", (NK, G_CT, GROUP_CH, LIFT, BLOCKS), F32).ap()
    ly_d = nc.dram_tensor("ly_d", (NK, G_CT, GROUP_CH, LIFT, BLOCKS), F32).ap()

    ctx = ExitStack()

    def sem(name):
        return ctx.enter_context(nc.semaphore(name))

    with ctx:
        begun = sem("begun")
        x_in = sem("x_in")
        vec_in = sem("vec_in")
        lam_ld = sem("lam_ld")
        consts = sem("consts")
        masks_made = sem("masks_made")
        vec_full = sem("vec_full")
        vec_done = sem("vec_done")
        dt_done = sem("dt_done")
        w_dma = [sem(f"w_dma{j}") for j in range(2)]
        w_hi_done = [sem(f"w_hi_done{j}") for j in range(2)]
        w_ready = [sem(f"w_ready{j}") for j in range(2)]
        full = [sem(f"full{s}") for s in range(2)]
        free = [sem(f"free{s}") for s in range(2)]
        dve_link = sem("dve_link")
        ssq_zero = sem("ssq_zero")
        sq_done = sem("sq_done")
        ssq_done = sem("ssq_done")
        norm_full = sem("norm_full")
        sd_done = sem("sd_done")
        rstd_done = sem("rstd_done")
        h_hi_done = sem("h_hi_done")
        h_ready = sem("h_ready")
        silu_done = sem("silu_done")
        g_full = sem("g_full")
        g_hi_done = sem("g_hi_done")
        g_ready = sem("g_ready")
        pin = sem("pin")
        ct_full = sem("ct_full")
        ct_done = sem("ct_done")
        bpart_done = sem("bpart_done")
        bl_full = sem("bl_full")
        wbst_done = sem("wbst_done")
        cpart_done = sem("cpart_done")
        tap_full = sem("tap_full")
        kz_done = sem("kz_done")
        pst = sem("pst")
        gates_done = sem("gates_done")
        sig_done = sem("sig_done")
        silu_g = sem("silu_g")
        sc_full = sem("sc_full")
        sc_read = sem("sc_read")
        qk_done = sem("qk_done")
        vt_full = sem("vt_full")
        vtok_done = sem("vtok_done")
        kt_full = sem("kt_full")
        ktok_done = sem("ktok_done")
        vseq_done = sem("vseq_done")
        decay_done = sem("decay_done")
        kvp_full = sem("kvp_full")
        kvs_full = sem("kvs_full")
        chain_done = sem("chain_done")
        s_out_done = sem("s_out_done")
        o_full = sem("o_full")
        osq_done = sem("osq_done")
        r_full = sem("r_full")
        osd_done = sem("osd_done")
        odg_done = sem("odg_done")
        rb_full = sem("rb_full")
        og_done = sem("og_done")
        o_hi_done = sem("o_hi_done")
        o_ready = sem("o_ready")
        s_ld = [sem(f"s_ld{b}") for b in range(2)]
        s_st = [sem(f"s_st{b}") for b in range(2)]
        rows_ld = sem("rows_ld")
        sin_full = sem("sin_full")
        sin_done = sem("sin_done")
        s0_zero = sem("s0_zero")
        wb_ld = [sem(f"wb_ld{b}") for b in range(2)]
        wy_ld = [sem(f"wy_ld{b}") for b in range(2)]
        u_done = sem("u_done")
        lu_st = sem("lu_st")
        lu_ld = [sem(f"lu_ld{h}") for h in range(2)]
        v_full = sem("v_full")
        v_read = sem("v_read")
        step_done = sem("step_done")
        fs_done = sem("fs_done")
        f_full = sem("f_full")
        f_done = sem("f_done")
        f_st = sem("f_st")
        ly_st = sem("ly_st")
        ly_ld = [sem(f"ly_ld{b}") for b in range(2)]
        yy_done = sem("yy_done")
        gelu_done = sem("gelu_done")
        z_hi_done = sem("z_hi_done")
        z_ready = sem("z_ready")
        gs_done = sem("gs_done")
        yn_done = sem("yn_done")
        y_st = sem("y_st")

        TILE_Y = next(p for p in PH if p.kind == "glu").tile0 - NK // 2
        TILE_END = END["tile"]
        up_at, at = {}, 0
        for p in PH:
            if p.kind == "up":
                up_at[p.name] = at
                at += 2 * p.pairs
        COL = {"ln_ffn1": 0, "ln_mix": 16, "ln_ffn2": 32, "ln_final": 48, "lb": 56, "s5_d": 72, "gnorm": 80}
        NVEC = 81
        NORMS = [(COL["ln_ffn1"], 0), (COL["ln_mix"], 1), (COL["ln_ffn2"], 2), (COL["ln_ffn1"] + NK, 3),
                 (COL["ln_mix"] + NK, None), (COL["ln_ffn2"] + NK, 4), (COL["ln_final"], None)]
        MAKES = {("down", ("ffn1_0", 1)): 1, ("hgrn_out", ("hgrn", 0)): 2, ("down", ("ffn2_0", 1)): 3,
                 ("down", ("ffn1_1", 1)): 4, ("glu", ("s5", 0)): 5, ("down", ("ffn2_1", 1)): 6}
        READS = {("up", ("ffn1_0", 0)): 0, ("hgrn_in", ("hgrn", 0)): 1, ("up", ("ffn2_0", 0)): 2,
                 ("up", ("ffn1_1", 0)): 3, ("up", ("ffn2_1", 0)): 5}

        def cols(t, i, n=1):
            flat = t[:].rearrange("p a b -> p (a b)")
            w = t.shape[2]
            return flat[:, bass.ds(i * w, n * w)]

        def halves(ap):
            return ap.rearrange("p (h t) -> p h t", h=2)

        def pair(s):
            return ps[:, 2 * s:2 * s + 2, 0:HALF]

        def f32(ap):
            return ap.bitcast(F32)

        def lifted(ap):
            return ap.rearrange("p (n t) -> p t n", t=LIFT)

        block = ctx.enter_context(nc.Block())

        @block.sync
        def _(sp):
            def load_rows(dst, src):
                sp.dma_start(dst, src).then_inc(vec_in, 16)

            at = 0
            for v, n in ((ln_ffn1, 16), (ln_mix, 16), (ln_ffn2, 16), (ln_final, 8), (hgrn_lb_logits, 16), (s5_d, 8)):
                flat = v.rearrange("l d -> (l d)") if len(v.shape) == 2 else v
                load_rows(vec_rows[at:at + n, :], flat.rearrange("(k c) -> k c", c=P))
                at += n
            load_rows(vec_rows[at:at + 1, :], hgrn_gnorm)
            assert at + 1 == NVEC

            def w_source(ph, j, i):
                kind, (name, g) = ph.kind, ph.name
                if kind in ("up", "down"):
                    layer = int(name[-1])
                    w_in, w_out = (ffn1_w_in, ffn1_w_out) if name[:4] == "ffn1" else (ffn2_w_in, ffn2_w_out)
                    f0 = g * F_GROUPS[0]
                if kind == "up":
                    v = w_in[layer].rearrange("(k p) (a f c) -> p k a f c", p=P, a=2, c=P)
                    return [v[:, :, a, i * 2 + (f0 + j), :] for a in range(2)]
                if kind == "down":
                    v = w_out[layer, f0 * P:(f0 + ph.kt) * P].rearrange("(k p) (m c) -> p k m c", p=P, c=P)
                    return [v[:, :, i * 2 + j, :]]
                if kind == "hgrn_in":
                    v = hgrn_w_in[0].rearrange("(k p) (r h c) -> p k r h c", p=P, r=4, c=P)
                    return [v[:, :, 2 * j + a, i, :] for a in range(2)]
                if kind == "hgrn_out":
                    return [hgrn_w_out[0].rearrange("(k p) (m c) -> p k m c", p=P, c=P)[:, :, i * 2 + j, :]]
                v = s5_w_glu[0].rearrange("(k p) (a m c) -> p k a m c", p=P, a=2, c=P)
                return [v[:, :, a, i * 2 + j, :] for a in range(2)]

            def load_pair(ph, i):
                for j in range(2):
                    sp.wait_ge(w_ready[j], i + ph.pair0)
                    sp.wait_ge(begun, 1)
                    dst = w_raw[j][:, 0:ph.size].rearrange("p (a k c) -> p a k c", a=ph.cols, c=P)
                    src = w_source(ph, j, i)
                    if ph.cols == 2:
                        for a in range(2):
                            sp.dma_start(dst[:, a], src[a]).then_inc(w_dma[j], 16)
                    else:
                        for r in range(2):
                            k0, k1 = r * ph.kt // 2, (r + 1) * ph.kt // 2
                            sp.dma_start(dst[:, 0, k0:k1], src[0][:, k0:k1]).then_inc(w_dma[j], 16)

            def load_piece(ct):
                sp.wait_ge(bpart_done, ct)
                sp.wait_ge(ct_full, ct)
                sp.wait_ge(begun, 1)
                for r, (b_d, c_d) in enumerate(((s5_b_re, s5_c_re), (s5_b_im, s5_c_im))):
                    b_v = b_d[0].rearrange("g p c -> (g p) c").rearrange("(a s q) c -> a q s c", s=ST_CT, q=P)
                    sp.dma_start(b_in[:, r], b_v[ct]).then_inc(pin, 16)
                    c_v = c_d[0].rearrange("g c p -> (g c) p").rearrange("(a q) p -> a q p", q=P)
                    for d in range(2):
                        sp.dma_start(c_in[:, r, d], c_v[ct]).then_inc(pin, 16)

            def store_piece(ct):
                sp.wait_ge(wbst_done, ct + 1)
                sp.dma_start(wb_d[ct], wb_st[:]).then_inc(pst, 16)
                sp.wait_ge(cpart_done, ct + 1)
                sp.dma_start(wc_d[ct].rearrange("p r s q -> p (r s) q"),
                             c_pow[:, :, :, GROUP_CH:].rearrange("p r s q -> p (r s) q")).then_inc(pst, 16)
                sp.wait_ge(kz_done, ct + 1)
                rows = wi_d[ct].rearrange("(t c) (s g) q -> t g c s q", c=GROUP_CH, g=2)
                for t in range(LIFT):
                    for g in range(2):
                        at = (LIFT - 1 - t) * GROUP_CH
                        sp.dma_start(rows[t, g], kz[GROUP_CH * g:GROUP_CH * (g + 1), :, at:at + P]).then_inc(pst, 16)

            def s_load(h, b):
                sp.dma_start(s_in[b][:], state_hgrn[0, :, h].rearrange("b k v -> k b v")).then_inc(s_ld[b], 16)

            def s_store(h, b):
                sp.wait_ge(s_out_done, h + 1)
                sp.wait_ge(begun, 1)
                sp.dma_start(hgrn_s[0, :, h].rearrange("b k v -> k b v"), s_out[b][:]).then_inc(s_st[b], 16)
                sp.wait_ge(chain_done, h + 1)
                sp.wait_ge(begun, 1)
                sp.dma_start(hgrn_p[0, 0, h], s_end[b][:]).then_inc(s_st[b], 16)

            sp.wait_ge(begun, 1)
            for ph in PH:
                makes_s5 = ph.kind == "down" and ph.name[0] == "ffn1_0"
                if ph.kind == "hgrn_in":
                    for i in range(2):
                        load_pair(ph, i)
                        if i == 0:
                            store_piece(NK - 1)
                            sp.wait_ge(h_ready, 2 * NK)
                            sp.wait_ge(pst, 288 * NK)
                        s_load(i, i)
                    with sp.Fori(1, HEADS // 2) as i:
                        for b in range(2):
                            load_pair(ph, i * 2 + b)
                            s_store(i * 2 + (b - 2), b)
                            sp.wait_ge(o_full, i * 2 + (b - 1))
                            sp.wait_ge(begun, 1)
                            s_load(i * 2 + b, b)
                elif makes_s5:
                    for i in range(ph.pairs):
                        ct = i + ph.name[1] * (NK // 2)
                        load_pair(ph, i)
                        load_piece(ct)
                        if ct:
                            store_piece(ct - 1)
                elif ph.kind == "glu":
                    load_pair(ph, 0)
                    sp.wait_ge(ssq_done, 5 * NK)
                    for r, s in enumerate((state_s5_re, state_s5_im)):
                        v = s[0].rearrange("b g p -> b (g p)").rearrange("b (s q) -> (b s) q", q=P)
                        sp.dma_start(st_rows[:, r], v.rearrange("(h r) q -> r h q", h=2)).then_inc(rows_ld, 16)
                    sp.wait_ge(pst, 288 * NK)
                    for ct in range(2):
                        sp.dma_start(wb[ct][:], wb_d[ct]).then_inc(wb_ld[ct], 16)
                        sp.dma_start(wc[ct][:], wc_d[ct]).then_inc(wy_ld[ct], 16)
                        sp.dma_start(wi[ct][:], wi_d[ct]).then_inc(wy_ld[ct], 16)
                    for h in range(2):
                        for ct in range(4 * h, 4 * h + 4):
                            sp.wait_ge(u_done, ct + 1)
                            sp.dma_start(lu_d[ct].rearrange("g c t n -> (g c) (t n)"), u_t[:, ct]).then_inc(lu_st, 16)
                        sp.wait_ge(lu_st, 64 * (h + 1))
                        for t in range(LIFT):
                            src = lu_d[4 * h:4 * h + 4].rearrange("k g c t n -> t c (k g) n")[t]
                            sp.dma_start(u_lift[GROUP_CH * t:GROUP_CH * (t + 1), 32 * h:32 * h + 32, :], src)\
                              .then_inc(lu_ld[h], 16)
                    for ct in range(2, NK):
                        sp.wait_ge(v_full, ct - 1)
                        sp.dma_start(wb[ct % 2][:], wb_d[ct]).then_inc(wb_ld[ct % 2], 16)
                    sp.wait_ge(f_done, 2)
                    for r, s in enumerate((re_p, im_p)):
                        v = s[0, 0].rearrange("g p -> (g p)").rearrange("(s q) -> s q", q=P)
                        sp.dma_start(v, fp_rows[:, r]).then_inc(f_st, 16)
                    for r, s in enumerate((re_s, im_s)):
                        v = s[0].rearrange("b g p -> b (g p)").rearrange("b (s q) -> (b s) q", q=P)
                        sp.dma_start(v.rearrange("(h r) q -> r h q", h=2), fs_rows[:, r]).then_inc(f_st, 16)
                    for ct in range(2, NK):
                        sp.wait_ge(full[ct % 2], TILE_Y + ct // 2)
                        sp.dma_start(wc[ct % 2][:], wc_d[ct]).then_inc(wy_ld[ct % 2], 16)
                        sp.dma_start(wi[ct % 2][:], wi_d[ct]).then_inc(wy_ld[ct % 2], 16)
                        if ct in (5, 7):
                            store_y = (ct - 5) // 2
                            for b in range(2):
                                sp.wait_ge(free[b], TILE_Y + 2 * (store_y + 1))
                            for t in range(LIFT):
                                dst = ly_d[4 * store_y:4 * store_y + 4].rearrange("k g c t n -> t c (k g) n")[t]
                                src = y_lift[GROUP_CH * t:GROUP_CH * (t + 1), 32 * store_y:32 * store_y + 32, :]
                                sp.dma_start(dst, src).then_inc(ly_st, 16)
                    for ct in range(NK):
                        sp.wait_ge(ly_st, 128 * (ct // 4 + 1))
                        sp.wait_ge(v_full, NK)
                        if ct >= 2:
                            sp.wait_ge(gelu_done, ct - 1)
                        sp.dma_start(y_f[ct % 2][:], ly_d[ct].rearrange("g c t n -> (g c) (t n)"))\
                          .then_inc(ly_ld[ct % 2], 16)
                    with sp.Fori(1, ph.pairs) as i:
                        load_pair(ph, i)
                else:
                    with sp.Fori(0, ph.pairs) as i:
                        load_pair(ph, i)
                    if ph.kind == "hgrn_out":
                        for h in (HEADS - 2, HEADS - 1):
                            s_store(h, h % 2)
            for c in range(CHUNKS + 1):
                sp.wait_ge(free[c % 2], TILE_END + c // 2 + 1)
                if c < CHUNKS:
                    sp.dma_start(y_prompt[0, c * P:(c + 1) * P, :], y_rows[:, c, :]).then_inc(y_st, 16)
                else:
                    sp.dma_start(y_sample.rearrange("b t d -> (b t) d"), y_rows[0:SAMPLE, c, :]).then_inc(y_st, 16)
            sp.wait_ge(y_st, 16 * (CHUNKS + 1))
            sp.wait_ge(f_st, 64)
            sp.wait_ge(pst, 288 * NK)
            sp.wait_ge(lu_st, 16 * NK)
            sp.wait_ge(ly_st, 16 * 2 * LIFT)
            for b in range(2):
                sp.wait_ge(s_st[b], 32 * HEADS // 2)

        @block.gpsimd
        def _(pool):
            nc.gpsimd.memset(ident[:], 0.0).then_inc(begun, 1)
            nc.gpsimd.memset(ones[:], 1.0).then_inc(consts, 1)
            nc.gpsimd.memset(eps_t[:], EPS).then_inc(consts, 1)
            pool.wait_ge(begun, 1)
            nc.gpsimd.affine_select(out=ident[:], in_=ident[:], compare_op=ALU.not_equal, fill=1.0, base=0,
                                    pattern=[[-1, P]], channel_multiplier=1).then_inc(consts, 1)
            nc.gpsimd.iota(m_i[0][:], pattern=[[1, P]], base=0, channel_multiplier=0).then_inc(consts, 1)
            nc.gpsimd.iota(m_i[1][:], pattern=[[0, P]], base=0, channel_multiplier=1).then_inc(consts, 1)
            nc.gpsimd.memset(kz[:], 0.0).then_inc(consts, 1)
            nc.gpsimd.memset(b_blk[:], 0.0).then_inc(consts, 1)
            nc.gpsimd.memset(own_seq[:], 1.0).then_inc(consts, 1)
            pool.wait_ge(consts, 8)
            nc.gpsimd.affine_select(out=own_seq[:], in_=own_seq[:], compare_op=ALU.is_ge, fill=0.0, base=0,
                                    pattern=[[-DEC_SEQ, DEC_BATCH]], channel_multiplier=1).then_inc(consts, 1)
            pool.wait_ge(consts, 9)
            nc.gpsimd.affine_select(out=own_seq[:], in_=own_seq[:], compare_op=ALU.is_ge, fill=0.0, base=DEC_SEQ - 1,
                                    pattern=[[DEC_SEQ, DEC_BATCH]], channel_multiplier=-1).then_inc(consts, 1)

            def rest(ph, j, i):
                pool.wait_ge(w_hi_done[j], i + (ph.pair0 + 1))
                n = ph.size
                nc.gpsimd.tensor_tensor(w_lo[j][:, 0:n], w_raw[j][:, 0:n], f32(w_hi[j][:, 0:n]), ALU.subtract)\
                    .then_inc(w_ready[j], 1)

            def states(m, b, turn):
                pool.wait_ge(s_ld[b], turn * 16 + 16)
                pool.wait_ge(s_st[b], turn * 32)
                pool.wait_ge(kvs_full, m)
                pool.wait_ge(vtok_done, m + 1)
                nc.gpsimd.tensor_tensor(
                    v_seq[:], v_tok[0:SAMPLE, CHUNKS, :].unsqueeze(1).to_broadcast([SAMPLE, DEC_BATCH, P]),
                    own_seq[:].unsqueeze(2).to_broadcast([SAMPLE, DEC_BATCH, P]), ALU.mult).then_inc(vseq_done, 1)
                pool.wait_ge(qk_done, m * LEVELS + SAMPLE_LEVELS)
                nc.gpsimd.tensor_tensor(
                    s_out[b][:], s_in[b][:],
                    e_t[:, 432 + PROMPT_BLOCKS:432 + BLOCKS].unsqueeze(2).to_broadcast([P, DEC_BATCH, P]),
                    ALU.mult).then_inc(decay_done, 1)

            for n, ph in enumerate(PH):
                if ph.kind == "hgrn_in":
                    rest(ph, 0, 0)
                    rest(ph, 1, 0)
                    rest(ph, 0, 1)
                    with pool.Fori(0, HEADS // 2 - 1) as i:
                        rest(ph, 1, i * 2 + 1)
                        states(i * 2, 0, i)
                        rest(ph, 0, i * 2 + 2)
                        rest(ph, 1, i * 2 + 2)
                        states(i * 2 + 1, 1, i)
                        rest(ph, 0, i * 2 + 3)
                    rest(ph, 1, HEADS - 1)
                    states(HEADS - 2, 0, HEADS // 2 - 1)
                    rest(PH[n + 1], 0, 0)
                    states(HEADS - 1, 1, HEADS // 2 - 1)
                    rest(PH[n + 1], 1, 0)
                else:
                    with pool.Fori(int(ph.kind == "hgrn_out"), ph.pairs) as i:
                        for j in range(2):
                            rest(ph, j, i)

        @block.scalar
        def _(act):
            act.dma_start(x_rows[:, 0:CHUNKS, :], x_prompt[0].rearrange("(c p) d -> p c d", p=P)).then_inc(x_in, 16)
            act.dma_start(x_rows[0:SAMPLE, CHUNKS, :], x_sample.rearrange("b t d -> (b t) d")).then_inc(x_in, 16)
            lam_rows = s5_a_re[0].rearrange("g p -> (g p)").rearrange("(s q) -> s q", q=P)
            act.dma_start(lam_in[0:ST, :], lam_rows).then_inc(lam_ld, 16)
            lam_rows = s5_a_im[0].rearrange("g p -> (g p)").rearrange("(s q) -> s q", q=P)
            act.dma_start(lam_in[ST:2 * ST, :], lam_rows).then_inc(lam_ld, 16)
            act.dma_start(dt_in[2 * ST:3 * ST, :], s5_log_dt[0].rearrange("(s g) -> s g", g=2)).then_inc(lam_ld, 16)

            def split(ph, j, i, prev, i_prev):
                if prev is not None:
                    if i_prev is None:
                        s, n = prev.last_use(j)
                        act.wait_ge(full[s], n)
                    elif prev.cols == 2:
                        act.wait_ge(full[1], i_prev * 2 + (prev.tile0 + j + 1))
                    else:
                        act.wait_ge(full[j], i_prev + (prev.tile0 + 1))
                act.wait_ge(w_dma[j], i * 32 + (ph.pair0 * 32 + 32))
                nc.scalar.activation(w_hi[j][:, 0:ph.size], w_raw[j][:, 0:ph.size], ACT.Copy).then_inc(w_hi_done[j], 1)

            def split_next(n, ph, j, i, last):
                if j == 0:
                    if isinstance(i, int) and i == 0:
                        split(ph, 1, 0, PH[n - 1] if n else None, None)
                    else:
                        split(ph, 1, i, ph, i - 1)
                elif not last:
                    split(ph, 0, i + 1, ph, i)
                elif n + 1 < len(PH):
                    split(PH[n + 1], 0, 0, ph, None)

            def norm_tile(r, m, taken):
                gain, fill = NORMS[r]
                act.wait_ge(*taken)
                act.wait_ge(ssq_done, m + r * NK)
                act.wait_ge(begun, 1)
                if fill is not None:
                    nc.scalar.activation(cols(h_hi, m), cols(x, m), ACT.Copy, scale=vec[:, bass.ds(m + gain, 1)])\
                        .then_inc(h_hi_done, 1)
                nc.scalar.activation(sq[:], cols(x, m), ACT.Square).then_inc(sq_done, 1)

            def root(r):
                act.wait_ge(norm_full, r + 1)
                nc.scalar.activation(halves(sq[:]), ps[:, 4:6, 0:HALF], ACT.Sqrt, scale=1.0 / D_MODEL, bias=eps_t[:])\
                    .then_inc(sd_done, 1)

            act.wait_ge(vec_full, 1)
            nc.scalar.activation(vec[:, 0:NVEC], ps[:, 6, 0:NVEC], ACT.Copy).then_inc(vec_done, 1)
            act.wait_ge(vec_done, 1)
            for m in range(NK):
                norm_tile(0, m, (free[m % 2], m // 2 + 1))
            split(PH[0], 0, 0, None, None)

            def ffn_up(n, ph):
                base = up_at[ph.name]

                def unit(i, j, last=False):
                    u = i * 2 + (base + j)
                    t = i * 2 + (ph.tile0 + j)
                    split_next(n, ph, j, i, last)
                    if ph.name[1] == 0 and j == 0 and isinstance(i, int) and i == 0:
                        root(READS[(ph.kind, ph.name)])
                    act.wait_ge(free[0], t + 1)
                    act.wait_ge(g_full, u)
                    nc.scalar.activation(t_s[:], t_a[:], ACT.Silu).then_inc(silu_done, 1)
                    act.wait_ge(g_full, u + 1)
                    act.wait_ge(begun, 1)
                    nc.scalar.activation(cols(g_hi, i * 2 + j), t_g[:], ACT.Copy).then_inc(g_hi_done, 1)

                for j in range(2):
                    unit(0, j)
                with act.Fori(1, ph.pairs - 1) as i:
                    for j in range(2):
                        unit(i, j)
                for j in range(2):
                    unit(ph.pairs - 1, j, last=True)

            def ffn_down(n, ph):
                r = MAKES.get((ph.kind, ph.name))
                pieces = ph.kind == "down" and ph.name[0] == "ffn1_0"

                def unit(i, j, last=False):
                    split_next(n, ph, j, i, last)
                    if pieces:
                        ct = i + ph.name[1] * (NK // 2)
                        if j == 0:
                            act.wait_ge(ct_full, ct + 1)
                            act.wait_ge(cpart_done, ct)
                            v = ps[:, 7, 0:2 * P].rearrange("p (q g c) -> p q g c", g=2, c=GROUP_CH)
                            o = c_t[:].rearrange("p r s c -> p (r s) c")
                            nc.scalar.activation(o[0:STATE], v[0:STATE, :, 0], ACT.Copy)
                            nc.scalar.activation(o[STATE:P], v[STATE:P, :, 1], ACT.Copy).then_inc(ct_done, 1)
                            act.wait_ge(bl_full, ct + 1)
                            act.wait_ge(pst, ct * 288)
                            for q in range(2):
                                ins = nc.scalar.activation(wb_st[:, q].rearrange("p s q -> p (s q)"), ps[:, 4 + q, :],
                                                           ACT.Copy)
                            ins.then_inc(wbst_done, 1)
                    if r is not None:
                        norm_tile(r, i * 2 + j, (free[j], i + (ph.tile0 + 1)))
                    if pieces and j == 1:
                        act.wait_ge(tap_full, ct_of(i) + 1)
                        nc.scalar.activation(kz[:, :, P - GROUP_CH:],
                                             ps[0:2 * GROUP_CH, 6, :].rearrange("p (s q) -> p s q", q=P), ACT.Copy)\
                            .then_inc(kz_done, 1)

                def ct_of(i):
                    return i + ph.name[1] * (NK // 2)

                for j in range(2):
                    unit(0, j)
                with act.Fori(1, ph.pairs - 1) as i:
                    for j in range(2):
                        unit(i, j)
                for j in range(2):
                    unit(ph.pairs - 1, j, last=True)

            def hgrn(n_ph, ph):
                def project_f(n, b):
                    act.wait_ge(free[1], n * 2 + (ph.tile0 + 1))
                    nc.scalar.activation(k_t[b][:], pre[:], ACT.Sigmoid, scale=-1.0).then_inc(sig_done, 1)
                    if not isinstance(n, int) or n:
                        act.wait_ge(qk_done, n * LEVELS - (LEVELS - 2))
                    nc.scalar.activation(f_t[:], pre[:], ACT.Sigmoid).then_inc(sig_done, 1)

                def project_g(n, b):
                    act.wait_ge(free[1], n * 2 + (ph.tile0 + 2))
                    nc.scalar.activation(s_g[b][:], pre[:], ACT.Silu).then_inc(silu_g, 1)

                def take_turned(m, bank_done, dst, done):
                    act.wait_ge(bank_done, m + 1)
                    act.wait_ge(o_full, m)
                    nc.scalar.activation(dst[:, 0:CHUNKS, :].rearrange("p c q -> p (c q)"), ps[:, 6, :], ACT.Copy)
                    nc.scalar.activation(dst[0:SAMPLE, CHUNKS, :], ps[0:SAMPLE, 7, 0:P], ACT.Copy).then_inc(done, 1)

                def tail(m):
                    take_turned(m, kt_full, k_tok, ktok_done)
                    act.wait_ge(o_full, m + 1)
                    act.wait_ge(r_full, m)
                    nc.scalar.activation(sq[:, 0:SEQ], ps[:, 5, :], ACT.Square)
                    nc.scalar.activation(sq[:, SEQ:T], ps[:, 4, 0:SAMPLE], ACT.Square).then_inc(osq_done, 1)
                    act.wait_ge(odg_done, m)
                    act.wait_ge(r_full, m + 1)
                    nc.scalar.activation(o_rs[:, 0:CHUNKS], ps[:, 6, 0:CHUNKS], ACT.Sqrt, scale=1.0 / P, bias=eps_t[:])
                    nc.scalar.activation(o_rs[0:SAMPLE, CHUNKS:CHUNKS + 1], ps[0:SAMPLE, 6, CHUNKS:CHUNKS + 1], ACT.Sqrt,
                                         scale=1.0 / P, bias=eps_t[0:SAMPLE]).then_inc(osd_done, 1)
                    act.wait_ge(og_done, m + 1)
                    act.wait_ge(begun, 1)
                    nc.scalar.activation(cols(o_hi, m), ssq[:], ACT.Copy).then_inc(o_hi_done, 1)

                def step(n, b, m, last=False):
                    if n is not None:
                        if isinstance(n, int) and n == 0:
                            split(ph, 1, 0, PH[n_ph - 1], None)
                            root(READS[(ph.kind, ph.name)])
                        else:
                            split(ph, 1, n, ph, n - 1)
                        project_f(n, b)
                    if m is not None:
                        act.wait_ge(pst, 288 * NK)
                        take_turned(m, vt_full, v_tok, vtok_done)
                    if n is not None:
                        if last:
                            split(PH[n_ph + 1], 0, 0, ph, None)
                        else:
                            split(ph, 0, n + 1, ph, n)
                        project_g(n, b)
                    if m is not None:
                        tail(m)

                step(0, 0, None)
                with act.Fori(0, HEADS // 2 - 1) as i:
                    step(i * 2 + 1, 1, i * 2)
                    step(i * 2 + 2, 0, i * 2 + 1)
                step(HEADS - 1, 1, HEADS - 2, last=True)
                step(None, 0, HEADS - 1)

            def s5(n, ph):
                root(4)
                act.wait_ge(sin_full, 1)
                for q in range(2):
                    v = ps[:, 6, 2 * P * q:2 * P * (q + 1)].rearrange("p (b s) -> p b s", s=ST)
                    ins = nc.scalar.activation(s5_s[:, q, :, PROMPT_BLOCKS:].rearrange("p s b -> p b s"), v, ACT.Copy)
                ins.then_inc(sin_done, 1)
                for ct in range(NK):
                    act.wait_ge(v_full, ct + 1)
                    b = 4 + 2 * (ct % 2)
                    o = s5_v[:, :, ST_CT * ct:ST_CT * (ct + 1), :].rearrange("p r s n -> p r (s n)")
                    nc.scalar.activation(o, ps[:, b:b + 2, 0:HALF], ACT.Copy).then_inc(v_read, 1)
                act.wait_ge(f_full, 1)
                nc.scalar.activation(fp_rows[:].rearrange("p r q -> p (r q)"), ps[0:ST, 4, 0:2 * P], ACT.Copy)\
                    .then_inc(f_done, 1)
                act.wait_ge(f_full, 2)
                nc.scalar.activation(fs_rows[:].rearrange("p r h q -> p (r h q)"), ps[:, 5, :], ACT.Copy)\
                    .then_inc(f_done, 1)
                for ct in range(NK):
                    s = ct % 2
                    act.wait_ge(full[s], TILE_Y + ct // 2 + 1)
                    o = y_lift[:, G_CT * ct:G_CT * (ct + 1), :].rearrange("p (s g) n -> p g s n", g=2)
                    nc.scalar.activation(o, pair(s).rearrange("p g (s n) -> p g s n", n=BLOCKS), ACT.Copy)\
                        .then_inc(free[s], 1)
                for ct in range(NK):
                    act.wait_ge(yy_done, ct + 1)
                    act.wait_ge(z_ready, ct)
                    nc.scalar.activation(z_t[:], y_f[ct % 2][:], ACT.Gelu_apprx_tanh).then_inc(gelu_done, 1)
                    act.wait_ge(gelu_done, ct + 1)
                    nc.scalar.activation(lifted(z_hi[:, ct]), z_t[:].rearrange("p (t n) -> p t n", t=LIFT), ACT.Copy)\
                        .then_inc(z_hi_done, 1)

                def unit(i, j, last=False):
                    split_next(n, ph, j, i, last)
                    t = i * 2 + (ph.tile0 + j)
                    act.wait_ge(full[1], t + 1)
                    act.wait_ge(gs_done, i * 2 + j)
                    nc.scalar.activation(halves(t_s[:]), pair(1), ACT.Sigmoid).then_inc(free[1], 1)
                    norm_tile(5, i * 2 + j, (gs_done, i * 2 + (j + 1)))

                for j in range(2):
                    unit(0, j)
                with act.Fori(1, ph.pairs - 1) as i:
                    for j in range(2):
                        unit(i, j)
                for j in range(2):
                    unit(ph.pairs - 1, j, last=True)

            for n, ph in enumerate(PH):
                {"up": ffn_up, "down": ffn_down, "hgrn_in": hgrn, "hgrn_out": ffn_down, "glu": s5}[ph.kind](n, ph)
            root(6)
            for c in range(1, CHUNKS + 1, 2):
                act.wait_ge(full[1], TILE_END + c // 2 + 1)
                nc.scalar.activation(y_rows[:, c, :].rearrange("p (h d) -> p h d", h=2), ps[:, 2:4, :], ACT.Copy)\
                    .then_inc(free[1], 1)

        @block.vector
        def _(dve):
            link = Chain(dve, dve_link)
            V = nc.vector

            def norm_tile(r, m):
                gain, fill = NORMS[r]
                if fill is not None:
                    dve.wait_ge(h_hi_done, m + (fill * NK + 1))
                    V.scalar_tensor_tensor(out=cols(h_lo, m), in0=cols(x, m), scalar=vec[:, bass.ds(m + gain, 1)],
                                           in1=f32(cols(h_hi, m)), op0=ALU.mult, op1=ALU.subtract).then_inc(h_ready, 1)
                dve.wait_ge(ssq_done, m + r * NK)
                dve.wait_ge(sq_done, m + (r * NK + 1))
                V.tensor_tensor(ssq[:], ssq[:], sq[:], ALU.add).then_inc(ssq_done, 1)

            def clear_ssq(r):
                if r:
                    dve.wait_ge(norm_full, r)
                V.memset(ssq[:], 0.0).then_inc(ssq_zero, 1)
                dve.wait_ge(ssq_zero, r + 1)

            def reciprocal(r):
                dve.wait_ge(sd_done, r + 1)
                V.reciprocal(rstd[:], sq[:]).then_inc(rstd_done, 1)
                dve.wait_ge(rstd_done, r + 1)

            def scaled(dst, s):
                return V.tensor_tensor(halves(dst), pair(s), halves(rstd[:]), ALU.mult)

            clear_ssq(0)
            for m in range(NK):
                s = m % 2
                dve.wait_ge(full[s], m // 2 + 1)
                V.tensor_copy(x[:, m, 0:SEQ], ps[:, 2 * s, :])
                V.tensor_copy(x[:, m, SEQ:T], ps[:, 2 * s + 1, 0:SAMPLE]).then_inc(free[s], 1)
                norm_tile(0, m)
            dve.wait_ge(lam_ld, 48)
            V.tensor_copy(lam_in[2 * ST:3 * ST].rearrange("s (g p) -> s g p", g=2),
                          dt_in[2 * ST:3 * ST].unsqueeze(2).to_broadcast([ST, 2, STATE])).then_inc(dt_done, 1)

            def bounds():
                a0, a1 = vec[:, COL["lb"]:COL["lb"] + NK], vec[:, COL["lb"] + NK:COL["lb"] + 2 * NK]
                dve.wait_ge(vec_done, 1)
                link(V.tensor_tensor(lb_t[:, 0], a0, a1, ALU.max))
                link(V.tensor_tensor(lb_t[:, 1], a0, lb_t[:, 0], ALU.subtract))
                link(V.tensor_tensor(lb_t[:, 2], a1, lb_t[:, 0], ALU.subtract))
                link(exp_of(lb_t[:, 1:3, :].rearrange("p a b -> p (a b)"), 2 * NK))
                link(V.tensor_tensor(lb_t[:, 0], lb_t[:, 1], lb_t[:, 2], ALU.add))
                link(V.reciprocal(lb_t[:, 0], lb_t[:, 0]))
                link(V.tensor_tensor(lb_t[:, 1], lb_t[:, 1], lb_t[:, 0], ALU.mult))
                link(V.tensor_tensor(lb_t[:, 2], lb_t[:, 1], lb_t[:, 1], ALU.subtract))
                link(V.tensor_scalar(lb[:], lb_t[:, 2], 0.0, 1.0 - 1e-4, ALU.max, ALU.min))
                link(V.tensor_scalar(lb_c[:], lb[:], -1.0, 1.0, ALU.mult, ALU.add))

            def exp_of(v, w):
                n, r, y = (lam_sc[:, k, 0:w] for k in (20, 21, 22))
                n_i = lam_sc[:, 23, 0:w].bitcast(I32)
                round_ = 1.5 * 2.0 ** 23
                link(V.tensor_scalar(v, v, -87.0, 88.0, ALU.max, ALU.min))
                link(V.tensor_scalar(n, v, 1.4426950408889634, round_, ALU.mult, ALU.add))
                link(V.tensor_scalar(n, n, -round_, None, ALU.add))
                link(V.scalar_tensor_tensor(out=r, in0=n, scalar=-0.693359375, in1=v, op0=ALU.mult, op1=ALU.add))
                link(V.scalar_tensor_tensor(out=r, in0=n, scalar=2.12194440e-4, in1=r, op0=ALU.mult, op1=ALU.add))
                link(V.tensor_scalar(y, r, 1.0 / 5040, None, ALU.mult))
                for c in (1.0 / 720, 1.0 / 120, 1.0 / 24, 1.0 / 6, 0.5, 1.0):
                    link(V.scalar_tensor_tensor(out=y, in0=y, scalar=c, in1=r, op0=ALU.add, op1=ALU.mult))
                link(V.tensor_scalar(y, y, 1.0, None, ALU.add))
                link(V.tensor_scalar(n_i, n, 127.0, 2.0 ** 23, ALU.add, ALU.mult))
                return V.tensor_tensor(v, y, n_i.bitcast(F32), ALU.mult)

            def make_masks():
                dve.wait_ge(consts, 5)
                query, key, differ, v = m_i[0][:], m_i[1][:], m_i[2][:], m_f[0][:]
                link(V.tensor_tensor(differ, query, key, ALU.bitwise_xor))
                link(V.tensor_tensor(m_f[1][:], query, key, ALU.is_gt))
                link(V.tensor_tensor(v, differ, m_f[1][:], ALU.mult))
                link(V.tensor_tensor(masks[:, 0, :], query, key, ALU.is_equal))
                link(V.tensor_copy(masks_s[:, 0, :], masks[0:SAMPLE, 0, 0:SAMPLE]))
                link(V.tensor_scalar(m_f[2][:], v, float(DEC_SEQ), None, ALU.is_lt))
                for n, half in enumerate(HALVINGS):
                    link(V.tensor_scalar(m_f[3][:], v, float(half), None, ALU.is_ge))
                    link(V.tensor_copy(masks[:, n + 1, :], m_f[3][:]))
                    if n + 1 < SAMPLE_LEVELS:
                        link(V.tensor_tensor(masks_s[:, n + 1, :], m_f[3][0:SAMPLE, 0:SAMPLE],
                                             m_f[2][0:SAMPLE, 0:SAMPLE], ALU.mult))

            def lambda_bar():
                row = lambda k: lam_sc[:, k, :]
                a_re, a_im, dt = (lam_c[:, k, :] for k in range(3))
                dve.wait_ge(lam_ld, 48)
                dve.wait_ge(vec_full, 2)
                link(V.tensor_copy(lam_c[:].rearrange("p k s -> p (k s)"), ps[:, 7, 0:3 * ST]))
                link(exp_of(dt, ST))
                link(V.tensor_tensor(row(0), a_re, dt, ALU.mult))
                link(V.tensor_tensor(row(1), a_im, dt, ALU.mult))
                link(exp_of(row(0), ST))
                round_ = 1.5 * 2.0 ** 23
                link(V.tensor_scalar(row(2), row(1), 0.15915494309189535, round_, ALU.mult, ALU.add))
                link(V.tensor_scalar(row(2), row(2), -round_, None, ALU.add))
                for part in (-6.28125, -1.9353071795864769e-3):
                    link(V.scalar_tensor_tensor(out=row(1), in0=row(2), scalar=part, in1=row(1), op0=ALU.mult, op1=ALU.add))
                link(V.tensor_scalar(row(1), row(1), 3.1415925, -3.1415925, ALU.min, ALU.max))
                link(V.tensor_scalar(row(3), row(1), 0.5, None, ALU.mult))
                link(V.tensor_tensor(row(4), row(3), row(3), ALU.mult))
                link(V.tensor_scalar(row(5), row(4), 1.0 / 6227020800, None, ALU.mult))
                for c in (-1.0 / 39916800, 1.0 / 362880, -1.0 / 5040, 1.0 / 120, -1.0 / 6):
                    link(V.scalar_tensor_tensor(out=row(5), in0=row(5), scalar=c, in1=row(4), op0=ALU.add, op1=ALU.mult))
                link(V.scalar_tensor_tensor(out=row(5), in0=row(5), scalar=1.0, in1=row(3), op0=ALU.add, op1=ALU.mult))
                link(V.tensor_scalar(row(6), row(4), 1.0 / 479001600, None, ALU.mult))
                for c in (-1.0 / 3628800, 1.0 / 40320, -1.0 / 720, 1.0 / 24, -0.5):
                    link(V.scalar_tensor_tensor(out=row(6), in0=row(6), scalar=c, in1=row(4), op0=ALU.add, op1=ALU.mult))
                link(V.tensor_scalar(row(6), row(6), 1.0, 2.0, ALU.add, ALU.mult))
                link(V.tensor_tensor(row(6), row(6), row(5), ALU.mult))
                link(V.tensor_tensor(row(7), row(5), row(5), ALU.mult))
                link(V.tensor_scalar(row(7), row(7), -2.0, None, ALU.mult))
                link(V.tensor_tensor(row(11), row(0), row(6), ALU.mult))
                link(V.tensor_tensor(row(10), row(0), row(7), ALU.mult))
                link(V.tensor_scalar(row(12), row(0), -1.0, None, ALU.add))
                link(V.tensor_tensor(row(10), row(10), row(12), ALU.add))
                link(V.tensor_tensor(row(12), a_re, a_re, ALU.mult))
                link(V.tensor_tensor(row(13), a_im, a_im, ALU.mult))
                link(V.tensor_tensor(row(12), row(12), row(13), ALU.add))
                link(V.reciprocal(row(12), row(12)))
                link(V.tensor_tensor(row(13), row(10), a_re, ALU.mult))
                link(V.tensor_tensor(row(14), row(11), a_im, ALU.mult))
                link(V.tensor_tensor(row(13), row(13), row(14), ALU.add))
                link(V.tensor_tensor(row(8), row(13), row(12), ALU.mult))
                link(V.tensor_tensor(row(13), row(11), a_re, ALU.mult))
                link(V.tensor_tensor(row(14), row(10), a_im, ALU.mult))
                link(V.tensor_tensor(row(13), row(13), row(14), ALU.subtract))
                link(V.tensor_tensor(row(9), row(13), row(12), ALU.mult))
                link(V.memset(lam_p[:, 0, :, 0:1], 1.0))
                link(V.memset(lam_p[:, 1, :, 0:1], 0.0))
                link(V.tensor_scalar(lam_p[:, 0, :, 1], row(10), 1.0, None, ALU.add))
                link(V.tensor_copy(lam_p[:, 1, :, 1], row(11)))
                for n in (1, 2, 4):
                    a_r, a_i = (lam_p[:, q, :, 1:n + 1] for q in range(2))
                    b_r, b_i = (lam_p[:, q, :, n:n + 1].to_broadcast([P, ST, n]) for q in range(2))
                    o_r, o_i = (lam_p[:, q, :, n + 1:2 * n + 1] for q in range(2))
                    t = p_t1[:, 0:ST * n].rearrange("p (s n) -> p s n", n=n)
                    link(V.tensor_tensor(o_r, a_r, b_r, ALU.mult))
                    link(V.tensor_tensor(t, a_i, b_i, ALU.mult))
                    link(V.tensor_tensor(o_r, o_r, t, ALU.subtract))
                    link(V.tensor_tensor(o_i, a_r, b_i, ALU.mult))
                    link(V.tensor_tensor(t, a_i, b_r, ALU.mult))
                    link(V.tensor_tensor(o_i, o_i, t, ALU.add))
                for q in range(2):
                    link(V.tensor_copy(lam_r[:, q], lam_p[:, q, :, 0:LIFT][:, :, ::-1]))
                link(V.tensor_copy(lam8[:, 0, 0], lam_p[:, 0, :, LIFT]))
                link(V.tensor_copy(lam8[:, 0, 1], lam_p[:, 0, :, LIFT]))
                link(V.tensor_copy(lam8[:, 1, 0], lam_p[:, 1, :, LIFT]))
                link(V.tensor_scalar(lam8[:, 1, 1], lam_p[:, 1, :, LIFT], -1.0, None, ALU.mult))

            def complex_mult(out_r, out_i, a, b, t1, t2, done, negate_i=False):
                (a_r, a_i), (b_r, b_i) = a, b
                link(V.tensor_tensor(t1, a_r, b_r, ALU.mult))
                link(V.tensor_tensor(t2, a_i, b_i, ALU.mult))
                link(V.tensor_tensor(out_r, t1, t2, ALU.subtract))
                link(V.tensor_tensor(t1, a_r, b_i, ALU.mult))
                link(V.tensor_tensor(t2, a_i, b_r, ALU.mult))
                if negate_i:
                    done(V.scalar_tensor_tensor(out=out_i, in0=t1, scalar=-1.0, in1=t2, op0=ALU.mult, op1=ALU.subtract))
                else:
                    done(V.tensor_tensor(out_i, t1, t2, ALU.add))

            def of_ct(row, ct):
                return lam_sc[:, row, bass.ds(ct * ST_CT, ST_CT)].unsqueeze(2).to_broadcast([P, ST_CT, GROUP_CH])

            def b_part(ct):
                dve.wait_ge(pin, ct * 96 + 96)
                dve.wait_ge(bl_full, ct)
                dve.wait_ge(tap_full, ct)
                t1, t2 = (t[:, 0:ST_CT * GROUP_CH].rearrange("p (s c) -> p s c", s=ST_CT) for t in (p_t1, p_t2))
                complex_mult(b_bar[:, 0], b_bar[:, 1], (b_in[:, 0], b_in[:, 1]), (of_ct(8, ct), of_ct(9, ct)), t1, t2,
                             link)
                for g in range(2):
                    rows = slice(STATE * g, STATE * (g + 1))
                    link(V.tensor_copy(
                        b_blk[rows, :, :, GROUP_CH * g:GROUP_CH * (g + 1)].rearrange("p r s c -> p (r s) c"),
                        b_bar[rows].rearrange("p r s c -> p (r s) c")))
                shape = [P, ST_CT, LIFT, GROUP_CH]
                t1, t2 = (t[:, 0:ST_CT * P].rearrange("p (s t c) -> p s t c", s=ST_CT, t=LIFT) for t in (p_t1, p_t2))
                power = [lam_r[:, q, bass.ds(ct * ST_CT, ST_CT), :].unsqueeze(3).to_broadcast(shape)
                         for q in range(2)]
                bar = [b_bar[:, q].unsqueeze(2).to_broadcast(shape) for q in range(2)]
                out = [b_pow[:, q].rearrange("p s (t c) -> p s t c", t=LIFT) for q in range(2)]
                complex_mult(out[0], out[1], power, bar, t1, t2, lambda ins: ins.then_inc(bpart_done, 1))

            def c_part(ct):
                dve.wait_ge(ct_done, ct + 1)
                dve.wait_ge(bpart_done, ct + 1)
                dve.wait_ge(pst, ct * 288)
                shape = [P, ST_CT, LIFT + 1, GROUP_CH]
                t1, t2 = (t[:].rearrange("p (s t c) -> p s t c", s=ST_CT, c=GROUP_CH) for t in (p_t1, p_t2))
                power = [lam_p[:, q, bass.ds(ct * ST_CT, ST_CT), :].unsqueeze(3).to_broadcast(shape) for q in range(2)]
                c = [c_t[:, q].unsqueeze(2).to_broadcast(shape) for q in range(2)]
                out = [c_pow[:, q].rearrange("p s (t c) -> p s t c", c=GROUP_CH) for q in range(2)]
                complex_mult(out[0], out[1], c, power, t1, t2, lambda ins: ins.then_inc(cpart_done, 1), negate_i=True)

            def ffn_up(ph):
                base = up_at[ph.name]
                if (ph.kind, ph.name) in READS:
                    reciprocal(READS[(ph.kind, ph.name)])

                def unit(i, j):
                    u = i * 2 + (base + j)
                    t = i * 2 + (ph.tile0 + j)
                    dve.wait_ge(full[0], t + 1)
                    scaled(t_a[:], 0).then_inc(free[0], 1)
                    dve.wait_ge(full[1], t + 1)
                    scaled(t_b[:], 1).then_inc(free[1], 1)
                    dve.wait_ge(g_ready, u)
                    dve.wait_ge(free[1], t + 1)
                    dve.wait_ge(silu_done, u + 1)
                    V.tensor_tensor(t_g[:], t_b[:], t_s[:], ALU.mult).then_inc(g_full, 1)
                    dve.wait_ge(g_hi_done, u + 1)
                    V.tensor_tensor(cols(g_lo, i * 2 + j), t_g[:], f32(cols(g_hi, i * 2 + j)), ALU.subtract)\
                        .then_inc(g_ready, 1)

                first = 0
                if ph is PH[0]:
                    for j in range(2):
                        unit(0, j)
                    make_masks()
                    bounds()
                    lambda_bar()
                    first = 1
                with dve.Fori(first, ph.pairs) as i:
                    for j in range(2):
                        unit(i, j)

            def down(ph):
                r = MAKES.get((ph.kind, ph.name))
                pieces = ph.kind == "down" and ph.name[0] == "ffn1_0"
                if r is not None:
                    if ph.kind == "hgrn_out":
                        dve.wait_ge(o_ready, HEADS)
                    clear_ssq(r)
                scale = 1.0 if ph.kind == "hgrn_out" else 0.5

                def unit(i, j):
                    if pieces:
                        (b_part, c_part)[j](i + ph.name[1] * (NK // 2))
                    m = i * 2 + j
                    dve.wait_ge(full[j], i + (ph.tile0 + 1))
                    V.scalar_tensor_tensor(out=halves(cols(x, m)), in0=pair(j), scalar=scale, in1=halves(cols(x, m)),
                                           op0=ALU.mult, op1=ALU.add).then_inc(free[j], 1)
                    if r is not None:
                        norm_tile(r, m)

                link.settle()
                at, per = link.base, 6 + 2 + 5 + 5 if pieces else 0
                with dve.Fori(0, ph.pairs) as i:
                    link.base = i * per + at
                    for j in range(2):
                        unit(i, j)
                    assert link.n == per
                    link.n = 0
                link.base = at + ph.pairs * per

            def hgrn(ph):
                reciprocal(1)
                link(V.memset(score[:], 0.0))

                def level(m, b, n):
                    dve.wait_ge(sc_full, m * LEVELS + (n + 1))
                    q, k = q_t[b], k_t[b]
                    if n == 0:
                        V.tensor_tensor(q[:], q[:], f_t[:], ALU.mult).then_inc(qk_done, 1)
                    else:
                        if n == 3:
                            dve.wait_ge(decay_done, m)
                        half = HALVINGS[n - 1]
                        span = T if half < DEC_SEQ else SEQ
                        blocks = span // (2 * half)
                        at = {1: None, 2: 0, 4: 288, 8: 432, 16: 504, 32: 536, 64: 552, 128: 560}
                        e = f_t[:, 0:span] if half == 1 else e_t[:, at[half]:at[half] + span // half]
                        e = e.rearrange("p (n h) -> p n h", h=2)
                        out = e_t[:, at[2 * half]:at[2 * half] + blocks]
                        qv = q[:, 0:span].rearrange("p (n h l) -> p n h l", h=2, l=half)
                        kv = k[:, 0:span].rearrange("p (n h l) -> p n h l", h=2, l=half)
                        shape = [P, blocks, half]
                        dve.wait_ge(qk_done, m * LEVELS + n)
                        V.tensor_tensor(qv[:, :, 1], qv[:, :, 1], e[:, :, 0:1].to_broadcast(shape), ALU.mult)
                        V.tensor_tensor(kv[:, :, 0], kv[:, :, 0], e[:, :, 1:2].to_broadcast(shape), ALU.mult)
                        V.tensor_tensor(out, e[:, :, 0], e[:, :, 1], ALU.mult).then_inc(qk_done, 1)
                    dve.wait_ge(begun, 1)
                    if n == 0:
                        dve.wait_ge(o_full, m)
                    dve.wait_ge(sc_read, m * LEVELS + n)
                    shape = [P, CHUNKS, P]
                    ins = V.copy_predicated(score[:, 0:SEQ].rearrange("p (c q) -> p c q", q=P),
                                            masks[:, n, :].unsqueeze(1).to_broadcast(shape),
                                            ps[:, 4 + n % 2, :].rearrange("p (c q) -> p c q", q=P))
                    if n < SAMPLE_LEVELS:
                        ins = V.copy_predicated(score[0:SAMPLE, SEQ:T], masks_s[:, n, :], ps[0:SAMPLE, 6 + n % 2, 0:SAMPLE])
                    ins.then_inc(sc_read, 1)

                def take(dst, s, n, k):
                    dve.wait_ge(full[s], n * 2 + (ph.tile0 + k + 1))
                    scaled(dst, s).then_inc(free[s], 1)

                def gates(n, b):
                    dve.wait_ge(sig_done, n * 2 + 2)
                    link(V.tensor_scalar(f_t[:], f_t[:], lb_c[:, bass.ds(n, 1)], lb[:, bass.ds(n, 1)], ALU.mult, ALU.add))
                    V.tensor_scalar(f_t[:], f_t[:], GATE_FLOOR, None, ALU.max)
                    V.tensor_scalar(k_t[b][:], k_t[b][:], lb_c[:, bass.ds(n, 1)], None, ALU.mult).then_inc(gates_done, 1)

                def tail(m, b, turn):
                    kv = lambda c: ps[:, 4, c * P:(c + 1) * P]
                    dve.wait_ge(kvp_full, m + 1)
                    link(V.tensor_copy(s_chunk[:, 0, :], kv(0)))
                    for c in range(1, CHUNKS):
                        decay = e_t[:, 560 + c:561 + c]
                        out = s_chunk[:, c, :] if c < CHUNKS - 1 else s_end[b][:]
                        if c == CHUNKS - 1:
                            dve.wait_ge(s_st[b], turn * 32)
                        ins = V.scalar_tensor_tensor(out=out, in0=s_chunk[:, c - 1, :], scalar=decay, in1=kv(c),
                                                     op0=ALU.mult, op1=ALU.add)
                        if c < CHUNKS - 1:
                            link(ins)
                    ins.then_inc(chain_done, 1)
                    dve.wait_ge(kvs_full, m + 1)
                    dve.wait_ge(decay_done, m + 1)
                    sv = s_out[b][:].rearrange("p b v -> p (b v)").rearrange("p (h w) -> p h w", h=2)
                    V.tensor_tensor(sv, sv, ps[:, 6:8, :], ALU.add).then_inc(s_out_done, 1)
                    dve.wait_ge(silu_g, m + 1)
                    dve.wait_ge(o_ready, m)
                    dve.wait_ge(osq_done, m + 1)
                    gn = vec[:, COL["gnorm"]:COL["gnorm"] + 1]
                    V.scalar_tensor_tensor(out=ssq[:, 0:SEQ], in0=ps[:, 5, :], scalar=gn, in1=s_g[b][:, 0:SEQ],
                                           op0=ALU.mult, op1=ALU.mult)
                    link(V.scalar_tensor_tensor(out=ssq[:, SEQ:T], in0=ps[:, 4, 0:SAMPLE], scalar=gn,
                                                in1=s_g[b][:, SEQ:T], op0=ALU.mult, op1=ALU.mult))
                    dve.wait_ge(osd_done, m + 1)
                    V.reciprocal(o_rs[:, 0:CHUNKS], o_rs[:, 0:CHUNKS])
                    link(V.reciprocal(o_rs[0:SAMPLE, CHUNKS:CHUNKS + 1], o_rs[0:SAMPLE, CHUNKS:CHUNKS + 1]))
                    shape = [P, CHUNKS, P]
                    V.tensor_tensor(o_dg[:, 0:CHUNKS, :], ident[:].unsqueeze(1).to_broadcast(shape),
                                    o_rs[:, 0:CHUNKS].unsqueeze(2).to_broadcast(shape), ALU.mult)
                    V.tensor_scalar(o_dg[0:SAMPLE, CHUNKS, 0:SAMPLE], ident[0:SAMPLE, 0:SAMPLE],
                                    o_rs[0:SAMPLE, CHUNKS:CHUNKS + 1], None, ALU.mult).then_inc(odg_done, 1)
                    dve.wait_ge(rb_full, m + 1)
                    V.tensor_tensor(ssq[:, 0:SEQ], ssq[:, 0:SEQ], ps[:, 7, :], ALU.mult)
                    V.tensor_tensor(ssq[:, SEQ:T], ssq[:, SEQ:T], ps[:, 6, 0:SAMPLE], ALU.mult).then_inc(og_done, 1)
                    dve.wait_ge(o_hi_done, m + 1)
                    V.tensor_tensor(cols(o_lo, m), ssq[:], f32(cols(o_hi, m)), ALU.subtract).then_inc(o_ready, 1)

                def step(n, b, m, turn):
                    links = int(n is not None) + (CHUNKS + 1 if m is not None else 0)
                    mb = 1 - b
                    if m is not None:
                        level(m, mb, 0)
                        level(m, mb, 1)
                    if n is not None:
                        take(q_t[b][:], 0, n, 0)
                    if m is not None:
                        level(m, mb, 2)
                        level(m, mb, 3)
                    if n is not None:
                        dve.wait_ge(silu_g, n)
                        take(pre[:], 1, n, 0)
                    if m is not None:
                        level(m, mb, 4)
                        level(m, mb, 5)
                    if n is not None:
                        gates(n, b)
                        dve.wait_ge(vt_full, n)
                        take(v_t[:], 0, n, 1)
                    if m is not None:
                        level(m, mb, 6)
                        level(m, mb, 7)
                    if n is not None:
                        take(pre[:], 1, n, 1)
                    if m is not None:
                        tail(m, mb, turn)
                    assert link.n == links, (link.n, links)

                link.settle()
                step(0, 0, None, None)
                link.settle()
                at = link.base
                one = 1 + CHUNKS + 1
                with dve.Fori(0, HEADS // 2 - 1) as i:
                    link.base = i * (2 * one) + at
                    step(i * 2 + 1, 1, i * 2, i)
                    link.settle()
                    step(i * 2 + 2, 0, i * 2 + 1, i)
                    link.n = 0
                link.base = at + (HEADS // 2 - 1) * 2 * one
                step(HEADS - 1, 1, HEADS - 2, HEADS // 2 - 1)
                link.settle()
                step(None, 0, HEADS - 1, HEADS // 2 - 1)
                link.settle()

            def s5(ph):
                reciprocal(4)
                for ct in range(NK):
                    V.scalar_tensor_tensor(out=u_t[:, ct].rearrange("p (t n) -> p t n", t=LIFT), in0=lifted(x[:, ct]),
                                           scalar=vec[:, NORMS[4][0] + ct:NORMS[4][0] + ct + 1], in1=lifted(rstd[:]),
                                           op0=ALU.mult, op1=ALU.mult).then_inc(u_done, 1)
                dve.wait_ge(ssq_done, 5 * NK)
                V.memset(s5_s[:, :, :, 0:1].rearrange("p r s n -> p (r s) n"), 0.0).then_inc(s0_zero, 1)
                dve.wait_ge(s0_zero, 1)
                dve.wait_ge(sin_done, 1)
                dve.wait_ge(v_read, NK)
                link.settle()
                s_n = s5_s[:].rearrange("p r s n -> p (r s) n")
                v_n = s5_v[:].rearrange("p r s n -> p (r s) n")

                def at_block(t, n):
                    return t[:, :, bass.ds(n, 1)].rearrange("p (r s) o -> p r (s o)", r=2)

                def advance(n, out):
                    before = at_block(s_n, n)
                    V.tensor_tensor(s5_t[:, 0], before, lam8[:, 0], ALU.mult)
                    link(V.tensor_tensor(s5_t[:, 1, ::-1], before, lam8[:, 1], ALU.mult))
                    link(V.tensor_tensor(s5_t[:, 0], s5_t[:, 0], at_block(v_n, n), ALU.add))
                    V.tensor_tensor(out, s5_t[:, 0], s5_t[:, 1], ALU.add).then_inc(step_done, 1)

                body, at = 7, link.base
                with dve.Fori(0, (PROMPT_BLOCKS - 1) // body) as i:
                    link.base = i * (2 * body) + at
                    for k in range(body):
                        n = i * body + k
                        advance(n, at_block(s_n, i * body + (k + 1)))
                        dve.wait_ge(step_done, i * body + (k + 1))
                    link.n = 0
                link.base = at + 2 * (PROMPT_BLOCKS - 1)
                advance(PROMPT_BLOCKS - 1, s5_fp[:])
                t1, t2 = (t[:, 0:2 * ST * DEC_BATCH].rearrange("p (r b s) -> p r b s", r=2, s=ST) for t in (sq, ssq))
                before = s5_s[:, :, :, PROMPT_BLOCKS:].rearrange("p r s b -> p r b s")
                adds = s5_v[:, :, :, PROMPT_BLOCKS:].rearrange("p r s b -> p r b s")
                shape = [P, 2, DEC_BATCH, ST]
                link(V.tensor_tensor(t1, before, lam8[:, 0].unsqueeze(2).to_broadcast(shape), ALU.mult))
                link(V.tensor_tensor(t2[:, ::-1], before, lam8[:, 1].unsqueeze(2).to_broadcast(shape), ALU.mult))
                link(V.tensor_tensor(t1, t1, adds, ALU.add))
                V.tensor_tensor(s5_fs[:], t1, t2, ALU.add).then_inc(fs_done, 1)
                for ct in range(NK):
                    b = ct % 2
                    dve.wait_ge(ly_ld[b], 16 * (ct // 2 + 1))
                    V.scalar_tensor_tensor(out=y_f[b][:], in0=u_t[:, ct], scalar=vec[:, COL["s5_d"] + ct:COL["s5_d"] + ct + 1],
                                           in1=y_f[b][:], op0=ALU.mult, op1=ALU.add).then_inc(yy_done, 1)
                    dve.wait_ge(z_hi_done, ct + 1)
                    dve.wait_ge(full[1], TILE_Y + NK // 2)
                    V.tensor_tensor(lifted(z_lo[:, ct]), z_t[:].rearrange("p (t n) -> p t n", t=LIFT),
                                    f32(lifted(z_hi[:, ct])), ALU.subtract).then_inc(z_ready, 1)
                clear_ssq(5)

                def unit(i, j):
                    t = i * 2 + (ph.tile0 + j)
                    m = i * 2 + j
                    dve.wait_ge(full[0], t + 1)
                    dve.wait_ge(free[1], t + 1)
                    V.tensor_tensor(halves(t_a[:]), pair(0), halves(t_s[:]), ALU.mult).then_inc(free[0], 1)
                    dve.wait_ge(free[0], t + 1)
                    V.tensor_tensor(cols(x, m), cols(x, m), t_a[:], ALU.add).then_inc(gs_done, 1)
                    norm_tile(5, m)

                with dve.Fori(0, ph.pairs) as i:
                    for j in range(2):
                        unit(i, j)

            for ph in PH:
                {"up": ffn_up, "down": down, "hgrn_in": hgrn, "hgrn_out": down, "glu": s5}[ph.kind](ph)
            reciprocal(6)
            for k in range(NK):
                V.scalar_tensor_tensor(out=y_n[:, k], in0=x[:, k], scalar=vec[:, COL["ln_final"] + k:COL["ln_final"] + k + 1],
                                       in1=rstd[:], op0=ALU.mult, op1=ALU.mult).then_inc(yn_done, 1)
            for c in range(0, CHUNKS + 1, 2):
                n = P if c < CHUNKS else SAMPLE
                dve.wait_ge(full[0], TILE_END + c // 2 + 1)
                V.tensor_copy(y_rows[0:n, c, :].rearrange("p (h d) -> p h d", h=2), ps[0:n, 0:2, :]).then_inc(free[0], 1)

        @block.tensor
        def _(pe):
            M = nc.tensor

            def turn(out, t, n=P, w=P):
                return M.transpose(out, t, ident[0:n, 0:n])

            def sum_tokens(r):
                pe.wait_ge(ssq_done, NK * (r + 1))
                pe.wait_ge(consts, 3)
                if r:
                    pe.wait_ge(sd_done, r)
                if r == 2:
                    pe.wait_ge(og_done, HEADS)
                if r == 5:
                    pe.wait_ge(f_done, 2)
                for h in range(2):
                    ins = M.matmul(ps[:, 4 + h, 0:HALF], ones[:], ssq[:, h * HALF:(h + 1) * HALF], start=True, stop=True)
                ins.then_inc(norm_full, 1)

            def product(ph, j, a, i, hi, lo, before=None):
                s, t = (a, i * 2 + (ph.tile0 + j)) if ph.cols == 2 else (j, i + ph.tile0)
                if a == 0:
                    pe.wait_ge(w_ready[j], i + (ph.pair0 + 1))
                pe.wait_ge(free[s], t)
                for k in range(ph.kt):
                    if before is not None:
                        before(k)
                    at = (a * ph.kt + k) * P
                    for n, (w, v) in enumerate(((w_hi, hi), (w_hi, lo), (w_lo, hi))):
                        for h in range(2):
                            ins = M.matmul(ps[:, 2 * s + h, 0:HALF], w[j][:, at:at + P], v[:, k, h * HALF:(h + 1) * HALF],
                                           start=k == 0 and n == 0, stop=k == ph.kt - 1 and n == 2)
                ins.then_inc(full[s], 1)

            pe.wait_ge(consts, 3)
            pe.wait_ge(vec_in, 7 * 16)
            turn(ps[:, 6, 0:NVEC], vec_rows[0:NVEC, :], NVEC).then_inc(vec_full, 1)
            pe.wait_ge(x_in, 32)
            for m in range(NK):
                s = m % 2
                if m >= 2:
                    pe.wait_ge(free[s], m // 2)
                for c in range(CHUNKS):
                    turn(ps[:, 2 * s, c * P:(c + 1) * P], x_rows[:, c, m * P:(m + 1) * P])
                turn(ps[:, 2 * s + 1, 0:SAMPLE], x_rows[0:SAMPLE, CHUNKS, m * P:(m + 1) * P], SAMPLE).then_inc(full[s], 1)
            pe.wait_ge(lam_ld, 48)
            pe.wait_ge(dt_done, 1)
            turn(ps[:, 7, 0:3 * ST], lam_in[0:3 * ST, :], 3 * ST).then_inc(vec_full, 1)

            def reads_norm(ph):
                r = READS[(ph.kind, ph.name)]
                fill = NORMS[r][1]

                def before(k):
                    pe.wait_ge(h_ready, fill * NK + k + 1)
                    if k == NK - 1:
                        sum_tokens(r)
                return before

            def ffn_up(ph):
                first = reads_norm(ph) if (ph.kind, ph.name) in READS else None
                for j in range(2):
                    for a in range(2):
                        product(ph, j, a, 0, h_hi, h_lo, first if (j, a) == (0, 0) else None)
                with pe.Fori(1, ph.pairs) as i:
                    for j in range(2):
                        for a in range(2):
                            product(ph, j, a, i, h_hi, h_lo)

            def c_turned(ct):
                pe.wait_ge(pin, ct * 96 + 96)
                pe.wait_ge(ct_done, ct)
                for r in range(2):
                    ins = turn(ps[:, 7, r * P:(r + 1) * P], c_in[:, r].rearrange("p d q -> p (d q)"))
                ins.then_inc(ct_full, 1)

            def b_turned(ct):
                pe.wait_ge(bpart_done, ct + 1)
                pe.wait_ge(wbst_done, ct)
                for r in range(2):
                    for st in range(ST_CT):
                        ins = turn(ps[:, 4 + r, st * P:(st + 1) * P], b_pow[:, r, st])
                ins.then_inc(bl_full, 1)

            def taps(ct):
                pe.wait_ge(cpart_done, ct + 1)
                pe.wait_ge(kz_done, ct)
                for st in range(ST_CT):
                    for r in range(2):
                        ins = M.matmul(ps[0:2 * GROUP_CH, 6, st * P:(st + 1) * P], b_blk[:, r, st], c_pow[:, r, st, 0:P],
                                       start=r == 0, stop=r == 1)
                ins.then_inc(tap_full, 1)

            def down(ph):
                pieces = ph.name[0] == "ffn1_0"
                made = up_at.get(ph.name, 0)

                def before(k):
                    if ph.kind == "hgrn_out":
                        pe.wait_ge(o_ready, k + 1)
                    elif k == 0:
                        pe.wait_ge(g_ready, made + ph.kt - 1)
                    elif k == ph.kt - 1:
                        pe.wait_ge(g_ready, made + ph.kt)

                hi, lo = (o_hi, o_lo) if ph.kind == "hgrn_out" else (g_hi, g_lo)
                ct0 = ph.name[1] * (NK // 2)

                def pair_of(i, first=None):
                    product(ph, 0, 0, i, hi, lo, first)
                    if pieces:
                        c_turned(i + ct0)
                        b_turned(i + ct0)
                    product(ph, 1, 0, i, hi, lo)
                    if pieces:
                        taps(i + ct0)

                if pieces:
                    pe.wait_ge(sd_done, 1)
                pair_of(0, before)
                with pe.Fori(1, ph.pairs) as i:
                    pair_of(i)

            def hgrn(ph):
                def level(m, b, n):
                    if n == 0:
                        pe.wait_ge(og_done, m)
                        pe.wait_ge(gates_done, m + 1)
                    else:
                        pe.wait_ge(qk_done, m * LEVELS + n)
                    if n >= 2:
                        pe.wait_ge(sc_read, m * LEVELS + (n - 1))
                    for c in range(CHUNKS):
                        at = slice(c * P, (c + 1) * P)
                        ins = M.matmul(ps[:, 4 + n % 2, at], k_t[b][:, at], q_t[b][:, at], start=True, stop=True)
                    if n < SAMPLE_LEVELS:
                        ins = M.matmul(ps[0:SAMPLE, 6 + n % 2, 0:SAMPLE], k_t[b][:, SEQ:T], q_t[b][:, SEQ:T],
                                       start=True, stop=True)
                    ins.then_inc(sc_full, 1)

                def turned(t, done):
                    for c in range(CHUNKS):
                        turn(ps[:, 6, c * P:(c + 1) * P], t[:, c * P:(c + 1) * P])
                    turn(ps[0:SAMPLE, 7, 0:P], t[:, SEQ:T]).then_inc(done, 1)

                def v_turned(m):
                    pe.wait_ge(free[0], m * 2 + (ph.tile0 + 2))
                    pe.wait_ge(sc_read, m * LEVELS + SAMPLE_LEVELS)
                    turned(v_t, vt_full)

                def tail(m, b):
                    pe.wait_ge(qk_done, m * LEVELS + LEVELS)
                    pe.wait_ge(vtok_done, m + 1)
                    turned(k_t[b], kt_full)
                    pe.wait_ge(ktok_done, m + 1)
                    pe.wait_ge(sc_read, m * LEVELS + (LEVELS - 1))
                    for c in range(CHUNKS):
                        ins = M.matmul(ps[:, 4, c * P:(c + 1) * P], k_tok[:, c, :], v_tok[:, c, :], start=True, stop=True)
                    ins.then_inc(kvp_full, 1)
                    pe.wait_ge(vseq_done, m + 1)
                    for h in range(2):
                        v = v_seq[:, 4 * h:4 * h + 4, :].rearrange("p b v -> p (b v)")
                        ins = M.matmul(ps[:, 6 + h, :], k_tok[0:SAMPLE, CHUNKS, :], v, start=True, stop=True)
                    ins.then_inc(kvs_full, 1)
                    pe.wait_ge(sc_read, m * LEVELS + LEVELS)
                    pe.wait_ge(chain_done, m + 1)
                    for c in range(CHUNKS):
                        at = slice(c * P, (c + 1) * P)
                        M.matmul(ps[:, 5, at], v_tok[:, c, :], score[:, at], start=True, stop=c == 0)
                        if c:
                            M.matmul(ps[:, 5, at], s_chunk[:, c - 1, :], q_t[b][:, at], start=False, stop=True)
                    pe.wait_ge(decay_done, m + 1)
                    M.matmul(ps[:, 4, 0:SAMPLE], v_tok[0:SAMPLE, CHUNKS, :], score[0:SAMPLE, SEQ:T], start=True, stop=False)
                    for n in range(DEC_BATCH):
                        at = SEQ + n * DEC_SEQ
                        ins = M.matmul(ps[:, 4, n * DEC_SEQ:(n + 1) * DEC_SEQ], s_in[b][:, n, :],
                                       q_t[b][:, at:at + DEC_SEQ], start=False, stop=n == DEC_BATCH - 1)
                    ins.then_inc(o_full, 1)
                    pe.wait_ge(osq_done, m + 1)
                    pe.wait_ge(s_out_done, m + 1)
                    for c in range(CHUNKS):
                        M.matmul(ps[:, 6, c:c + 1], sq[:, c * P:(c + 1) * P], ones[:, 0:1], start=True, stop=True)
                    M.matmul(ps[0:SAMPLE, 6, CHUNKS:CHUNKS + 1], sq[:, SEQ:T], ones[:, 0:1], start=True, stop=True)\
                     .then_inc(r_full, 1)
                    pe.wait_ge(odg_done, m + 1)
                    for c in range(CHUNKS):
                        M.matmul(ps[:, 7, c * P:(c + 1) * P], ones[:], o_dg[:, c, :], start=True, stop=True)
                    M.matmul(ps[:, 6, 0:SAMPLE], ones[0:SAMPLE, :], o_dg[0:SAMPLE, CHUNKS, 0:SAMPLE], start=True, stop=True)\
                     .then_inc(rb_full, 1)

                def step(n, b, m):
                    first = reads_norm(ph) if isinstance(n, int) and n == 0 else None
                    if m is not None:
                        level(m, 1 - b, 0)
                        level(m, 1 - b, 1)
                    if n is not None:
                        product(ph, 0, 0, n, h_hi, h_lo, first)
                    if m is not None:
                        level(m, 1 - b, 2)
                        level(m, 1 - b, 3)
                    if n is not None:
                        product(ph, 0, 1, n, h_hi, h_lo)
                    if m is not None:
                        level(m, 1 - b, 4)
                        level(m, 1 - b, 5)
                        v_turned(m)
                    if n is not None:
                        product(ph, 1, 0, n, h_hi, h_lo)
                    if m is not None:
                        level(m, 1 - b, 6)
                        level(m, 1 - b, 7)
                    if n is not None:
                        product(ph, 1, 1, n, h_hi, h_lo)
                    if m is not None:
                        tail(m, 1 - b)

                pe.wait_ge(wbst_done, NK)
                pe.wait_ge(kz_done, NK)
                step(0, 0, None)
                with pe.Fori(0, HEADS // 2 - 1) as i:
                    step(i * 2 + 1, 1, i * 2)
                    step(i * 2 + 2, 0, i * 2 + 1)
                step(HEADS - 1, 1, HEADS - 2)
                step(None, 0, HEADS - 1)

            def s5(ph):
                sum_tokens(4)
                pe.wait_ge(rows_ld, 32)
                for q in range(2):
                    for h in range(2):
                        at = (2 * q + h) * P
                        ins = turn(ps[:, 6, at:at + P], st_rows[:, q, h])
                ins.then_inc(sin_full, 1)
                pe.wait_ge(sd_done, 5)
                for ct in range(NK):
                    pe.wait_ge(lu_ld[ct // 4], 16 * LIFT)
                    pe.wait_ge(wb_ld[ct % 2], 16 * (ct // 2 + 1))
                    if ct == 1:
                        pe.wait_ge(sin_done, 1)
                    if ct >= 2:
                        pe.wait_ge(v_read, ct - 1)
                    for r in range(2):
                        for g in range(2):
                            for st in range(ST_CT):
                                ins = M.matmul(
                                    ps[STATE * g:STATE * (g + 1), 4 + 2 * (ct % 2) + r, st * BLOCKS:(st + 1) * BLOCKS],
                                    wb[ct % 2][:, r, st, STATE * g:STATE * (g + 1)], u_lift[:, G_CT * ct + 2 * st + g, :],
                                    start=True, stop=True)
                    ins.then_inc(v_full, 1)
                pe.wait_ge(v_read, NK)
                pe.wait_ge(step_done, PROMPT_BLOCKS)
                for q in range(2):
                    ins = turn(ps[0:ST, 4, q * P:(q + 1) * P], s5_fp[:, q])
                ins.then_inc(f_full, 1)
                pe.wait_ge(fs_done, 1)
                for q in range(2):
                    for h in range(2):
                        at = (2 * q + h) * P
                        ins = turn(ps[:, 5, at:at + P], s5_fs[:, q, 4 * h:4 * h + 4].rearrange("p b s -> p (b s)"))
                ins.then_inc(f_full, 1)
                for ct in range(NK):
                    s = ct % 2
                    pe.wait_ge(wy_ld[s], 32 * (ct // 2 + 1))
                    pe.wait_ge(free[s], TILE_Y + ct // 2)
                    for g in range(G_CT):
                        st, g2 = g // 2, g % 2
                        rows = slice(STATE * g2, STATE * (g2 + 1))
                        out = ps[:, 2 * s + g2, st * BLOCKS:(st + 1) * BLOCKS]
                        M.matmul(out, wi[s][:, g], u_lift[:, G_CT * ct + g, :], start=True, stop=False)
                        M.matmul(out, wc[s][rows, 0, st], s5_s[rows, 0, ST_CT * ct + st, :], start=False, stop=False)
                        ins = M.matmul(out, wc[s][rows, 1, st], s5_s[rows, 1, ST_CT * ct + st, :], start=False, stop=True)
                    ins.then_inc(full[s], 1)

                def z_here(k):
                    pe.wait_ge(z_ready, k + 1)

                for j in range(2):
                    for a in range(2):
                        product(ph, j, a, 0, z_hi, z_lo, z_here if (j, a) == (0, 0) else None)
                with pe.Fori(1, ph.pairs) as i:
                    for j in range(2):
                        for a in range(2):
                            product(ph, j, a, i, z_hi, z_lo)

            for ph in PH:
                {"up": ffn_up, "down": down, "hgrn_in": hgrn, "hgrn_out": down, "glu": s5}[ph.kind](ph)

            sum_tokens(6)
            pe.wait_ge(yn_done, NK)
            for c in range(CHUNKS + 1):
                s, n = c % 2, P if c < CHUNKS else SAMPLE
                pe.wait_ge(free[s], TILE_END + c // 2)
                for k in range(NK):
                    ins = turn(ps[0:n, 2 * s + k // 4, (k % 4) * P:(k % 4 + 1) * P], y_n[:, k, c * P:c * P + n])
                ins.then_inc(full[s], 1)


_INS = ["x_prompt", "x_sample", "state_hgrn", "state_s5_re", "state_s5_im", "ln_ffn1", "ffn1_w_in", "ffn1_w_out",
        "ln_mix", "ln_ffn2", "ffn2_w_in", "ffn2_w_out", "hgrn_lb_logits", "hgrn_w_in", "hgrn_gnorm", "hgrn_w_out",
        "s5_a_re", "s5_a_im", "s5_log_dt", "s5_b_re", "s5_b_im", "s5_c_re", "s5_c_im", "s5_d", "s5_w_glu", "ln_final"]
_OUTS = [(1, SEQ, D_MODEL), (DEC_BATCH, DEC_SEQ, D_MODEL), (1, 1, HEADS, P, P), (1, 1, GROUPS, STATE),
         (1, 1, GROUPS, STATE), (1, DEC_BATCH, HEADS, P, P), (1, DEC_BATCH, GROUPS, STATE),
         (1, DEC_BATCH, GROUPS, STATE)]


def kernel(**inputs):
    import numpy as _np
    import concourse.bacc as _bacc
    from concourse import mybir as _mybir
    from concourse.bass_utils import run_bass_kernel_spmd as _run

    nc = _bacc.Bacc("TRN2", target_bir_lowering=False, num_devices=1)
    arrays, args = {}, []
    for name in _INS:
        a = _np.ascontiguousarray(inputs[name])
        arrays[f"in_{name}_dram"] = a
        args.append(nc.dram_tensor(f"in_{name}_dram", a.shape, _mybir.dt.from_np(a.dtype), kind="ExternalInput").ap())
    for i, shape in enumerate(_OUTS):
        args.append(nc.dram_tensor(f"out_{i}_dram", shape, F32, kind="ExternalOutput").ap())
    build_trunk(nc, *args)
    r = _run(nc, [arrays], core_ids=[0])
    return tuple(r.results[0][f"out_{i}_dram"] for i in range(len(_OUTS)))
```

```python
from contextlib import ExitStack

import concourse.bass as bass
from concourse import mybir

F32 = mybir.dt.float32
F32R = mybir.dt.float32r
I32 = mybir.dt.int32
U8 = mybir.dt.uint8
ALU = mybir.AluOpType
ACT = mybir.ActivationFunctionType

D_MODEL = 1024
SEQ = 512
DEC_BATCH = 8
DEC_SEQ = 8
D_FF = 2816
HEADS = 8
GROUPS = 64
GROUP_CH = 16
STATE = 64
EPS = 1e-6
GATE_FLOOR = 1e-30

P = 128
SAMPLE = DEC_BATCH * DEC_SEQ
T = SEQ + SAMPLE
HALF = T // 2
BANK = 512
NK = D_MODEL // P
CHUNKS = SEQ // P
F_GROUPS = (12, 10)
HALVINGS = (1, 2, 4, 8, 16, 32, 64)
LEVELS = 1 + len(HALVINGS)
SAMPLE_LEVELS = 4
LIFT = 8
BLOCKS = T // LIFT
PROMPT_BLOCKS = SEQ // LIFT
ST = GROUPS // 2
SUPER = 8
STEPS = PROMPT_BLOCKS // SUPER
ST_CT = ST // NK
G_CT = GROUPS // NK
UNIT = NK * 2 * P

VECS = ["ln_ffn1", "ln_mix", "ln_ffn2", "ln_final", "hgrn_lb_logits", "s5_d", "hgrn_gnorm"]


class Phase:

    def __init__(self, kind, name, pairs, kt, cols, at):
        self.kind, self.name, self.pairs, self.kt, self.cols = kind, name, pairs, kt, cols
        self.size = kt * cols * P
        self.pair0, self.tile0 = at["pair"], at["tile"]
        at["pair"] += pairs
        at["tile"] += pairs * cols

    def last_use(self, j):
        end = self.tile0 + self.pairs * self.cols
        return (1, end - 1 + j) if self.cols == 2 else (j, end)


def phases():
    at = {"pair": 0, "tile": NK // 2}
    out = []

    def ffn(name):
        for g, n in enumerate(F_GROUPS):
            out.append(Phase("up", (name, g), n // 2, NK, 2, at))
            out.append(Phase("down", (name, g), NK // 2, n, 1, at))

    ffn("ffn1_0")
    out.append(Phase("hgrn_in", ("hgrn", 0), HEADS, NK, 2, at))
    out.append(Phase("hgrn_out", ("hgrn", 0), NK // 2, NK, 1, at))
    ffn("ffn2_0")
    ffn("ffn1_1")
    out.append(Phase("glu", ("s5", 0), NK // 2, NK, 2, at))
    ffn("ffn2_1")
    return out, at


class Chain:

    def __init__(self, eng, sem):
        self.eng, self.sem, self.base, self.n = eng, sem, 0, 0

    def __call__(self, ins):
        self.n += 1
        ins.then_inc(self.sem, 1)
        self.eng.wait_ge(self.sem, self.base + self.n)

    def settle(self):
        done, self.base, self.n = self.n, self.base + self.n, 0
        return done


def build_trunk(nc, x_prompt, x_sample, state_hgrn, state_s5_re, state_s5_im, ln_ffn1, ffn1_w_in, ffn1_w_out,
                ln_mix, ln_ffn2, ffn2_w_in, ffn2_w_out, hgrn_lb_logits, hgrn_w_in, hgrn_gnorm, hgrn_w_out,
                s5_a_re, s5_a_im, s5_log_dt, s5_b_re, s5_b_im, s5_c_re, s5_c_im, s5_d, s5_w_glu, ln_final,
                y_prompt, y_sample, hgrn_p, re_p, im_p, hgrn_s, re_s, im_s):
    PH, END = phases()

    place = {"at": nc.sbuf_base + (-nc.sbuf_base) % 64}
    limit = nc.sbuf_usable_end

    def sb(name, shape, dt=F32, at=None):
        size = 1 if dt == U8 else 4
        for n in shape[1:]:
            size *= n
        size += -size % 32
        where = place["at"] if at is None else at
        if at is None:
            place["at"] += size
        assert where + size <= limit, (name, where + size, limit)
        return nc.alloc_sbuf_tensor_at(name, shape, dt, offset=where)

    x = sb("x", [P, NK, T])
    h_at = place["at"]
    h_hi = sb("h_hi", [P, NK, T], F32R)
    h_lo = sb("h_lo", [P, NK, T], F32R)
    w_raw = [sb(f"w_raw{j}", [P, UNIT]) for j in range(2)]
    w_hi = [sb(f"w_hi{j}", [P, UNIT], F32R) for j in range(2)]
    w_lo = [sb(f"w_lo{j}", [P, UNIT], F32R) for j in range(2)]
    rstd = sb("rstd", [P, T])
    ssq = sb("ssq", [P, T])
    sq = sb("sq", [P, T])
    ident = sb("ident", [P, P])
    ones = sb("ones", [P, P])
    eps_t = sb("eps_t", [P, 1])
    vec = sb("vec", [P, P])
    lb = sb("lb", [P, NK])
    lb_c = sb("lb_c", [P, NK])
    lb_t = sb("lb_t", [P, 4, NK])
    lam8 = sb("lam8", [P, 2, 2, ST])
    lam64 = sb("lam64", [P, 2, 2, ST])
    own_seq = sb("own_seq", [SAMPLE, DEC_BATCH])
    masks = sb("masks", [P, LEVELS, P], U8)
    masks_s = sb("masks_s", [SAMPLE, SAMPLE_LEVELS, SAMPLE], U8)
    overlay = place["at"]

    g_at = place["at"]
    g_hi = sb("g_hi", [P, F_GROUPS[0], T], F32R)
    g_lo = sb("g_lo", [P, F_GROUPS[0], T], F32R)
    t_a = sb("t_a", [P, T])
    t_b = sb("t_b", [P, T])
    t_s = sb("t_s", [P, T])
    t_g = sb("t_g", [P, T])
    dt_in = sb("dt_in", [P, 2])
    lam_c = sb("lam_c", [P, 3, ST])
    lam_sc = sb("lam_sc", [P, 24, ST])
    lam_p = sb("lam_p", [P, 2, ST, LIFT + 1])
    lam_r = sb("lam_r", [P, 2, ST, LIFT])
    b_in = sb("b_in", [P, 2, ST_CT, GROUP_CH])
    b_bar = sb("b_bar", [P, 2, ST_CT, GROUP_CH])
    b_blk = sb("b_blk", [P, 2, ST_CT, 2 * GROUP_CH])
    c_in = sb("c_in", [P, 2, 2, STATE])
    c_t = sb("c_t", [P, 2, ST_CT, GROUP_CH])
    start_at = place["at"]
    b_pow = sb("b_pow", [P, 2, ST_CT, LIFT * GROUP_CH])
    c_pow = sb("c_pow", [P, 2, ST_CT, (LIFT + 1) * GROUP_CH])
    p_t1 = sb("p_t1", [P, ST_CT * (LIFT + 1) * GROUP_CH])
    p_t2 = sb("p_t2", [P, ST_CT * (LIFT + 1) * GROUP_CH])
    mask_at = place["at"]
    wb_st = sb("wb_st", [P, 2, ST_CT, P])
    kz = sb("kz", [2 * GROUP_CH, ST_CT, (2 * LIFT - 1) * GROUP_CH])
    ffn_end = place["at"]
    assert place["at"] <= limit

    x_rows = sb("x_rows", [P, CHUNKS + 1, D_MODEL], at=g_at)

    place["at"] = overlay
    o_hi = sb("o_hi", [P, NK, T], F32R)
    o_lo = sb("o_lo", [P, NK, T], F32R)
    q_t = [sb(f"q_t{b}", [P, T]) for b in range(2)]
    k_t = [sb(f"k_t{b}", [P, T]) for b in range(2)]
    s_g = [sb(f"s_g{b}", [P, T]) for b in range(2)]
    f_t = sb("f_t", [P, T])
    v_t = sb("v_t", [P, T])
    pre = sb("pre", [P, T])
    e_t = sb("e_t", [P, 608])
    score = sb("score", [P, T])
    v_tok = sb("v_tok", [P, CHUNKS + 1, P])
    k_tok = sb("k_tok", [P, CHUNKS + 1, P])
    v_seq = sb("v_seq", [SAMPLE, DEC_BATCH, P])
    s_chunk = sb("s_chunk", [P, CHUNKS - 1, P])
    s_end = [sb(f"s_end{b}", [P, P]) for b in range(2)]
    s_in = [sb(f"s_in{b}", [P, DEC_BATCH, P]) for b in range(2)]
    s_out = [sb(f"s_out{b}", [P, DEC_BATCH, P]) for b in range(2)]
    o_rs = sb("o_rs", [P, T])
    assert place["at"] <= limit

    place["at"] = overlay
    u_at = place["at"]
    u_t = sb("u_t", [P, NK, T])
    lift_at = place["at"]
    u_lift = sb("u_lift", [P, GROUPS, BLOCKS])
    z_hi = sb("z_hi", [P, NK, T], F32R, at=u_at)
    z_lo = sb("z_lo", [P, NK, T], F32R, at=lift_at)
    turned = [sb(f"turned{b}", [BLOCKS, G_CT * P]) for b in range(4)]
    wb = [sb(f"wb{b}", [P, 2, ST_CT, P]) for b in range(2)]
    wc = [sb(f"wc{b}", [P, 2, ST_CT, P]) for b in range(2)]
    wi = [sb(f"wi{b}", [P, G_CT, P]) for b in range(2)]
    y_f = [sb(f"y_f{b}", [P, T]) for b in range(2)]
    z_t = [sb(f"z_t{b}", [P, T]) for b in range(2)]
    st_rows = sb("st_rows", [P, 2, 2, P])
    e_at = place["at"]
    s5_e = sb("s5_e", [P, 2, ST, SUPER])
    s5_b = sb("s5_b", [P, 2, ST, SUPER + 1])
    s5_fs = sb("s5_fs", [P, 2, DEC_BATCH, ST])
    fp_rows = sb("fp_rows", [ST, 2, P])
    fs_rows = sb("fs_rows", [P, 2, 2, P], at=e_at)
    assert place["at"] <= limit
    s5_v = sb("s5_v", [P, 2, ST, BLOCKS], at=h_at)
    s5_s = sb("s5_s", [P, 2, ST, BLOCKS], at=h_at + 4 * NK * T)

    y_n = sb("y_n", [P, NK, T], at=h_at)
    y_rows = sb("y_rows", [P, CHUNKS + 1, D_MODEL], at=g_at)

    vec_rows = sb("vec_rows", [P, P], at=start_at)
    lam_in = sb("lam_in", [P, P], at=start_at + 4 * P)
    m_i = [sb(f"m_i{n}", [P, P], I32, at=mask_at + 4 * P * n) for n in range(4)]
    m_f = [sb(f"m_f{n}", [P, P], F32, at=mask_at + 4 * P * (4 + n)) for n in range(4)]
    ps = nc.alloc_psum_tensor("ps", [P, 8, BANK], F32)

    wb_d = nc.dram_tensor("wb_d", (NK, P, 2, ST_CT, P), F32).ap()
    wc_d = nc.dram_tensor("wc_d", (NK, P, 2, ST_CT, P), F32).ap()
    wi_d = nc.dram_tensor("wi_d", (NK, P, G_CT, P), F32).ap()

    ctx = ExitStack()

    def sem(name):
        return ctx.enter_context(nc.semaphore(name))

    with ctx:
        begun = sem("begun")
        x_in = sem("x_in")
        vec_in = sem("vec_in")
        lam_ld = sem("lam_ld")
        consts = sem("consts")
        masks_made = sem("masks_made")
        vec_full = sem("vec_full")
        vec_done = sem("vec_done")
        dt_done = sem("dt_done")
        w_dma = [sem(f"w_dma{j}") for j in range(2)]
        w_hi_done = [sem(f"w_hi_done{j}") for j in range(2)]
        w_ready = [sem(f"w_ready{j}") for j in range(2)]
        full = [sem(f"full{s}") for s in range(2)]
        free = [sem(f"free{s}") for s in range(2)]
        dve_link = sem("dve_link")
        ssq_zero = sem("ssq_zero")
        sq_done = sem("sq_done")
        ssq_done = sem("ssq_done")
        norm_full = sem("norm_full")
        sd_done = sem("sd_done")
        rstd_done = sem("rstd_done")
        h_hi_done = sem("h_hi_done")
        h_ready = sem("h_ready")
        silu_done = sem("silu_done")
        g_full = sem("g_full")
        g_hi_done = sem("g_hi_done")
        g_ready = sem("g_ready")
        pin = sem("pin")
        ct_full = sem("ct_full")
        ct_done = sem("ct_done")
        bpart_done = sem("bpart_done")
        bl_full = sem("bl_full")
        wbst_done = sem("wbst_done")
        cpart_done = sem("cpart_done")
        tap_full = sem("tap_full")
        kz_done = sem("kz_done")
        pst = sem("pst")
        gates_done = sem("gates_done")
        sig_done = sem("sig_done")
        silu_g = sem("silu_g")
        sc_full = sem("sc_full")
        sc_read = sem("sc_read")
        qk_done = sem("qk_done")
        vt_full = sem("vt_full")
        vtok_done = sem("vtok_done")
        kt_full = sem("kt_full")
        ktok_done = sem("ktok_done")
        vseq_done = sem("vseq_done")
        decay_done = sem("decay_done")
        kvp_full = sem("kvp_full")
        kvs_full = sem("kvs_full")
        chain_done = sem("chain_done")
        s_out_done = sem("s_out_done")
        o_full = sem("o_full")
        osq_done = sem("osq_done")
        r_full = sem("r_full")
        osd_done = sem("osd_done")
        inv_done = sem("inv_done")
        on_done = sem("on_done")
        og_done = sem("og_done")
        o_hi_done = sem("o_hi_done")
        o_ready = sem("o_ready")
        s_ld = [sem(f"s_ld{b}") for b in range(2)]
        s_st = [sem(f"s_st{b}") for b in range(2)]
        rows_ld = sem("rows_ld")
        sin_full = sem("sin_full")
        sin_done = sem("sin_done")
        s0_zero = sem("s0_zero")
        wb_ld = [sem(f"wb_ld{b}") for b in range(2)]
        wy_ld = [sem(f"wy_ld{b}") for b in range(2)]
        u_done = sem("u_done")
        t1_full = sem("t1_full")
        t1_read = sem("t1_read")
        t2_full = sem("t2_full")
        t2_read = sem("t2_read")
        v_full = sem("v_full")
        v_read = sem("v_read")
        e_done = sem("e_done")
        b_done = sem("b_done")
        step_done = sem("step_done")
        scan_done = sem("scan_done")
        fs_done = sem("fs_done")
        f_full = sem("f_full")
        f_done = sem("f_done")
        f_st = sem("f_st")
        y_full = sem("y_full")
        y_read = sem("y_read")
        t3_full = sem("t3_full")
        t3_read = sem("t3_read")
        yy_done = sem("yy_done")
        gelu_done = sem("gelu_done")
        z_hi_done = sem("z_hi_done")
        z_ready = sem("z_ready")
        gs_done = sem("gs_done")
        yn_done = sem("yn_done")
        y_st = sem("y_st")

        TILE_END = END["tile"]
        up_at, at = {}, 0
        for p in PH:
            if p.kind == "up":
                up_at[p.name] = at
                at += 2 * p.pairs
        COL = {"ln_ffn1": 0, "ln_mix": 16, "ln_ffn2": 32, "ln_final": 48, "lb": 56, "s5_d": 72, "gnorm": 80}
        NVEC = 81
        NORMS = [(COL["ln_ffn1"], 0), (COL["ln_mix"], 1), (COL["ln_ffn2"], 2), (COL["ln_ffn1"] + NK, 3),
                 (COL["ln_mix"] + NK, None), (COL["ln_ffn2"] + NK, 4), (COL["ln_final"], None)]
        MAKES = {("down", ("ffn1_0", 1)): 1, ("hgrn_out", ("hgrn", 0)): 2, ("down", ("ffn2_0", 1)): 3,
                 ("down", ("ffn1_1", 1)): 4, ("glu", ("s5", 0)): 5, ("down", ("ffn2_1", 1)): 6}
        READS = {("up", ("ffn1_0", 0)): 0, ("hgrn_in", ("hgrn", 0)): 1, ("up", ("ffn2_0", 0)): 2,
                 ("up", ("ffn1_1", 0)): 3, ("up", ("ffn2_1", 0)): 5}

        def cols(t, i, n=1):
            flat = t[:].rearrange("p a b -> p (a b)")
            w = t.shape[2]
            return flat[:, bass.ds(i * w, n * w)]

        def halves(ap):
            return ap.rearrange("p (h t) -> p h t", h=2)

        def pair(s):
            return ps[:, 2 * s:2 * s + 2, 0:HALF]

        def f32(ap):
            return ap.bitcast(F32)

        def lifted(ap):
            return ap.rearrange("p (n t) -> p t n", t=LIFT)

        block = ctx.enter_context(nc.Block())

        @block.sync
        def _(sp):
            def load_rows(dst, src):
                sp.dma_start(dst, src).then_inc(vec_in, 16)

            at = 0
            for v, n in ((ln_ffn1, 16), (ln_mix, 16), (ln_ffn2, 16), (ln_final, 8), (hgrn_lb_logits, 16), (s5_d, 8)):
                flat = v.rearrange("l d -> (l d)") if len(v.shape) == 2 else v
                load_rows(vec_rows[at:at + n, :], flat.rearrange("(k c) -> k c", c=P))
                at += n
            load_rows(vec_rows[at:at + 1, :], hgrn_gnorm)
            assert at + 1 == NVEC

            def w_source(ph, j, i):
                kind, (name, g) = ph.kind, ph.name
                if kind in ("up", "down"):
                    layer = int(name[-1])
                    w_in, w_out = (ffn1_w_in, ffn1_w_out) if name[:4] == "ffn1" else (ffn2_w_in, ffn2_w_out)
                    f0 = g * F_GROUPS[0]
                if kind == "up":
                    v = w_in[layer].rearrange("(k p) (a f c) -> p k a f c", p=P, a=2, c=P)
                    return [v[:, :, a, i * 2 + (f0 + j), :] for a in range(2)]
                if kind == "down":
                    v = w_out[layer, f0 * P:(f0 + ph.kt) * P].rearrange("(k p) (m c) -> p k m c", p=P, c=P)
                    return [v[:, :, i * 2 + j, :]]
                if kind == "hgrn_in":
                    v = hgrn_w_in[0].rearrange("(k p) (r h c) -> p k r h c", p=P, r=4, c=P)
                    return [v[:, :, 2 * j + a, i, :] for a in range(2)]
                if kind == "hgrn_out":
                    return [hgrn_w_out[0].rearrange("(k p) (m c) -> p k m c", p=P, c=P)[:, :, i * 2 + j, :]]
                v = s5_w_glu[0].rearrange("(k p) (a m c) -> p k a m c", p=P, a=2, c=P)
                return [v[:, :, a, i * 2 + j, :] for a in range(2)]

            def load_pair(ph, i):
                for j in range(2):
                    sp.wait_ge(w_ready[j], i + ph.pair0)
                    sp.wait_ge(begun, 1)
                    dst = w_raw[j][:, 0:ph.size].rearrange("p (a k c) -> p a k c", a=ph.cols, c=P)
                    src = w_source(ph, j, i)
                    if ph.cols == 2:
                        for a in range(2):
                            sp.dma_start(dst[:, a], src[a]).then_inc(w_dma[j], 16)
                    else:
                        for r in range(2):
                            k0, k1 = r * ph.kt // 2, (r + 1) * ph.kt // 2
                            sp.dma_start(dst[:, 0, k0:k1], src[0][:, k0:k1]).then_inc(w_dma[j], 16)

            def load_piece(ct):
                sp.wait_ge(bpart_done, ct)
                sp.wait_ge(ct_full, ct)
                sp.wait_ge(begun, 1)
                for r, (b_d, c_d) in enumerate(((s5_b_re, s5_c_re), (s5_b_im, s5_c_im))):
                    b_v = b_d[0].rearrange("g p c -> (g p) c").rearrange("(a s q) c -> a q s c", s=ST_CT, q=P)
                    sp.dma_start(b_in[:, r], b_v[ct]).then_inc(pin, 16)
                    c_v = c_d[0].rearrange("g c p -> (g c) p").rearrange("(a q) p -> a q p", q=P)
                    for d in range(2):
                        sp.dma_start(c_in[:, r, d], c_v[ct]).then_inc(pin, 16)

            def store_piece(ct):
                sp.wait_ge(wbst_done, ct + 1)
                sp.dma_start(wb_d[ct], wb_st[:]).then_inc(pst, 16)
                sp.wait_ge(cpart_done, ct + 1)
                sp.dma_start(wc_d[ct].rearrange("p r s q -> p (r s) q"),
                             c_pow[:, :, :, GROUP_CH:].rearrange("p r s q -> p (r s) q")).then_inc(pst, 16)
                sp.wait_ge(kz_done, ct + 1)
                rows = wi_d[ct].rearrange("(t c) (s g) q -> t g c s q", c=GROUP_CH, g=2)
                for t in range(LIFT):
                    for g in range(2):
                        at = (LIFT - 1 - t) * GROUP_CH
                        sp.dma_start(rows[t, g], kz[GROUP_CH * g:GROUP_CH * (g + 1), :, at:at + P]).then_inc(pst, 16)

            def s_load(h, b):
                sp.dma_start(s_in[b][:], state_hgrn[0, :, h].rearrange("b k v -> k b v")).then_inc(s_ld[b], 16)

            def s_store(h, b):
                sp.wait_ge(s_out_done, h + 1)
                sp.wait_ge(begun, 1)
                sp.dma_start(hgrn_s[0, :, h].rearrange("b k v -> k b v"), s_out[b][:]).then_inc(s_st[b], 16)
                sp.wait_ge(chain_done, h + 1)
                sp.wait_ge(begun, 1)
                sp.dma_start(hgrn_p[0, 0, h], s_end[b][:]).then_inc(s_st[b], 16)

            sp.wait_ge(begun, 1)
            for ph in PH:
                makes_s5 = ph.kind == "down" and ph.name[0] == "ffn1_0"
                if ph.kind == "hgrn_in":
                    for i in range(2):
                        load_pair(ph, i)
                        if i == 0:
                            store_piece(NK - 1)
                            sp.wait_ge(h_ready, 2 * NK)
                            sp.wait_ge(pst, 288 * NK)
                        s_load(i, i)
                    with sp.Fori(1, HEADS // 2) as i:
                        for b in range(2):
                            load_pair(ph, i * 2 + b)
                            s_store(i * 2 + (b - 2), b)
                            sp.wait_ge(o_full, i * 2 + (b - 1))
                            sp.wait_ge(begun, 1)
                            s_load(i * 2 + b, b)
                elif makes_s5:
                    for i in range(ph.pairs):
                        ct = i + ph.name[1] * (NK // 2)
                        load_pair(ph, i)
                        load_piece(ct)
                        if ct:
                            store_piece(ct - 1)
                elif ph.kind == "glu":
                    load_pair(ph, 0)
                    sp.wait_ge(ssq_done, 5 * NK)
                    for r, s in enumerate((state_s5_re, state_s5_im)):
                        v = s[0].rearrange("b g p -> b (g p)").rearrange("b (s q) -> (b s) q", q=P)
                        sp.dma_start(st_rows[:, r], v.rearrange("(h r) q -> r h q", h=2)).then_inc(rows_ld, 16)
                    sp.wait_ge(pst, 288 * NK)
                    for ct in range(2):
                        sp.dma_start(wb[ct][:], wb_d[ct]).then_inc(wb_ld[ct], 16)
                        sp.dma_start(wc[ct][:], wc_d[ct]).then_inc(wy_ld[ct], 16)
                        sp.dma_start(wi[ct][:], wi_d[ct]).then_inc(wy_ld[ct], 16)
                    for ct in range(2, NK):
                        sp.wait_ge(v_full, ct - 1)
                        sp.dma_start(wb[ct % 2][:], wb_d[ct]).then_inc(wb_ld[ct % 2], 16)
                    for ct in range(2, NK):
                        sp.wait_ge(y_full, ct - 1)
                        sp.dma_start(wc[ct % 2][:], wc_d[ct]).then_inc(wy_ld[ct % 2], 16)
                        sp.dma_start(wi[ct % 2][:], wi_d[ct]).then_inc(wy_ld[ct % 2], 16)
                    sp.wait_ge(f_done, 2)
                    for r, s in enumerate((re_p, im_p)):
                        v = s[0, 0].rearrange("g p -> (g p)").rearrange("(s q) -> s q", q=P)
                        sp.dma_start(v, fp_rows[:, r]).then_inc(f_st, 16)
                    for r, s in enumerate((re_s, im_s)):
                        v = s[0].rearrange("b g p -> b (g p)").rearrange("b (s q) -> (b s) q", q=P)
                        sp.dma_start(v.rearrange("(h r) q -> r h q", h=2), fs_rows[:, r]).then_inc(f_st, 16)
                    with sp.Fori(1, ph.pairs) as i:
                        load_pair(ph, i)
                else:
                    with sp.Fori(0, ph.pairs) as i:
                        load_pair(ph, i)
                    if ph.kind == "hgrn_out":
                        for h in (HEADS - 2, HEADS - 1):
                            s_store(h, h % 2)
            for c in range(CHUNKS + 1):
                sp.wait_ge(free[c % 2], TILE_END + c // 2 + 1)
                if c < CHUNKS:
                    sp.dma_start(y_prompt[0, c * P:(c + 1) * P, :], y_rows[:, c, :]).then_inc(y_st, 16)
                else:
                    sp.dma_start(y_sample.rearrange("b t d -> (b t) d"), y_rows[0:SAMPLE, c, :]).then_inc(y_st, 16)
            sp.wait_ge(y_st, 16 * (CHUNKS + 1))
            sp.wait_ge(f_st, 64)
            sp.wait_ge(pst, 288 * NK)
            for b in range(2):
                sp.wait_ge(s_st[b], 32 * HEADS // 2)

        @block.gpsimd
        def _(pool):
            nc.gpsimd.memset(ident[:], 0.0).then_inc(begun, 1)
            nc.gpsimd.memset(ones[:], 1.0).then_inc(consts, 1)
            nc.gpsimd.memset(eps_t[:], EPS).then_inc(consts, 1)
            pool.wait_ge(begun, 1)
            nc.gpsimd.affine_select(out=ident[:], in_=ident[:], compare_op=ALU.not_equal, fill=1.0, base=0,
                                    pattern=[[-1, P]], channel_multiplier=1).then_inc(consts, 1)
            nc.gpsimd.iota(m_i[0][:], pattern=[[1, P]], base=0, channel_multiplier=0).then_inc(consts, 1)
            nc.gpsimd.iota(m_i[1][:], pattern=[[0, P]], base=0, channel_multiplier=1).then_inc(consts, 1)
            nc.gpsimd.memset(kz[:], 0.0).then_inc(consts, 1)
            nc.gpsimd.memset(b_blk[:], 0.0).then_inc(consts, 1)
            nc.gpsimd.memset(own_seq[:], 1.0).then_inc(consts, 1)
            pool.wait_ge(consts, 8)
            nc.gpsimd.affine_select(out=own_seq[:], in_=own_seq[:], compare_op=ALU.is_ge, fill=0.0, base=0,
                                    pattern=[[-DEC_SEQ, DEC_BATCH]], channel_multiplier=1).then_inc(consts, 1)
            pool.wait_ge(consts, 9)
            nc.gpsimd.affine_select(out=own_seq[:], in_=own_seq[:], compare_op=ALU.is_ge, fill=0.0, base=DEC_SEQ - 1,
                                    pattern=[[DEC_SEQ, DEC_BATCH]], channel_multiplier=-1).then_inc(consts, 1)

            def rest(ph, j, i):
                pool.wait_ge(w_hi_done[j], i + (ph.pair0 + 1))
                n = ph.size
                nc.gpsimd.tensor_tensor(w_lo[j][:, 0:n], w_raw[j][:, 0:n], f32(w_hi[j][:, 0:n]), ALU.subtract)\
                    .then_inc(w_ready[j], 1)

            def states(m, b, turn):
                pool.wait_ge(s_ld[b], turn * 16 + 16)
                pool.wait_ge(s_st[b], turn * 32)
                pool.wait_ge(kvs_full, m)
                pool.wait_ge(vtok_done, m + 1)
                nc.gpsimd.tensor_tensor(
                    v_seq[:], v_tok[0:SAMPLE, CHUNKS, :].unsqueeze(1).to_broadcast([SAMPLE, DEC_BATCH, P]),
                    own_seq[:].unsqueeze(2).to_broadcast([SAMPLE, DEC_BATCH, P]), ALU.mult).then_inc(vseq_done, 1)
                pool.wait_ge(qk_done, m * LEVELS + SAMPLE_LEVELS)
                nc.gpsimd.tensor_tensor(
                    s_out[b][:], s_in[b][:],
                    e_t[:, 432 + PROMPT_BLOCKS:432 + BLOCKS].unsqueeze(2).to_broadcast([P, DEC_BATCH, P]),
                    ALU.mult).then_inc(decay_done, 1)

            for n, ph in enumerate(PH):
                if ph.kind == "hgrn_in":
                    rest(ph, 0, 0)
                    rest(ph, 1, 0)
                    rest(ph, 0, 1)
                    with pool.Fori(0, HEADS // 2 - 1) as i:
                        rest(ph, 1, i * 2 + 1)
                        states(i * 2, 0, i)
                        rest(ph, 0, i * 2 + 2)
                        rest(ph, 1, i * 2 + 2)
                        states(i * 2 + 1, 1, i)
                        rest(ph, 0, i * 2 + 3)
                    rest(ph, 1, HEADS - 1)
                    states(HEADS - 2, 0, HEADS // 2 - 1)
                    rest(PH[n + 1], 0, 0)
                    states(HEADS - 1, 1, HEADS // 2 - 1)
                    rest(PH[n + 1], 1, 0)
                else:
                    with pool.Fori(int(ph.kind == "hgrn_out"), ph.pairs) as i:
                        for j in range(2):
                            rest(ph, j, i)

        @block.scalar
        def _(act):
            act.dma_start(x_rows[:, 0:CHUNKS, :], x_prompt[0].rearrange("(c p) d -> p c d", p=P)).then_inc(x_in, 16)
            act.dma_start(x_rows[0:SAMPLE, CHUNKS, :], x_sample.rearrange("b t d -> (b t) d")).then_inc(x_in, 16)
            lam_rows = s5_a_re[0].rearrange("g p -> (g p)").rearrange("(s q) -> s q", q=P)
            act.dma_start(lam_in[0:ST, :], lam_rows).then_inc(lam_ld, 16)
            lam_rows = s5_a_im[0].rearrange("g p -> (g p)").rearrange("(s q) -> s q", q=P)
            act.dma_start(lam_in[ST:2 * ST, :], lam_rows).then_inc(lam_ld, 16)
            act.dma_start(dt_in[2 * ST:3 * ST, :], s5_log_dt[0].rearrange("(s g) -> s g", g=2)).then_inc(lam_ld, 16)

            def split(ph, j, i, prev, i_prev):
                if prev is not None:
                    if i_prev is None:
                        s, n = prev.last_use(j)
                        act.wait_ge(full[s], n)
                    elif prev.cols == 2:
                        act.wait_ge(full[1], i_prev * 2 + (prev.tile0 + j + 1))
                    else:
                        act.wait_ge(full[j], i_prev + (prev.tile0 + 1))
                act.wait_ge(w_dma[j], i * 32 + (ph.pair0 * 32 + 32))
                nc.scalar.activation(w_hi[j][:, 0:ph.size], w_raw[j][:, 0:ph.size], ACT.Copy).then_inc(w_hi_done[j], 1)

            def split_next(n, ph, j, i, last):
                if j == 0:
                    if isinstance(i, int) and i == 0:
                        split(ph, 1, 0, PH[n - 1] if n else None, None)
                    else:
                        split(ph, 1, i, ph, i - 1)
                elif not last:
                    split(ph, 0, i + 1, ph, i)
                elif n + 1 < len(PH):
                    split(PH[n + 1], 0, 0, ph, None)

            def norm_tile(r, m, taken):
                gain, fill = NORMS[r]
                act.wait_ge(*taken)
                act.wait_ge(ssq_done, m + r * NK)
                act.wait_ge(begun, 1)
                if fill is not None:
                    nc.scalar.activation(cols(h_hi, m), cols(x, m), ACT.Copy, scale=vec[:, bass.ds(m + gain, 1)])\
                        .then_inc(h_hi_done, 1)
                nc.scalar.activation(sq[:], cols(x, m), ACT.Square).then_inc(sq_done, 1)

            def root(r):
                act.wait_ge(norm_full, r + 1)
                nc.scalar.activation(halves(sq[:]), ps[:, 4:6, 0:HALF], ACT.Sqrt, scale=1.0 / D_MODEL, bias=eps_t[:])\
                    .then_inc(sd_done, 1)

            act.wait_ge(vec_full, 1)
            nc.scalar.activation(vec[:, 0:NVEC], ps[:, 6, 0:NVEC], ACT.Copy).then_inc(vec_done, 1)
            act.wait_ge(vec_done, 1)
            for m in range(NK):
                norm_tile(0, m, (free[m % 2], m // 2 + 1))
            split(PH[0], 0, 0, None, None)

            def ffn_up(n, ph):
                base = up_at[ph.name]

                def unit(i, j, last=False):
                    u = i * 2 + (base + j)
                    t = i * 2 + (ph.tile0 + j)
                    split_next(n, ph, j, i, last)
                    if ph.name[1] == 0 and j == 0 and isinstance(i, int) and i == 0:
                        root(READS[(ph.kind, ph.name)])
                    act.wait_ge(free[0], t + 1)
                    act.wait_ge(g_full, u)
                    nc.scalar.activation(t_s[:], t_a[:], ACT.Silu).then_inc(silu_done, 1)
                    act.wait_ge(g_full, u + 1)
                    act.wait_ge(begun, 1)
                    nc.scalar.activation(cols(g_hi, i * 2 + j), t_g[:], ACT.Copy).then_inc(g_hi_done, 1)

                for j in range(2):
                    unit(0, j)
                with act.Fori(1, ph.pairs - 1) as i:
                    for j in range(2):
                        unit(i, j)
                for j in range(2):
                    unit(ph.pairs - 1, j, last=True)

            def ffn_down(n, ph):
                r = MAKES.get((ph.kind, ph.name))
                pieces = ph.kind == "down" and ph.name[0] == "ffn1_0"

                def unit(i, j, last=False):
                    split_next(n, ph, j, i, last)
                    if pieces:
                        ct = i + ph.name[1] * (NK // 2)
                        if j == 0:
                            act.wait_ge(ct_full, ct + 1)
                            act.wait_ge(cpart_done, ct)
                            v = ps[:, 7, 0:2 * P].rearrange("p (q g c) -> p q g c", g=2, c=GROUP_CH)
                            o = c_t[:].rearrange("p r s c -> p (r s) c")
                            nc.scalar.activation(o[0:STATE], v[0:STATE, :, 0], ACT.Copy)
                            nc.scalar.activation(o[STATE:P], v[STATE:P, :, 1], ACT.Copy).then_inc(ct_done, 1)
                            act.wait_ge(bl_full, ct + 1)
                            act.wait_ge(pst, ct * 288)
                            for q in range(2):
                                ins = nc.scalar.activation(wb_st[:, q].rearrange("p s q -> p (s q)"), ps[:, 4 + q, :],
                                                           ACT.Copy)
                            ins.then_inc(wbst_done, 1)
                    if r is not None:
                        norm_tile(r, i * 2 + j, (free[j], i + (ph.tile0 + 1)))
                    if pieces and j == 1:
                        act.wait_ge(tap_full, ct_of(i) + 1)
                        nc.scalar.activation(kz[:, :, P - GROUP_CH:],
                                             ps[0:2 * GROUP_CH, 6, :].rearrange("p (s q) -> p s q", q=P), ACT.Copy)\
                            .then_inc(kz_done, 1)

                def ct_of(i):
                    return i + ph.name[1] * (NK // 2)

                for j in range(2):
                    unit(0, j)
                with act.Fori(1, ph.pairs - 1) as i:
                    for j in range(2):
                        unit(i, j)
                for j in range(2):
                    unit(ph.pairs - 1, j, last=True)

            def hgrn(n_ph, ph):
                def project_f(n, b):
                    act.wait_ge(free[1], n * 2 + (ph.tile0 + 1))
                    nc.scalar.activation(k_t[b][:], pre[:], ACT.Sigmoid, scale=-1.0).then_inc(sig_done, 1)
                    if not isinstance(n, int) or n:
                        act.wait_ge(qk_done, n * LEVELS - (LEVELS - 2))
                    nc.scalar.activation(f_t[:], pre[:], ACT.Sigmoid).then_inc(sig_done, 1)

                def project_g(n, b):
                    act.wait_ge(free[1], n * 2 + (ph.tile0 + 2))
                    nc.scalar.activation(s_g[b][:], pre[:], ACT.Silu).then_inc(silu_g, 1)

                def take_turned(m, bank_done, dst, done):
                    act.wait_ge(bank_done, m + 1)
                    if not isinstance(m, int) or m:
                        act.wait_ge(o_full, m)
                    nc.scalar.activation(dst[:, 0:CHUNKS, :].rearrange("p c q -> p (c q)"), ps[:, 6, :], ACT.Copy)
                    nc.scalar.activation(dst[0:SAMPLE, CHUNKS, :], ps[0:SAMPLE, 7, 0:P], ACT.Copy).then_inc(done, 1)

                def tail(m):
                    take_turned(m, kt_full, k_tok, ktok_done)
                    act.wait_ge(o_full, m + 1)
                    if not isinstance(m, int) or m:
                        act.wait_ge(og_done, m)
                    nc.scalar.activation(sq[:, 0:SEQ], ps[:, 5, :], ACT.Square)
                    nc.scalar.activation(sq[:, SEQ:T], ps[:, 4, 0:SAMPLE], ACT.Square).then_inc(osq_done, 1)
                    act.wait_ge(r_full, m + 1)
                    nc.scalar.activation(halves(sq[:]), ps[:, 6:8, 0:HALF], ACT.Sqrt, scale=1.0 / P, bias=eps_t[:])\
                        .then_inc(osd_done, 1)

                def o_high(head):
                    if head is not None:
                        act.wait_ge(og_done, head + 1)
                        act.wait_ge(begun, 1)
                        nc.scalar.activation(cols(o_hi, head), ssq[:], ACT.Copy).then_inc(o_hi_done, 1)

                def step(n, b, m, before, last=False):
                    if n is not None:
                        if isinstance(n, int) and n == 0:
                            split(ph, 1, 0, PH[n_ph - 1], None)
                            root(READS[(ph.kind, ph.name)])
                        else:
                            split(ph, 1, n, ph, n - 1)
                        project_f(n, b)
                    if m is not None:
                        act.wait_ge(pst, 288 * NK)
                        take_turned(m, vt_full, v_tok, vtok_done)
                    if n is not None:
                        if last:
                            split(PH[n_ph + 1], 0, 0, ph, None)
                        else:
                            split(ph, 0, n + 1, ph, n)
                    o_high(before)
                    if n is not None:
                        project_g(n, b)
                    if m is not None:
                        tail(m)

                step(0, 0, None, None)
                step(1, 1, 0, None)
                with act.Fori(0, HEADS // 2 - 2) as i:
                    step(i * 2 + 2, 0, i * 2 + 1, i * 2)
                    step(i * 2 + 3, 1, i * 2 + 2, i * 2 + 1)
                step(HEADS - 2, 0, HEADS - 3, HEADS - 4)
                step(HEADS - 1, 1, HEADS - 2, HEADS - 3, last=True)
                step(None, 0, HEADS - 1, HEADS - 2)
                step(None, 0, None, HEADS - 1)

            def s5(n, ph):
                root(4)
                act.wait_ge(sin_full, 1)
                for q in range(2):
                    v = ps[:, 6, 2 * P * q:2 * P * (q + 1)].rearrange("p (b s) -> p b s", s=ST)
                    ins = nc.scalar.activation(s5_s[:, q, :, PROMPT_BLOCKS:].rearrange("p s b -> p b s"), v, ACT.Copy)
                ins.then_inc(sin_done, 1)
                def take_v(ct):
                    act.wait_ge(v_full, ct + 1)
                    b = 4 + 2 * (ct % 2)
                    o = s5_v[:, :, ST_CT * ct:ST_CT * (ct + 1), :].rearrange("p r s n -> p r (s n)")
                    nc.scalar.activation(o, ps[:, b:b + 2, 0:HALF], ACT.Copy).then_inc(v_read, 1)

                for at in range(NK + 2):
                    if at < NK:
                        act.wait_ge(t1_full, at + 1)
                        if at >= 2:
                            act.wait_ge(t2_full, at - 1)
                        o = turned[at % 2][:].rearrange("n (g t c) -> n t g c", g=G_CT, t=LIFT)
                        for h in range(2):
                            v = ps[0:BLOCKS, h, :].rearrange("n (t g c) -> n t g c", g=G_CT, c=GROUP_CH)
                            ins = nc.scalar.activation(o[:, 4 * h:4 * h + 4], v, ACT.Copy)
                        ins.then_inc(t1_read, 1)
                    if at >= 2:
                        take_v(at - 2)
                    if 1 <= at <= NK:
                        ct = at - 1
                        act.wait_ge(t2_full, ct + 1)
                        o = u_lift[:, G_CT * ct:G_CT * (ct + 1), :].rearrange("p g n -> p (g n)")
                        nc.scalar.activation(halves(o), pair(1), ACT.Copy).then_inc(t2_read, 1)

                def take_y(ct):
                    act.wait_ge(y_full, ct + 1)
                    if ct >= 4:
                        act.wait_ge(t3_full, ct - 3)
                    o = turned[ct % 4][:].rearrange("n (t s g c) -> n g s t c", t=LIFT, g=2, c=GROUP_CH)
                    for g in range(2):
                        v = ps[0:BLOCKS, 4 + 2 * (ct % 2) + g, :].rearrange("n (s t c) -> n s t c", t=LIFT, c=GROUP_CH)
                        ins = nc.scalar.activation(o[:, g], v, ACT.Copy)
                    ins.then_inc(y_read, 1)

                def gelu(ct):
                    act.wait_ge(yy_done, ct + 1)
                    if ct >= 2:
                        act.wait_ge(z_ready, ct - 1)
                    nc.scalar.activation(z_t[ct % 2][:], y_f[ct % 2][:], ACT.Gelu_apprx_tanh).then_inc(gelu_done, 1)
                    act.wait_ge(gelu_done, ct + 1)
                    nc.scalar.activation(lifted(z_hi[:, ct]), z_t[ct % 2][:].rearrange("p (t n) -> p t n", t=LIFT),
                                         ACT.Copy).then_inc(z_hi_done, 1)

                for ct in range(5):
                    take_y(ct)
                act.wait_ge(f_full, 1)
                nc.scalar.activation(fp_rows[:].rearrange("p r q -> p (r q)"), ps[0:ST, 0, 0:2 * P], ACT.Copy)\
                    .then_inc(f_done, 1)
                act.wait_ge(f_full, 2)
                nc.scalar.activation(fs_rows[:].rearrange("p r h q -> p (r h q)"), ps[:, 1, :], ACT.Copy)\
                    .then_inc(f_done, 1)
                gelu(0)
                gelu(1)
                for ct in range(5, NK):
                    take_y(ct)
                    gelu(2 * (ct - 4))
                    gelu(2 * (ct - 4) + 1)

                def unit(i, j, last=False):
                    split_next(n, ph, j, i, last)
                    t = i * 2 + (ph.tile0 + j)
                    act.wait_ge(full[1], t + 1)
                    act.wait_ge(gs_done, i * 2 + j)
                    nc.scalar.activation(halves(t_s[:]), pair(1), ACT.Sigmoid).then_inc(free[1], 1)
                    norm_tile(5, i * 2 + j, (gs_done, i * 2 + (j + 1)))

                for j in range(2):
                    unit(0, j)
                with act.Fori(1, ph.pairs - 1) as i:
                    for j in range(2):
                        unit(i, j)
                for j in range(2):
                    unit(ph.pairs - 1, j, last=True)

            for n, ph in enumerate(PH):
                {"up": ffn_up, "down": ffn_down, "hgrn_in": hgrn, "hgrn_out": ffn_down, "glu": s5}[ph.kind](n, ph)
            root(6)
            for c in range(1, CHUNKS + 1, 2):
                act.wait_ge(full[1], TILE_END + c // 2 + 1)
                nc.scalar.activation(y_rows[:, c, :].rearrange("p (h d) -> p h d", h=2), ps[:, 2:4, :], ACT.Copy)\
                    .then_inc(free[1], 1)

        @block.vector
        def _(dve):
            link = Chain(dve, dve_link)
            V = nc.vector

            def norm_tile(r, m):
                gain, fill = NORMS[r]
                if fill is not None:
                    dve.wait_ge(h_hi_done, m + (fill * NK + 1))
                    V.scalar_tensor_tensor(out=cols(h_lo, m), in0=cols(x, m), scalar=vec[:, bass.ds(m + gain, 1)],
                                           in1=f32(cols(h_hi, m)), op0=ALU.mult, op1=ALU.subtract).then_inc(h_ready, 1)
                dve.wait_ge(ssq_done, m + r * NK)
                dve.wait_ge(sq_done, m + (r * NK + 1))
                V.tensor_tensor(ssq[:], ssq[:], sq[:], ALU.add).then_inc(ssq_done, 1)

            def clear_ssq(r):
                if r:
                    dve.wait_ge(norm_full, r)
                V.memset(ssq[:], 0.0).then_inc(ssq_zero, 1)
                dve.wait_ge(ssq_zero, r + 1)

            def reciprocal(r):
                dve.wait_ge(sd_done, r + 1)
                V.reciprocal(rstd[:], sq[:]).then_inc(rstd_done, 1)
                dve.wait_ge(rstd_done, r + 1)

            def scaled(dst, s):
                return V.tensor_tensor(halves(dst), pair(s), halves(rstd[:]), ALU.mult)

            clear_ssq(0)
            for m in range(NK):
                s = m % 2
                dve.wait_ge(full[s], m // 2 + 1)
                V.tensor_copy(x[:, m, 0:SEQ], ps[:, 2 * s, :])
                V.tensor_copy(x[:, m, SEQ:T], ps[:, 2 * s + 1, 0:SAMPLE]).then_inc(free[s], 1)
                norm_tile(0, m)
            dve.wait_ge(lam_ld, 48)
            V.tensor_copy(lam_in[2 * ST:3 * ST].rearrange("s (g p) -> s g p", g=2),
                          dt_in[2 * ST:3 * ST].unsqueeze(2).to_broadcast([ST, 2, STATE])).then_inc(dt_done, 1)

            def bounds():
                a0, a1 = vec[:, COL["lb"]:COL["lb"] + NK], vec[:, COL["lb"] + NK:COL["lb"] + 2 * NK]
                dve.wait_ge(vec_done, 1)
                link(V.tensor_tensor(lb_t[:, 0], a0, a1, ALU.max))
                link(V.tensor_tensor(lb_t[:, 1], a0, lb_t[:, 0], ALU.subtract))
                link(V.tensor_tensor(lb_t[:, 2], a1, lb_t[:, 0], ALU.subtract))
                link(exp_of(lb_t[:, 1:3, :].rearrange("p a b -> p (a b)"), 2 * NK))
                link(V.tensor_tensor(lb_t[:, 0], lb_t[:, 1], lb_t[:, 2], ALU.add))
                link(V.reciprocal(lb_t[:, 0], lb_t[:, 0]))
                link(V.tensor_tensor(lb_t[:, 1], lb_t[:, 1], lb_t[:, 0], ALU.mult))
                link(V.tensor_tensor(lb_t[:, 2], lb_t[:, 1], lb_t[:, 1], ALU.subtract))
                link(V.tensor_scalar(lb[:], lb_t[:, 2], 0.0, 1.0 - 1e-4, ALU.max, ALU.min))
                link(V.tensor_scalar(lb_c[:], lb[:], -1.0, 1.0, ALU.mult, ALU.add))

            def exp_of(v, w):
                n, r, y = (lam_sc[:, k, 0:w] for k in (20, 21, 22))
                n_i = lam_sc[:, 23, 0:w].bitcast(I32)
                round_ = 1.5 * 2.0 ** 23
                link(V.tensor_scalar(v, v, -87.0, 88.0, ALU.max, ALU.min))
                link(V.tensor_scalar(n, v, 1.4426950408889634, round_, ALU.mult, ALU.add))
                link(V.tensor_scalar(n, n, -round_, None, ALU.add))
                link(V.scalar_tensor_tensor(out=r, in0=n, scalar=-0.693359375, in1=v, op0=ALU.mult, op1=ALU.add))
                link(V.scalar_tensor_tensor(out=r, in0=n, scalar=2.12194440e-4, in1=r, op0=ALU.mult, op1=ALU.add))
                link(V.tensor_scalar(y, r, 1.0 / 5040, None, ALU.mult))
                for c in (1.0 / 720, 1.0 / 120, 1.0 / 24, 1.0 / 6, 0.5, 1.0):
                    link(V.scalar_tensor_tensor(out=y, in0=y, scalar=c, in1=r, op0=ALU.add, op1=ALU.mult))
                link(V.tensor_scalar(y, y, 1.0, None, ALU.add))
                link(V.tensor_scalar(n_i, n, 127.0, 2.0 ** 23, ALU.add, ALU.mult))
                return V.tensor_tensor(v, y, n_i.bitcast(F32), ALU.mult)

            def make_masks():
                dve.wait_ge(consts, 5)
                query, key, differ, v = m_i[0][:], m_i[1][:], m_i[2][:], m_f[0][:]
                link(V.tensor_tensor(differ, query, key, ALU.bitwise_xor))
                link(V.tensor_tensor(m_f[1][:], query, key, ALU.is_gt))
                link(V.tensor_tensor(v, differ, m_f[1][:], ALU.mult))
                link(V.tensor_tensor(masks[:, 0, :], query, key, ALU.is_equal))
                link(V.tensor_copy(masks_s[:, 0, :], masks[0:SAMPLE, 0, 0:SAMPLE]))
                link(V.tensor_scalar(m_f[2][:], v, float(DEC_SEQ), None, ALU.is_lt))
                for n, half in enumerate(HALVINGS):
                    link(V.tensor_scalar(m_f[3][:], v, float(half), None, ALU.is_ge))
                    link(V.tensor_copy(masks[:, n + 1, :], m_f[3][:]))
                    if n + 1 < SAMPLE_LEVELS:
                        link(V.tensor_tensor(masks_s[:, n + 1, :], m_f[3][0:SAMPLE, 0:SAMPLE],
                                             m_f[2][0:SAMPLE, 0:SAMPLE], ALU.mult))

            def row(k):
                return lam_sc[:, k, :]

            a_re, a_im, dt = (lam_c[:, k, :] for k in range(3))

            def step_sizes():
                dve.wait_ge(vec_full, 2)
                link(V.tensor_copy(lam_c[:].rearrange("p k s -> p (k s)"), ps[:, 7, 0:3 * ST]))
                link(exp_of(dt, ST))
                link(V.tensor_tensor(row(0), a_re, dt, ALU.mult))
                link(V.tensor_tensor(row(1), a_im, dt, ALU.mult))
                link(exp_of(row(0), ST))

            def lambda_bar():
                round_ = 1.5 * 2.0 ** 23
                link(V.tensor_scalar(row(2), row(1), 0.15915494309189535, round_, ALU.mult, ALU.add))
                link(V.tensor_scalar(row(2), row(2), -round_, None, ALU.add))
                for part in (-6.28125, -1.9353071795864769e-3):
                    link(V.scalar_tensor_tensor(out=row(1), in0=row(2), scalar=part, in1=row(1), op0=ALU.mult, op1=ALU.add))
                link(V.tensor_scalar(row(1), row(1), 3.1415925, -3.1415925, ALU.min, ALU.max))
                link(V.tensor_scalar(row(3), row(1), 0.5, None, ALU.mult))
                link(V.tensor_tensor(row(4), row(3), row(3), ALU.mult))
                link(V.tensor_scalar(row(5), row(4), 1.0 / 6227020800, None, ALU.mult))
                for c in (-1.0 / 39916800, 1.0 / 362880, -1.0 / 5040, 1.0 / 120, -1.0 / 6):
                    link(V.scalar_tensor_tensor(out=row(5), in0=row(5), scalar=c, in1=row(4), op0=ALU.add, op1=ALU.mult))
                link(V.scalar_tensor_tensor(out=row(5), in0=row(5), scalar=1.0, in1=row(3), op0=ALU.add, op1=ALU.mult))
                link(V.tensor_scalar(row(6), row(4), 1.0 / 479001600, None, ALU.mult))
                for c in (-1.0 / 3628800, 1.0 / 40320, -1.0 / 720, 1.0 / 24, -0.5):
                    link(V.scalar_tensor_tensor(out=row(6), in0=row(6), scalar=c, in1=row(4), op0=ALU.add, op1=ALU.mult))
                link(V.tensor_scalar(row(6), row(6), 1.0, 2.0, ALU.add, ALU.mult))
                link(V.tensor_tensor(row(6), row(6), row(5), ALU.mult))
                link(V.tensor_tensor(row(7), row(5), row(5), ALU.mult))
                link(V.tensor_scalar(row(7), row(7), -2.0, None, ALU.mult))
                link(V.tensor_tensor(row(11), row(0), row(6), ALU.mult))
                link(V.tensor_tensor(row(10), row(0), row(7), ALU.mult))
                link(V.tensor_scalar(row(12), row(0), -1.0, None, ALU.add))
                link(V.tensor_tensor(row(10), row(10), row(12), ALU.add))

            def b_factor():
                link(V.tensor_tensor(row(12), a_re, a_re, ALU.mult))
                link(V.tensor_tensor(row(13), a_im, a_im, ALU.mult))
                link(V.tensor_tensor(row(12), row(12), row(13), ALU.add))
                link(V.reciprocal(row(12), row(12)))
                link(V.tensor_tensor(row(13), row(10), a_re, ALU.mult))
                link(V.tensor_tensor(row(14), row(11), a_im, ALU.mult))
                link(V.tensor_tensor(row(13), row(13), row(14), ALU.add))
                link(V.tensor_tensor(row(8), row(13), row(12), ALU.mult))
                link(V.tensor_tensor(row(13), row(11), a_re, ALU.mult))
                link(V.tensor_tensor(row(14), row(10), a_im, ALU.mult))
                link(V.tensor_tensor(row(13), row(13), row(14), ALU.subtract))
                link(V.tensor_tensor(row(9), row(13), row(12), ALU.mult))

            def powers():
                link(V.memset(lam_p[:, 0, :, 0:1], 1.0))
                link(V.memset(lam_p[:, 1, :, 0:1], 0.0))
                link(V.tensor_scalar(lam_p[:, 0, :, 1], row(10), 1.0, None, ALU.add))
                link(V.tensor_copy(lam_p[:, 1, :, 1], row(11)))
                for n in (1, 2, 4):
                    a_r, a_i = (lam_p[:, q, :, 1:n + 1] for q in range(2))
                    b_r, b_i = (lam_p[:, q, :, n:n + 1].to_broadcast([P, ST, n]) for q in range(2))
                    o_r, o_i = (lam_p[:, q, :, n + 1:2 * n + 1] for q in range(2))
                    t = p_t1[:, 0:ST * n].rearrange("p (s n) -> p s n", n=n)
                    link(V.tensor_tensor(o_r, a_r, b_r, ALU.mult))
                    link(V.tensor_tensor(t, a_i, b_i, ALU.mult))
                    link(V.tensor_tensor(o_r, o_r, t, ALU.subtract))
                    link(V.tensor_tensor(o_i, a_r, b_i, ALU.mult))
                    link(V.tensor_tensor(t, a_i, b_r, ALU.mult))
                    link(V.tensor_tensor(o_i, o_i, t, ALU.add))
                for q in range(2):
                    link(V.tensor_copy(lam_r[:, q], lam_p[:, q, :, 0:LIFT][:, :, ::-1]))
                link(V.tensor_copy(lam8[:, 0, 0], lam_p[:, 0, :, LIFT]))
                link(V.tensor_copy(lam8[:, 0, 1], lam_p[:, 0, :, LIFT]))
                link(V.tensor_copy(lam8[:, 1, 0], lam_p[:, 1, :, LIFT]))
                link(V.tensor_scalar(lam8[:, 1, 1], lam_p[:, 1, :, LIFT], -1.0, None, ALU.mult))
                link(V.tensor_copy(row(12), lam_p[:, 0, :, LIFT]))
                link(V.tensor_copy(row(13), lam_p[:, 1, :, LIFT]))
                for _ in range(3):
                    link(V.tensor_tensor(row(14), row(12), row(12), ALU.mult))
                    link(V.tensor_tensor(row(15), row(13), row(13), ALU.mult))
                    link(V.scalar_tensor_tensor(out=row(13), in0=row(12), scalar=2.0, in1=row(13), op0=ALU.mult, op1=ALU.mult))
                    link(V.tensor_tensor(row(12), row(14), row(15), ALU.subtract))
                link(V.tensor_copy(lam64[:, 0, 0], row(12)))
                link(V.tensor_copy(lam64[:, 0, 1], row(12)))
                link(V.tensor_copy(lam64[:, 1, 0], row(13)))
                link(V.tensor_scalar(lam64[:, 1, 1], row(13), -1.0, None, ALU.mult))

            def complex_mult(out_r, out_i, a, b, t1, t2, done, negate_i=False):
                (a_r, a_i), (b_r, b_i) = a, b
                link(V.tensor_tensor(t1, a_r, b_r, ALU.mult))
                link(V.tensor_tensor(t2, a_i, b_i, ALU.mult))
                link(V.tensor_tensor(out_r, t1, t2, ALU.subtract))
                link(V.tensor_tensor(t1, a_r, b_i, ALU.mult))
                link(V.tensor_tensor(t2, a_i, b_r, ALU.mult))
                if negate_i:
                    done(V.scalar_tensor_tensor(out=out_i, in0=t1, scalar=-1.0, in1=t2, op0=ALU.mult, op1=ALU.subtract))
                else:
                    done(V.tensor_tensor(out_i, t1, t2, ALU.add))

            def of_ct(row, ct):
                return lam_sc[:, row, bass.ds(ct * ST_CT, ST_CT)].unsqueeze(2).to_broadcast([P, ST_CT, GROUP_CH])

            def b_part(ct):
                dve.wait_ge(pin, ct * 96 + 96)
                dve.wait_ge(bl_full, ct)
                dve.wait_ge(tap_full, ct)
                t1, t2 = (t[:, 0:ST_CT * GROUP_CH].rearrange("p (s c) -> p s c", s=ST_CT) for t in (p_t1, p_t2))
                complex_mult(b_bar[:, 0], b_bar[:, 1], (b_in[:, 0], b_in[:, 1]), (of_ct(8, ct), of_ct(9, ct)), t1, t2,
                             link)
                for g in range(2):
                    rows = slice(STATE * g, STATE * (g + 1))
                    link(V.tensor_copy(
                        b_blk[rows, :, :, GROUP_CH * g:GROUP_CH * (g + 1)].rearrange("p r s c -> p (r s) c"),
                        b_bar[rows].rearrange("p r s c -> p (r s) c")))
                shape = [P, ST_CT, LIFT, GROUP_CH]
                t1, t2 = (t[:, 0:ST_CT * P].rearrange("p (s t c) -> p s t c", s=ST_CT, t=LIFT) for t in (p_t1, p_t2))
                power = [lam_r[:, q, bass.ds(ct * ST_CT, ST_CT), :].unsqueeze(3).to_broadcast(shape)
                         for q in range(2)]
                bar = [b_bar[:, q].unsqueeze(2).to_broadcast(shape) for q in range(2)]
                out = [b_pow[:, q].rearrange("p s (t c) -> p s t c", t=LIFT) for q in range(2)]
                complex_mult(out[0], out[1], power, bar, t1, t2, lambda ins: ins.then_inc(bpart_done, 1))

            def c_part(ct):
                dve.wait_ge(ct_done, ct + 1)
                dve.wait_ge(bpart_done, ct + 1)
                dve.wait_ge(pst, ct * 288)
                shape = [P, ST_CT, LIFT + 1, GROUP_CH]
                t1, t2 = (t[:].rearrange("p (s t c) -> p s t c", s=ST_CT, c=GROUP_CH) for t in (p_t1, p_t2))
                power = [lam_p[:, q, bass.ds(ct * ST_CT, ST_CT), :].unsqueeze(3).to_broadcast(shape) for q in range(2)]
                c = [c_t[:, q].unsqueeze(2).to_broadcast(shape) for q in range(2)]
                out = [c_pow[:, q].rearrange("p s (t c) -> p s t c", c=GROUP_CH) for q in range(2)]
                complex_mult(out[0], out[1], c, power, t1, t2, lambda ins: ins.then_inc(cpart_done, 1), negate_i=True)

            def ffn_up(ph):
                base = up_at[ph.name]
                if (ph.kind, ph.name) in READS:
                    reciprocal(READS[(ph.kind, ph.name)])

                def unit(i, j):
                    u = i * 2 + (base + j)
                    t = i * 2 + (ph.tile0 + j)
                    dve.wait_ge(full[0], t + 1)
                    scaled(t_a[:], 0).then_inc(free[0], 1)
                    dve.wait_ge(full[1], t + 1)
                    scaled(t_b[:], 1).then_inc(free[1], 1)
                    dve.wait_ge(g_ready, u)
                    dve.wait_ge(free[1], t + 1)
                    dve.wait_ge(silu_done, u + 1)
                    V.tensor_tensor(t_g[:], t_b[:], t_s[:], ALU.mult).then_inc(g_full, 1)
                    dve.wait_ge(g_hi_done, u + 1)
                    V.tensor_tensor(cols(g_lo, i * 2 + j), t_g[:], f32(cols(g_hi, i * 2 + j)), ALU.subtract)\
                        .then_inc(g_ready, 1)

                first = 0
                if ph is PH[0]:
                    unit(0, 0)
                    unit(0, 1)
                    make_masks()
                    unit(1, 0)
                    bounds()
                    unit(1, 1)
                    step_sizes()
                    unit(2, 0)
                    lambda_bar()
                    unit(2, 1)
                    b_factor()
                    unit(3, 0)
                    powers()
                    unit(3, 1)
                    first = 4
                with dve.Fori(first, ph.pairs) as i:
                    for j in range(2):
                        unit(i, j)

            def down(ph):
                r = MAKES.get((ph.kind, ph.name))
                pieces = ph.kind == "down" and ph.name[0] == "ffn1_0"
                if r is not None:
                    if ph.kind == "hgrn_out":
                        dve.wait_ge(o_ready, HEADS)
                    clear_ssq(r)
                scale = 1.0 if ph.kind == "hgrn_out" else 0.5

                def unit(i, j):
                    if pieces:
                        (b_part, c_part)[j](i + ph.name[1] * (NK // 2))
                    m = i * 2 + j
                    dve.wait_ge(full[j], i + (ph.tile0 + 1))
                    V.scalar_tensor_tensor(out=halves(cols(x, m)), in0=pair(j), scalar=scale, in1=halves(cols(x, m)),
                                           op0=ALU.mult, op1=ALU.add).then_inc(free[j], 1)
                    if r is not None:
                        norm_tile(r, m)

                link.settle()
                at, per = link.base, 6 + 2 + 5 + 5 if pieces else 0
                with dve.Fori(0, ph.pairs) as i:
                    link.base = i * per + at
                    for j in range(2):
                        unit(i, j)
                    assert link.n == per
                    link.n = 0
                link.base = at + ph.pairs * per

            def hgrn(ph):
                reciprocal(1)
                link(V.memset(score[:], 0.0))

                def level(m, b, n):
                    dve.wait_ge(sc_full, m * LEVELS + (n + 1))
                    q, k = q_t[b], k_t[b]
                    if n == 0:
                        V.tensor_tensor(q[:], q[:], f_t[:], ALU.mult).then_inc(qk_done, 1)
                    else:
                        if n == 3 and (not isinstance(m, int) or m):
                            dve.wait_ge(decay_done, m)
                        half = HALVINGS[n - 1]
                        span = T if half < DEC_SEQ else SEQ
                        blocks = span // (2 * half)
                        at = {1: None, 2: 0, 4: 288, 8: 432, 16: 504, 32: 536, 64: 552, 128: 560}
                        e = f_t[:, 0:span] if half == 1 else e_t[:, at[half]:at[half] + span // half]
                        e = e.rearrange("p (n h) -> p n h", h=2)
                        out = e_t[:, at[2 * half]:at[2 * half] + blocks]
                        qv = q[:, 0:span].rearrange("p (n h l) -> p n h l", h=2, l=half)
                        kv = k[:, 0:span].rearrange("p (n h l) -> p n h l", h=2, l=half)
                        shape = [P, blocks, half]
                        dve.wait_ge(qk_done, m * LEVELS + n)
                        V.tensor_tensor(qv[:, :, 1], qv[:, :, 1], e[:, :, 0:1].to_broadcast(shape), ALU.mult)
                        V.tensor_tensor(kv[:, :, 0], kv[:, :, 0], e[:, :, 1:2].to_broadcast(shape), ALU.mult)
                        V.tensor_tensor(out, e[:, :, 0], e[:, :, 1], ALU.mult).then_inc(qk_done, 1)
                    dve.wait_ge(begun, 1)
                    if n == 0 and (not isinstance(m, int) or m):
                        dve.wait_ge(o_full, m)
                    dve.wait_ge(sc_read, m * LEVELS + n)
                    shape = [P, CHUNKS, P]
                    ins = V.copy_predicated(score[:, 0:SEQ].rearrange("p (c q) -> p c q", q=P),
                                            masks[:, n, :].unsqueeze(1).to_broadcast(shape),
                                            ps[:, 4 + n % 2, :].rearrange("p (c q) -> p c q", q=P))
                    if n < SAMPLE_LEVELS:
                        ins = V.copy_predicated(score[0:SAMPLE, SEQ:T], masks_s[:, n, :], ps[0:SAMPLE, 6 + n % 2, 0:SAMPLE])
                    ins.then_inc(sc_read, 1)

                def take(dst, s, n, k):
                    dve.wait_ge(full[s], n * 2 + (ph.tile0 + k + 1))
                    scaled(dst, s).then_inc(free[s], 1)

                def gates(n, b):
                    dve.wait_ge(sig_done, n * 2 + 2)
                    link(V.tensor_scalar(f_t[:], f_t[:], lb_c[:, bass.ds(n, 1)], lb[:, bass.ds(n, 1)], ALU.mult, ALU.add))
                    V.tensor_scalar(f_t[:], f_t[:], GATE_FLOOR, None, ALU.max)
                    V.tensor_scalar(k_t[b][:], k_t[b][:], lb_c[:, bass.ds(n, 1)], None, ALU.mult).then_inc(gates_done, 1)

                def tail(m, b, turn):
                    kv = lambda c: ps[:, 4, c * P:(c + 1) * P]
                    dve.wait_ge(kvp_full, m + 1)
                    link(V.tensor_copy(s_chunk[:, 0, :], kv(0)))
                    for c in range(1, CHUNKS):
                        decay = e_t[:, 560 + c:561 + c]
                        out = s_chunk[:, c, :] if c < CHUNKS - 1 else s_end[b][:]
                        if c == CHUNKS - 1:
                            dve.wait_ge(s_st[b], turn * 32)
                        ins = V.scalar_tensor_tensor(out=out, in0=s_chunk[:, c - 1, :], scalar=decay, in1=kv(c),
                                                     op0=ALU.mult, op1=ALU.add)
                        if c < CHUNKS - 1:
                            link(ins)
                    ins.then_inc(chain_done, 1)
                    dve.wait_ge(kvs_full, m + 1)
                    dve.wait_ge(decay_done, m + 1)
                    sv = s_out[b][:].rearrange("p b v -> p (b v)").rearrange("p (h w) -> p h w", h=2)
                    V.tensor_tensor(sv, sv, ps[:, 6:8, :], ALU.add).then_inc(s_out_done, 1)
                    dve.wait_ge(silu_g, m + 1)
                    dve.wait_ge(o_ready, m)
                    dve.wait_ge(osq_done, m + 1)
                    gn = vec[:, COL["gnorm"]:COL["gnorm"] + 1]
                    V.scalar_tensor_tensor(out=ssq[:, 0:SEQ], in0=ps[:, 5, :], scalar=gn, in1=s_g[b][:, 0:SEQ],
                                           op0=ALU.mult, op1=ALU.mult)
                    V.scalar_tensor_tensor(out=ssq[:, SEQ:T], in0=ps[:, 4, 0:SAMPLE], scalar=gn,
                                           in1=s_g[b][:, SEQ:T], op0=ALU.mult, op1=ALU.mult).then_inc(on_done, 1)

                def invert(head, quarter):
                    if head is not None:
                        dve.wait_ge(osd_done, head + 1)
                        at = slice(quarter * T // 4, (quarter + 1) * T // 4)
                        V.reciprocal(o_rs[:, at], sq[:, at]).then_inc(inv_done, 1)

                def normalise(head):
                    if head is not None:
                        dve.wait_ge(on_done, head + 1)
                        dve.wait_ge(inv_done, head * 4 + 4)
                        V.tensor_tensor(ssq[:], ssq[:], o_rs[:], ALU.mult).then_inc(og_done, 1)

                def o_rest(head):
                    if head is not None:
                        dve.wait_ge(o_hi_done, head + 1)
                        V.tensor_tensor(cols(o_lo, head), ssq[:], f32(cols(o_hi, head)), ALU.subtract).then_inc(o_ready, 1)

                def step(n, b, m, turn, before):
                    links = int(n is not None) + (CHUNKS - 1 if m is not None else 0)
                    mb = 1 - b
                    if m is not None:
                        level(m, mb, 0)
                    if n is not None:
                        take(q_t[b][:], 0, n, 0)
                    if m is not None:
                        level(m, mb, 1)
                    invert(before, 0)
                    if m is not None:
                        level(m, mb, 2)
                    if n is not None:
                        if not isinstance(n, int) or n:
                            dve.wait_ge(silu_g, n)
                        take(pre[:], 1, n, 0)
                    invert(before, 1)
                    if m is not None:
                        level(m, mb, 3)
                    invert(before, 2)
                    if m is not None:
                        level(m, mb, 4)
                    if n is not None:
                        gates(n, b)
                    invert(before, 3)
                    if n is not None:
                        if not isinstance(n, int) or n:
                            dve.wait_ge(vt_full, n)
                        take(v_t[:], 0, n, 1)
                    if m is not None:
                        level(m, mb, 5)
                    normalise(before)
                    if m is not None:
                        level(m, mb, 6)
                    o_rest(before)
                    if m is not None:
                        level(m, mb, 7)
                    if n is not None:
                        take(pre[:], 1, n, 1)
                    if m is not None:
                        tail(m, mb, turn)
                    assert link.n == links, (link.n, links)

                link.settle()
                step(0, 0, None, None, None)
                link.settle()
                step(1, 1, 0, 0, None)
                link.settle()
                at = link.base
                one = 1 + CHUNKS - 1
                with dve.Fori(0, HEADS // 2 - 1) as i:
                    link.base = i * (2 * one) + at
                    step(i * 2 + 2, 0, i * 2 + 1, i, i * 2)
                    link.settle()
                    step(i * 2 + 3, 1, i * 2 + 2, i + 1, i * 2 + 1)
                    link.n = 0
                link.base = at + (HEADS // 2 - 1) * 2 * one
                step(None, 0, HEADS - 1, HEADS // 2 - 1, HEADS - 2)
                link.settle()
                step(None, 0, None, None, HEADS - 1)

            def s5(ph):
                reciprocal(4)
                for ct in range(NK):
                    V.scalar_tensor_tensor(out=u_t[:, ct].rearrange("p (t n) -> p t n", t=LIFT), in0=lifted(x[:, ct]),
                                           scalar=vec[:, NORMS[4][0] + ct:NORMS[4][0] + ct + 1], in1=lifted(rstd[:]),
                                           op0=ALU.mult, op1=ALU.mult).then_inc(u_done, 1)
                link.settle()
                dve.wait_ge(norm_full, 5)
                half_st = ST // 2

                def advance(out, before, adds, lam, done):
                    w = 2 * half_st * (SUPER if len(out.shape) == 4 else 1)
                    t1, t2 = (t[:, 0:w].rearrange("p (r s) -> p r s", r=2) for t in (sq, ssq))
                    if len(out.shape) == 4:
                        t1, t2 = (t.rearrange("p r (s b) -> p r s b", b=SUPER) for t in (t1, t2))
                    V.tensor_tensor(t1, before, lam[0], ALU.mult)
                    link(V.tensor_tensor(t2[:, ::-1], before, lam[1], ALU.mult))
                    link(V.tensor_tensor(t1, t1, adds, ALU.add))
                    done(V.tensor_tensor(out, t1, t2, ALU.add))

                def scan(half):
                    tiles = slice(half * half_st, (half + 1) * half_st)
                    dve.wait_ge(v_read, (half + 1) * NK // 2)
                    shape = [P, 2, half_st, SUPER]
                    by8 = [lam8[:, q, :, tiles].unsqueeze(3).to_broadcast(shape) for q in range(2)]
                    by64 = [lam64[:, q, :, tiles] for q in range(2)]
                    v = s5_v[:, :, tiles, 0:PROMPT_BLOCKS].rearrange("p r s (b j) -> p r s b j", j=STEPS)
                    s = s5_s[:, :, tiles, 0:PROMPT_BLOCKS].rearrange("p r s (b j) -> p r s b j", j=STEPS)
                    e, edge = s5_e[:, :, tiles], s5_b[:, :, tiles]
                    link(V.tensor_scalar(e, v[:, :, :, :, 0], 1.0, None, ALU.mult))
                    for j in range(1, STEPS):
                        advance(e, e, v[:, :, :, :, j], by8, link)
                    link(V.memset(edge[:, :, :, 0:1], 0.0))
                    for b in range(SUPER):
                        advance(edge[:, :, :, b + 1], edge[:, :, :, b], e[:, :, :, b], by64, link)
                    link(V.tensor_scalar(s[:, :, :, :, 0], edge[:, :, :, 0:SUPER], 1.0, None, ALU.mult))
                    for j in range(1, STEPS - 1):
                        advance(s[:, :, :, :, j], s[:, :, :, :, j - 1], v[:, :, :, :, j - 1], by8, link)
                    j = STEPS - 1
                    advance(s[:, :, :, :, j], s[:, :, :, :, j - 1], v[:, :, :, :, j - 1], by8,
                            lambda ins: ins.then_inc(scan_done, 1))
                    dve.wait_ge(scan_done, half + 1)

                scan(0)
                scan(1)
                t1, t2 = (t[:, 0:2 * ST * DEC_BATCH].rearrange("p (r b s) -> p r b s", r=2, s=ST) for t in (sq, ssq))
                before = s5_s[:, :, :, PROMPT_BLOCKS:].rearrange("p r s b -> p r b s")
                adds = s5_v[:, :, :, PROMPT_BLOCKS:].rearrange("p r s b -> p r b s")
                shape = [P, 2, DEC_BATCH, ST]
                dve.wait_ge(sin_done, 1)
                link(V.tensor_tensor(t1, before, lam8[:, 0].unsqueeze(2).to_broadcast(shape), ALU.mult))
                link(V.tensor_tensor(t2[:, ::-1], before, lam8[:, 1].unsqueeze(2).to_broadcast(shape), ALU.mult))
                link(V.tensor_tensor(t1, t1, adds, ALU.add))
                V.tensor_tensor(s5_fs[:], t1, t2, ALU.add).then_inc(fs_done, 1)

                def z_rest(ct):
                    dve.wait_ge(z_hi_done, ct + 1)
                    V.tensor_tensor(lifted(z_lo[:, ct]), z_t[ct % 2][:].rearrange("p (t n) -> p t n", t=LIFT),
                                    f32(lifted(z_hi[:, ct])), ALU.subtract).then_inc(z_ready, 1)

                for ct in range(NK):
                    dve.wait_ge(t3_full, ct + 1)
                    if ct >= 2:
                        dve.wait_ge(gelu_done, ct - 1)
                    V.scalar_tensor_tensor(out=halves(y_f[ct % 2][:]), in0=halves(u_t[:, ct]),
                                           scalar=vec[:, COL["s5_d"] + ct:COL["s5_d"] + ct + 1],
                                           in1=pair(1), op0=ALU.mult, op1=ALU.add).then_inc(yy_done, 1)
                    if ct:
                        z_rest(ct - 1)
                z_rest(NK - 1)
                link.settle()
                dve.wait_ge(fs_done, 1)
                clear_ssq(5)

                def unit(i, j):
                    t = i * 2 + (ph.tile0 + j)
                    m = i * 2 + j
                    dve.wait_ge(full[0], t + 1)
                    dve.wait_ge(free[1], t + 1)
                    V.tensor_tensor(halves(t_a[:]), pair(0), halves(t_s[:]), ALU.mult).then_inc(free[0], 1)
                    dve.wait_ge(free[0], t + 1)
                    V.tensor_tensor(cols(x, m), cols(x, m), t_a[:], ALU.add).then_inc(gs_done, 1)
                    norm_tile(5, m)

                with dve.Fori(0, ph.pairs) as i:
                    for j in range(2):
                        unit(i, j)

            for ph in PH:
                {"up": ffn_up, "down": down, "hgrn_in": hgrn, "hgrn_out": down, "glu": s5}[ph.kind](ph)
            reciprocal(6)
            for k in range(NK):
                V.scalar_tensor_tensor(out=y_n[:, k], in0=x[:, k], scalar=vec[:, COL["ln_final"] + k:COL["ln_final"] + k + 1],
                                       in1=rstd[:], op0=ALU.mult, op1=ALU.mult).then_inc(yn_done, 1)
            for c in range(0, CHUNKS + 1, 2):
                n = P if c < CHUNKS else SAMPLE
                dve.wait_ge(full[0], TILE_END + c // 2 + 1)
                V.tensor_copy(y_rows[0:n, c, :].rearrange("p (h d) -> p h d", h=2), ps[0:n, 0:2, :]).then_inc(free[0], 1)

        @block.tensor
        def _(pe):
            M = nc.tensor

            def turn(out, t, n=P, w=P):
                return M.transpose(out, t, ident[0:n, 0:n])

            def sum_tokens(r):
                pe.wait_ge(ssq_done, NK * (r + 1))
                pe.wait_ge(consts, 3)
                if r:
                    pe.wait_ge(sd_done, r)
                if r == 2:
                    pe.wait_ge(og_done, HEADS)
                if r == 5:
                    pe.wait_ge(y_read, NK)
                for h in range(2):
                    ins = M.matmul(ps[:, 4 + h, 0:HALF], ones[:], ssq[:, h * HALF:(h + 1) * HALF], start=True, stop=True)
                ins.then_inc(norm_full, 1)

            def product(ph, j, a, i, hi, lo, before=None, part=None):
                k0, k1 = part or (0, ph.kt)
                s, t = (a, i * 2 + (ph.tile0 + j)) if ph.cols == 2 else (j, i + ph.tile0)
                if k0 == 0:
                    if a == 0:
                        pe.wait_ge(w_ready[j], i + (ph.pair0 + 1))
                    pe.wait_ge(free[s], t)
                for k in range(k0, k1):
                    if before is not None:
                        before(k)
                    at = (a * ph.kt + k) * P
                    for n, (w, v) in enumerate(((w_hi, hi), (w_hi, lo), (w_lo, hi))):
                        for h in range(2):
                            ins = M.matmul(ps[:, 2 * s + h, 0:HALF], w[j][:, at:at + P], v[:, k, h * HALF:(h + 1) * HALF],
                                           start=k == 0 and n == 0, stop=k == ph.kt - 1 and n == 2)
                if k1 == ph.kt:
                    ins.then_inc(full[s], 1)

            pe.wait_ge(consts, 3)
            pe.wait_ge(vec_in, 7 * 16)
            turn(ps[:, 6, 0:NVEC], vec_rows[0:NVEC, :], NVEC).then_inc(vec_full, 1)
            pe.wait_ge(x_in, 32)
            for m in range(NK):
                s = m % 2
                if m >= 2:
                    pe.wait_ge(free[s], m // 2)
                for c in range(CHUNKS):
                    turn(ps[:, 2 * s, c * P:(c + 1) * P], x_rows[:, c, m * P:(m + 1) * P])
                turn(ps[:, 2 * s + 1, 0:SAMPLE], x_rows[0:SAMPLE, CHUNKS, m * P:(m + 1) * P], SAMPLE).then_inc(full[s], 1)
            pe.wait_ge(lam_ld, 48)
            pe.wait_ge(dt_done, 1)
            turn(ps[:, 7, 0:3 * ST], lam_in[0:3 * ST, :], 3 * ST).then_inc(vec_full, 1)

            def reads_norm(ph):
                r = READS[(ph.kind, ph.name)]
                fill = NORMS[r][1]

                def before(k):
                    pe.wait_ge(h_ready, fill * NK + k + 1)
                    if k == NK - 1:
                        sum_tokens(r)
                return before

            def ffn_up(ph):
                first = reads_norm(ph) if (ph.kind, ph.name) in READS else None
                for j in range(2):
                    for a in range(2):
                        product(ph, j, a, 0, h_hi, h_lo, first if (j, a) == (0, 0) else None)
                with pe.Fori(1, ph.pairs) as i:
                    for j in range(2):
                        for a in range(2):
                            product(ph, j, a, i, h_hi, h_lo)

            def c_turned(ct):
                pe.wait_ge(pin, ct * 96 + 96)
                pe.wait_ge(ct_done, ct)
                for r in range(2):
                    ins = turn(ps[:, 7, r * P:(r + 1) * P], c_in[:, r].rearrange("p d q -> p (d q)"))
                ins.then_inc(ct_full, 1)

            def b_turned(ct):
                pe.wait_ge(bpart_done, ct + 1)
                pe.wait_ge(wbst_done, ct)
                for r in range(2):
                    for st in range(ST_CT):
                        ins = turn(ps[:, 4 + r, st * P:(st + 1) * P], b_pow[:, r, st])
                ins.then_inc(bl_full, 1)

            def taps(ct):
                pe.wait_ge(cpart_done, ct + 1)
                pe.wait_ge(kz_done, ct)
                for st in range(ST_CT):
                    for r in range(2):
                        ins = M.matmul(ps[0:2 * GROUP_CH, 6, st * P:(st + 1) * P], b_blk[:, r, st], c_pow[:, r, st, 0:P],
                                       start=r == 0, stop=r == 1)
                ins.then_inc(tap_full, 1)

            def down(ph):
                pieces = ph.name[0] == "ffn1_0"
                made = up_at.get(ph.name, 0)

                def before(k):
                    if ph.kind == "hgrn_out":
                        pe.wait_ge(o_ready, k + 1)
                    elif k == 0:
                        pe.wait_ge(g_ready, made + ph.kt - 1)
                    elif k == ph.kt - 1:
                        pe.wait_ge(g_ready, made + ph.kt)

                hi, lo = (o_hi, o_lo) if ph.kind == "hgrn_out" else (g_hi, g_lo)
                ct0 = ph.name[1] * (NK // 2)

                def pair_of(i, first=None):
                    if first is None:
                        product(ph, 0, 0, i, hi, lo)
                    else:
                        product(ph, 0, 0, i, hi, lo, first, (0, ph.kt - 1))
                        product(ph, 1, 0, i, hi, lo, None, (0, ph.kt - 1))
                        product(ph, 0, 0, i, hi, lo, first, (ph.kt - 1, ph.kt))
                    if pieces:
                        c_turned(i + ct0)
                        b_turned(i + ct0)
                    product(ph, 1, 0, i, hi, lo, None, None if first is None else (ph.kt - 1, ph.kt))
                    if pieces:
                        taps(i + ct0)

                if pieces:
                    pe.wait_ge(sd_done, 1)
                pair_of(0, before)
                with pe.Fori(1, ph.pairs) as i:
                    pair_of(i)

            def hgrn(ph):
                def level(m, b, n):
                    if n == 0:
                        if not isinstance(m, int) or m:
                            pe.wait_ge(on_done, m)
                            pe.wait_ge(osd_done, m)
                        pe.wait_ge(gates_done, m + 1)
                    else:
                        pe.wait_ge(qk_done, m * LEVELS + n)
                    if n >= 2:
                        pe.wait_ge(sc_read, m * LEVELS + (n - 1))
                    for c in range(CHUNKS):
                        at = slice(c * P, (c + 1) * P)
                        ins = M.matmul(ps[:, 4 + n % 2, at], k_t[b][:, at], q_t[b][:, at], start=True, stop=True)
                    if n < SAMPLE_LEVELS:
                        ins = M.matmul(ps[0:SAMPLE, 6 + n % 2, 0:SAMPLE], k_t[b][:, SEQ:T], q_t[b][:, SEQ:T],
                                       start=True, stop=True)
                    ins.then_inc(sc_full, 1)

                def turned(t, done):
                    for c in range(CHUNKS):
                        turn(ps[:, 6, c * P:(c + 1) * P], t[:, c * P:(c + 1) * P])
                    turn(ps[0:SAMPLE, 7, 0:P], t[:, SEQ:T]).then_inc(done, 1)

                def v_turned(m):
                    pe.wait_ge(free[0], m * 2 + (ph.tile0 + 2))
                    pe.wait_ge(sc_read, m * LEVELS + SAMPLE_LEVELS)
                    turned(v_t, vt_full)

                def tail(m, b):
                    pe.wait_ge(qk_done, m * LEVELS + LEVELS)
                    pe.wait_ge(vtok_done, m + 1)
                    turned(k_t[b], kt_full)
                    pe.wait_ge(ktok_done, m + 1)
                    pe.wait_ge(sc_read, m * LEVELS + (LEVELS - 1))
                    for c in range(CHUNKS):
                        ins = M.matmul(ps[:, 4, c * P:(c + 1) * P], k_tok[:, c, :], v_tok[:, c, :], start=True, stop=True)
                    ins.then_inc(kvp_full, 1)
                    pe.wait_ge(vseq_done, m + 1)
                    for h in range(2):
                        v = v_seq[:, 4 * h:4 * h + 4, :].rearrange("p b v -> p (b v)")
                        ins = M.matmul(ps[:, 6 + h, :], k_tok[0:SAMPLE, CHUNKS, :], v, start=True, stop=True)
                    ins.then_inc(kvs_full, 1)
                    pe.wait_ge(sc_read, m * LEVELS + LEVELS)
                    pe.wait_ge(chain_done, m + 1)
                    for c in range(CHUNKS):
                        at = slice(c * P, (c + 1) * P)
                        M.matmul(ps[:, 5, at], v_tok[:, c, :], score[:, at], start=True, stop=c == 0)
                        if c:
                            M.matmul(ps[:, 5, at], s_chunk[:, c - 1, :], q_t[b][:, at], start=False, stop=True)
                    pe.wait_ge(decay_done, m + 1)
                    M.matmul(ps[:, 4, 0:SAMPLE], v_tok[0:SAMPLE, CHUNKS, :], score[0:SAMPLE, SEQ:T], start=True, stop=False)
                    for n in range(DEC_BATCH):
                        at = SEQ + n * DEC_SEQ
                        ins = M.matmul(ps[:, 4, n * DEC_SEQ:(n + 1) * DEC_SEQ], s_in[b][:, n, :],
                                       q_t[b][:, at:at + DEC_SEQ], start=False, stop=n == DEC_BATCH - 1)
                    ins.then_inc(o_full, 1)
                    pe.wait_ge(osq_done, m + 1)
                    pe.wait_ge(s_out_done, m + 1)
                    for h in range(2):
                        ins = M.matmul(ps[:, 6 + h, 0:HALF], ones[:], sq[:, h * HALF:(h + 1) * HALF], start=True, stop=True)
                    ins.then_inc(r_full, 1)

                def step(n, b, m):
                    first = reads_norm(ph) if isinstance(n, int) and n == 0 else None
                    parts = [(0, 0, 0, 4), (0, 0, 4, 8), (0, 1, 0, 4), (0, 1, 4, 8), (1, 0, 0, 4), (1, 0, 4, 8),
                             (1, 1, 0, 3), (1, 1, 3, 6), (1, 1, 6, 8)]
                    for at, (j, a, k0, k1) in enumerate(parts):
                        if n is not None:
                            product(ph, j, a, n, h_hi, h_lo, first if (j, a) == (0, 0) else None, (k0, k1))
                        if m is not None and at < LEVELS:
                            level(m, 1 - b, at)
                            if at == SAMPLE_LEVELS:
                                v_turned(m)
                    if m is not None:
                        tail(m, 1 - b)

                pe.wait_ge(wbst_done, NK)
                pe.wait_ge(kz_done, NK)
                step(0, 0, None)
                with pe.Fori(0, HEADS // 2 - 1) as i:
                    step(i * 2 + 1, 1, i * 2)
                    step(i * 2 + 2, 0, i * 2 + 1)
                step(HEADS - 1, 1, HEADS - 2)
                step(None, 0, HEADS - 1)

            def s5(ph):
                sum_tokens(4)
                pe.wait_ge(rows_ld, 32)
                for q in range(2):
                    for h in range(2):
                        at = (2 * q + h) * P
                        ins = turn(ps[:, 6, at:at + P], st_rows[:, q, h])
                ins.then_inc(sin_full, 1)
                pe.wait_ge(sd_done, 5)

                def blocks_first(ct):
                    pe.wait_ge(u_done, ct + 1)
                    if ct:
                        pe.wait_ge(t1_read, ct)
                    for t in range(LIFT):
                        ins = turn(ps[0:BLOCKS, t // 4, (t % 4) * P:(t % 4 + 1) * P], u_t[:, ct, t * BLOCKS:(t + 1) * BLOCKS])
                    ins.then_inc(t1_full, 1)

                def places_first(ct):
                    pe.wait_ge(t1_read, ct + 1)
                    if ct:
                        pe.wait_ge(t2_read, ct)
                    for g in range(G_CT):
                        ins = turn(ps[:, 2 + g // 4, (g % 4) * BLOCKS:(g % 4 + 1) * BLOCKS],
                                   turned[ct % 2][:, g * P:(g + 1) * P], BLOCKS)
                    ins.then_inc(t2_full, 1)

                def block_adds(ct):
                    pe.wait_ge(t2_read, ct + 1)
                    pe.wait_ge(wb_ld[ct % 2], 16 * (ct // 2 + 1))
                    if ct == 1:
                        pe.wait_ge(sin_done, 1)
                    if ct >= 2:
                        pe.wait_ge(v_read, ct - 1)
                    for r in range(2):
                        for g in range(2):
                            for st in range(ST_CT):
                                ins = M.matmul(
                                    ps[STATE * g:STATE * (g + 1), 4 + 2 * (ct % 2) + r, st * BLOCKS:(st + 1) * BLOCKS],
                                    wb[ct % 2][:, r, st, STATE * g:STATE * (g + 1)], u_lift[:, G_CT * ct + 2 * st + g, :],
                                    start=True, stop=True)
                    ins.then_inc(v_full, 1)

                for at in range(NK + 2):
                    if at < NK:
                        blocks_first(at)
                    if at >= 2:
                        block_adds(at - 2)
                    if 1 <= at <= NK:
                        places_first(at - 1)

                def outputs(ct):
                    pe.wait_ge(wy_ld[ct % 2], 32 * (ct // 2 + 1))
                    if ct < 2:
                        pe.wait_ge(v_read, NK)
                    else:
                        pe.wait_ge(y_read, ct - 1)
                    for g in range(G_CT):
                        st, g2 = g // 2, g % 2
                        rows = slice(STATE * g2, STATE * (g2 + 1))
                        out = ps[0:BLOCKS, 4 + 2 * (ct % 2) + g2, st * P:(st + 1) * P]
                        M.matmul(out, u_lift[:, G_CT * ct + g, :], wi[ct % 2][:, g], start=True, stop=False)
                        M.matmul(out, s5_s[rows, 0, ST_CT * ct + st, :], wc[ct % 2][rows, 0, st], start=False, stop=False)
                        ins = M.matmul(out, s5_s[rows, 1, ST_CT * ct + st, :], wc[ct % 2][rows, 1, st], start=False, stop=True)
                    ins.then_inc(y_full, 1)

                def channels_first(ct):
                    pe.wait_ge(y_read, ct + 1)
                    if ct:
                        pe.wait_ge(yy_done, ct)
                    for t in range(LIFT):
                        ins = turn(ps[:, 2 + t // 4, (t % 4) * BLOCKS:(t % 4 + 1) * BLOCKS],
                                   turned[ct % 4][:, t * P:(t + 1) * P], BLOCKS)
                    ins.then_inc(t3_full, 1)

                def last_states():
                    pe.wait_ge(t1_read, NK)
                    pe.wait_ge(scan_done, 2)
                    for q in range(2):
                        ins = turn(ps[0:ST, 0, q * P:(q + 1) * P], s5_b[:, q, :, SUPER])
                    ins.then_inc(f_full, 1)
                    pe.wait_ge(fs_done, 1)
                    for q in range(2):
                        for h in range(2):
                            at = (2 * q + h) * P
                            ins = turn(ps[:, 1, at:at + P], s5_fs[:, q, 4 * h:4 * h + 4].rearrange("p b s -> p (b s)"))
                    ins.then_inc(f_full, 1)

                def glu_part(k0, k1):
                    if k0 == 0:
                        pe.wait_ge(f_done, 2)
                    product(ph, 0, 0, 0, z_hi, z_lo, lambda k: pe.wait_ge(z_ready, k + 1), (k0, k1))

                pe.wait_ge(sin_done, 1)
                pe.wait_ge(scan_done, 1)
                for ct in range(4):
                    outputs(ct)
                pe.wait_ge(scan_done, 2)
                outputs(4)
                channels_first(0)
                last_states()
                channels_first(1)
                outputs(5)
                channels_first(2)
                glu_part(0, 1)
                channels_first(3)
                glu_part(1, 2)
                outputs(6)
                channels_first(4)
                glu_part(2, 3)
                channels_first(5)
                glu_part(3, 4)
                outputs(7)
                channels_first(6)
                glu_part(4, 6)
                channels_first(7)
                glu_part(6, 8)
                pe.wait_ge(yy_done, NK)
                product(ph, 0, 1, 0, z_hi, z_lo)
                for a in range(2):
                    product(ph, 1, a, 0, z_hi, z_lo)
                with pe.Fori(1, ph.pairs) as i:
                    for j in range(2):
                        for a in range(2):
                            product(ph, j, a, i, z_hi, z_lo)

            for ph in PH:
                {"up": ffn_up, "down": down, "hgrn_in": hgrn, "hgrn_out": down, "glu": s5}[ph.kind](ph)

            sum_tokens(6)
            pe.wait_ge(yn_done, NK)
            for c in range(CHUNKS + 1):
                s, n = c % 2, P if c < CHUNKS else SAMPLE
                pe.wait_ge(free[s], TILE_END + c // 2)
                for k in range(NK):
                    ins = turn(ps[0:n, 2 * s + k // 4, (k % 4) * P:(k % 4 + 1) * P], y_n[:, k, c * P:c * P + n])
                ins.then_inc(full[s], 1)


_INS = ["x_prompt", "x_sample", "state_hgrn", "state_s5_re", "state_s5_im", "ln_ffn1", "ffn1_w_in", "ffn1_w_out",
        "ln_mix", "ln_ffn2", "ffn2_w_in", "ffn2_w_out", "hgrn_lb_logits", "hgrn_w_in", "hgrn_gnorm", "hgrn_w_out",
        "s5_a_re", "s5_a_im", "s5_log_dt", "s5_b_re", "s5_b_im", "s5_c_re", "s5_c_im", "s5_d", "s5_w_glu", "ln_final"]
_OUTS = [(1, SEQ, D_MODEL), (DEC_BATCH, DEC_SEQ, D_MODEL), (1, 1, HEADS, P, P), (1, 1, GROUPS, STATE),
         (1, 1, GROUPS, STATE), (1, DEC_BATCH, HEADS, P, P), (1, DEC_BATCH, GROUPS, STATE),
         (1, DEC_BATCH, GROUPS, STATE)]


def kernel(**inputs):
    import numpy as _np
    import concourse.bacc as _bacc
    from concourse import mybir as _mybir
    from concourse.bass_utils import run_bass_kernel_spmd as _run

    nc = _bacc.Bacc("TRN2", target_bir_lowering=False, num_devices=1)
    arrays, args = {}, []
    for name in _INS:
        a = _np.ascontiguousarray(inputs[name])
        arrays[f"in_{name}_dram"] = a
        args.append(nc.dram_tensor(f"in_{name}_dram", a.shape, _mybir.dt.from_np(a.dtype), kind="ExternalInput").ap())
    for i, shape in enumerate(_OUTS):
        args.append(nc.dram_tensor(f"out_{i}_dram", shape, F32, kind="ExternalOutput").ap())
    build_trunk(nc, *args)
    r = _run(nc, [arrays], core_ids=[0])
    return tuple(r.results[0][f"out_{i}_dram"] for i in range(len(_OUTS)))
```

```python
from contextlib import ExitStack

import concourse.bass as bass
from concourse import mybir

F32 = mybir.dt.float32
F32R = mybir.dt.float32r
I32 = mybir.dt.int32
U8 = mybir.dt.uint8
ALU = mybir.AluOpType
ACT = mybir.ActivationFunctionType

D_MODEL = 1024
SEQ = 512
DEC_BATCH = 8
DEC_SEQ = 8
D_FF = 2816
HEADS = 8
GROUPS = 64
GROUP_CH = 16
STATE = 64
EPS = 1e-6
GATE_FLOOR = 1e-30

P = 128
SAMPLE = DEC_BATCH * DEC_SEQ
T = SEQ + SAMPLE
HALF = T // 2
BANK = 512
NK = D_MODEL // P
CHUNKS = SEQ // P
F_GROUPS = (12, 10)
HALVINGS = (1, 2, 4, 8, 16, 32, 64)
LEVELS = 1 + len(HALVINGS)
SAMPLE_LEVELS = 4
LIFT = 8
BLOCKS = T // LIFT
PROMPT_BLOCKS = SEQ // LIFT
ST = GROUPS // 2
SUPER = 8
STEPS = PROMPT_BLOCKS // SUPER
ST_CT = ST // NK
G_CT = GROUPS // NK
UNIT = NK * 2 * P

VECS = ["ln_ffn1", "ln_mix", "ln_ffn2", "ln_final", "hgrn_lb_logits", "s5_d", "hgrn_gnorm"]


class Phase:

    def __init__(self, kind, name, pairs, kt, cols, at):
        self.kind, self.name, self.pairs, self.kt, self.cols = kind, name, pairs, kt, cols
        self.size = kt * cols * P
        self.pair0, self.tile0 = at["pair"], at["tile"]
        at["pair"] += pairs
        at["tile"] += pairs * cols

    def last_use(self, j):
        end = self.tile0 + self.pairs * self.cols
        return (int(self.kind != "glu"), end - 1 + j) if self.cols == 2 else (j, end)


def phases():
    at = {"pair": 0, "tile": 0}
    out = []

    def ffn(name):
        for g, n in enumerate(F_GROUPS):
            out.append(Phase("up", (name, g), n // 2, NK, 2, at))
            out.append(Phase("down", (name, g), NK // 2, n, 1, at))

    ffn("ffn1_0")
    out.append(Phase("hgrn_in", ("hgrn", 0), HEADS, NK, 2, at))
    out.append(Phase("hgrn_out", ("hgrn", 0), NK // 2, NK, 1, at))
    ffn("ffn2_0")
    ffn("ffn1_1")
    out.append(Phase("glu", ("s5", 0), NK // 2, NK, 2, at))
    ffn("ffn2_1")
    return out


class Chain:

    def __init__(self, eng, sem):
        self.eng, self.sem, self.base, self.n = eng, sem, 0, 0

    def __call__(self, ins):
        self.n += 1
        ins.then_inc(self.sem, 1)
        self.eng.wait_ge(self.sem, self.base + self.n)

    def begin(self, ins):
        self.n += 1
        ins.then_inc(self.sem, 1)
        return self.base + self.n

    def settle(self):
        done, self.base, self.n = self.n, self.base + self.n, 0
        return done


def build_trunk(nc, x_prompt, x_sample, state_hgrn, state_s5_re, state_s5_im, ln_ffn1, ffn1_w_in, ffn1_w_out,
                ln_mix, ln_ffn2, ffn2_w_in, ffn2_w_out, hgrn_lb_logits, hgrn_w_in, hgrn_gnorm, hgrn_w_out,
                s5_a_re, s5_a_im, s5_log_dt, s5_b_re, s5_b_im, s5_c_re, s5_c_im, s5_d, s5_w_glu, ln_final,
                y_prompt, y_sample, hgrn_p, re_p, im_p, hgrn_s, re_s, im_s):
    PH = phases()

    place = {"at": nc.sbuf_base + (-nc.sbuf_base) % 64}
    limit = nc.sbuf_usable_end

    def sb(name, shape, dt=F32, at=None):
        size = 1 if dt == U8 else 4
        for n in shape[1:]:
            size *= n
        size += -size % 32
        where = place["at"] if at is None else at
        if at is None:
            place["at"] += size
        assert where + size <= limit, (name, where + size, limit)
        return nc.alloc_sbuf_tensor_at(name, shape, dt, offset=where)

    x = sb("x", [P, NK, T])
    h_at = place["at"]
    h_hi = sb("h_hi", [P, NK, T], F32R)
    h_lo = sb("h_lo", [P, NK, T], F32R)
    w_raw = [sb(f"w_raw{j}", [P, UNIT]) for j in range(2)]
    w_hi = [sb(f"w_hi{j}", [P, UNIT], F32R) for j in range(2)]
    w_lo = [sb(f"w_lo{j}", [P, UNIT], F32R) for j in range(2)]
    rstd = sb("rstd", [P, T])
    ssq = sb("ssq", [P, T])
    sq = sb("sq", [P, T])
    ident = sb("ident", [P, P])
    ones = sb("ones", [P, P])
    eps_t = sb("eps_t", [P, 1])
    vec = sb("vec", [P, P])
    lb = sb("lb", [P, NK])
    lb_c = sb("lb_c", [P, NK])
    lb_t = sb("lb_t", [P, 4, NK])
    lam8 = sb("lam8", [P, 2, 2, ST])
    lam64 = sb("lam64", [P, 2, 2, ST])
    own_seq = sb("own_seq", [SAMPLE, DEC_BATCH])
    masks = sb("masks", [P, LEVELS, P], U8)
    masks_s = sb("masks_s", [SAMPLE, SAMPLE_LEVELS, SAMPLE], U8)
    overlay = place["at"]

    g_at = place["at"]
    g_hi = sb("g_hi", [P, F_GROUPS[0], T], F32R)
    g_lo = sb("g_lo", [P, F_GROUPS[0], T], F32R)
    t_a = sb("t_a", [P, T])
    t_b = sb("t_b", [P, T])
    t_s = sb("t_s", [P, T])
    t_g = sb("t_g", [P, T])
    dt_in = sb("dt_in", [P, 2])
    lam_c = sb("lam_c", [P, 3, ST])
    lam_sc = sb("lam_sc", [P, 24, ST])
    lam_p = sb("lam_p", [P, 2, ST, LIFT + 1])
    lam_r = sb("lam_r", [P, 2, ST, LIFT])
    b_in = sb("b_in", [P, 2, ST_CT, GROUP_CH])
    b_bar = sb("b_bar", [P, 2, ST_CT, GROUP_CH])
    b_blk = sb("b_blk", [P, 2, ST_CT, 2 * GROUP_CH])
    c_in = sb("c_in", [P, 2, 2, STATE])
    c_t = sb("c_t", [P, 2, ST_CT, GROUP_CH])
    start_at = place["at"]
    b_pow = sb("b_pow", [P, 2, ST_CT, LIFT * GROUP_CH])
    c_pow = sb("c_pow", [P, 2, ST_CT, (LIFT + 1) * GROUP_CH])
    p_t1 = sb("p_t1", [P, ST_CT * (LIFT + 1) * GROUP_CH])
    p_t2 = sb("p_t2", [P, ST_CT * (LIFT + 1) * GROUP_CH])
    mask_at = place["at"]
    wb_st = sb("wb_st", [P, 2, ST_CT, P])
    kz = sb("kz", [2 * GROUP_CH, ST_CT, (2 * LIFT - 1) * GROUP_CH])
    assert place["at"] <= limit

    x_rows = sb("x_rows", [P, CHUNKS + 1, D_MODEL], at=g_at)

    place["at"] = overlay
    o_hi = sb("o_hi", [P, NK, T], F32R)
    o_lo = sb("o_lo", [P, NK, T], F32R)
    q_t = [sb(f"q_t{b}", [P, T]) for b in range(2)]
    k_t = [sb(f"k_t{b}", [P, T]) for b in range(2)]
    s_g = [sb(f"s_g{b}", [P, T]) for b in range(2)]
    f_t = sb("f_t", [P, T])
    v_t = sb("v_t", [P, T])
    pre = sb("pre", [P, T])
    e_t = sb("e_t", [P, 608])
    score = sb("score", [P, T])
    v_tok = sb("v_tok", [P, CHUNKS + 1, P])
    k_tok = sb("k_tok", [P, CHUNKS + 1, P])
    v_seq = sb("v_seq", [SAMPLE, DEC_BATCH, P])
    s_chunk = sb("s_chunk", [P, CHUNKS - 1, P])
    s_end = [sb(f"s_end{b}", [P, P]) for b in range(2)]
    s_in = [sb(f"s_in{b}", [P, DEC_BATCH, P]) for b in range(2)]
    s_out = [sb(f"s_out{b}", [P, DEC_BATCH, P]) for b in range(2)]
    o_rs = sb("o_rs", [P, T])
    assert place["at"] <= limit

    place["at"] = overlay
    u_at = place["at"]
    u_t = sb("u_t", [P, NK, T])
    lift_at = place["at"]
    u_lift = sb("u_lift", [P, GROUPS, BLOCKS])
    z_hi = sb("z_hi", [P, NK, T], F32R, at=u_at)
    z_lo = sb("z_lo", [P, NK, T], F32R, at=lift_at)
    turned = [sb(f"turned{b}", [BLOCKS, G_CT * P]) for b in range(4)]
    wb = [sb(f"wb{b}", [P, 2, ST_CT, P]) for b in range(2)]
    wc = [sb(f"wc{b}", [P, G_CT, P]) for b in range(2)]
    wi = [sb(f"wi{b}", [P, G_CT, P]) for b in range(2)]
    y_f = [sb(f"y_f{b}", [P, T]) for b in range(2)]
    z_t = [sb(f"z_t{b}", [P, T]) for b in range(2)]
    st_rows = sb("st_rows", [P, 2, 2, P])
    e_at = place["at"]
    s5_e = sb("s5_e", [P, 2, ST, SUPER])
    s5_b = sb("s5_b", [P, 2, ST, SUPER + 1])
    s5_fs = sb("s5_fs", [P, 2, DEC_BATCH, ST])
    fp_rows = sb("fp_rows", [ST, 2, P])
    fs_rows = sb("fs_rows", [P, 2, 2, P], at=e_at)
    assert place["at"] <= limit
    s5_v = sb("s5_v", [P, 2, ST, BLOCKS], at=h_at)
    s5_s = sb("s5_s", [P, 2, ST, BLOCKS], at=h_at + 4 * NK * T)

    def stacked(ct):
        half, c = divmod(ct, NK // 2)
        at = half * ST // 2 + (c % 2) * G_CT
        return s5_v[:, c // 2, at:at + G_CT, :].rearrange("p (s g) n -> p s g n", g=2)

    y_n = sb("y_n", [P, NK, T], at=h_at)
    y_rs = sb("y_rs", [P, 8], at=h_at + 4 * NK * T)
    y_rows = sb("y_rows", [P, CHUNKS + 1, D_MODEL], at=g_at)

    vec_rows = sb("vec_rows", [P, P], at=start_at)
    lam_in = sb("lam_in", [P, P], at=start_at + 4 * P)
    m_i = [sb(f"m_i{n}", [P, P], I32, at=mask_at + 4 * P * n) for n in range(4)]
    m_f = [sb(f"m_f{n}", [P, P], F32, at=mask_at + 4 * P * (4 + n)) for n in range(4)]
    ps = nc.alloc_psum_tensor("ps", [P, 8, BANK], F32)

    wb_d = nc.dram_tensor("wb_d", (NK, P, 2, ST_CT, P), F32).ap()
    wc_d = nc.dram_tensor("wc_d", (NK, P, 2, ST_CT, P), F32).ap()
    kz_d = nc.dram_tensor("kz_d", (NK, 2, GROUP_CH, ST_CT, (2 * LIFT - 1) * GROUP_CH), F32).ap()
    wi_d = nc.dram_tensor("wi_d", (NK, P, G_CT, P), F32).ap()

    ctx = ExitStack()

    def sem(name):
        return ctx.enter_context(nc.semaphore(name))

    with ctx:
        begun = sem("begun")
        x_in = sem("x_in")
        vec_in = sem("vec_in")
        lam_ld = sem("lam_ld")
        consts = sem("consts")
        vec_full = sem("vec_full")
        vec_done = sem("vec_done")
        dt_done = sem("dt_done")
        w_dma = [sem(f"w_dma{j}") for j in range(2)]
        w_hi_done = [sem(f"w_hi_done{j}") for j in range(2)]
        w_ready = [sem(f"w_ready{j}") for j in range(2)]
        full = [sem(f"full{s}") for s in range(2)]
        free = [sem(f"free{s}") for s in range(2)]
        x_full = sem("x_full")
        x_read = sem("x_read")
        dve_link = sem("dve_link")
        ssq_zero = sem("ssq_zero")
        sq_done = sem("sq_done")
        ssq_done = sem("ssq_done")
        norm_full = sem("norm_full")
        sd_done = sem("sd_done")
        rstd_done = sem("rstd_done")
        h_hi_done = sem("h_hi_done")
        h_ready = sem("h_ready")
        silu_done = sem("silu_done")
        g_full = sem("g_full")
        g_hi_done = sem("g_hi_done")
        g_ready = sem("g_ready")
        pin = sem("pin")
        ct_full = sem("ct_full")
        ct_done = sem("ct_done")
        bpart_done = sem("bpart_done")
        bl_full = sem("bl_full")
        wbst_done = sem("wbst_done")
        cpart_done = sem("cpart_done")
        tap_full = sem("tap_full")
        kz_done = sem("kz_done")
        wb_st_done = sem("wb_st_done")
        wc_st_done = sem("wc_st_done")
        kz_st_done = sem("kz_st_done")
        wi_st_done = sem("wi_st_done")
        yt_full = sem("yt_full")
        rms_full = sem("rms_full")
        rms_root = sem("rms_root")
        rms_done = sem("rms_done")
        y_low = sem("y_low")
        y_high = sem("y_high")
        gates_done = sem("gates_done")
        sig_done = sem("sig_done")
        silu_g = sem("silu_g")
        sc_full = sem("sc_full")
        sc_read = sem("sc_read")
        qk_done = sem("qk_done")
        vt_full = sem("vt_full")
        vtok_done = sem("vtok_done")
        kt_full = sem("kt_full")
        ktok_done = sem("ktok_done")
        vseq_done = sem("vseq_done")
        decay_done = sem("decay_done")
        kvp_full = sem("kvp_full")
        kvs_full = sem("kvs_full")
        chain_done = sem("chain_done")
        s_out_done = sem("s_out_done")
        o_full = sem("o_full")
        osq_done = sem("osq_done")
        r_full = sem("r_full")
        osd_done = sem("osd_done")
        inv_done = sem("inv_done")
        on_done = sem("on_done")
        og_done = sem("og_done")
        o_hi_done = sem("o_hi_done")
        o_ready = sem("o_ready")
        s_ld = [sem(f"s_ld{b}") for b in range(2)]
        s_st = [sem(f"s_st{b}") for b in range(2)]
        rows_ld = sem("rows_ld")
        sin_full = sem("sin_full")
        sin_done = sem("sin_done")
        wb_ld = [sem(f"wb_ld{b}") for b in range(2)]
        wy_ld = [sem(f"wy_ld{b}") for b in range(2)]
        u_done = sem("u_done")
        t1_full = sem("t1_full")
        t1_read = sem("t1_read")
        t2_full = sem("t2_full")
        t2_read = sem("t2_read")
        v_full = sem("v_full")
        v_read = sem("v_read")
        scan_done = sem("scan_done")
        fs_link = sem("fs_link")
        fs_done = sem("fs_done")
        stacked_done = sem("stacked_done")
        f_full = sem("f_full")
        f_done = sem("f_done")
        f_st = sem("f_st")
        y_full = sem("y_full")
        y_read = sem("y_read")
        t3_full = sem("t3_full")
        yy_done = sem("yy_done")
        gelu_done = sem("gelu_done")
        z_hi_done = sem("z_hi_done")
        z_ready = sem("z_ready")
        gs_done = sem("gs_done")
        yn_done = sem("yn_done")
        y_st = sem("y_st")

        up_at, at = {}, 0
        for p in PH:
            if p.kind == "up":
                up_at[p.name] = at
                at += 2 * p.pairs
        COL = {"ln_ffn1": 0, "ln_mix": 16, "ln_ffn2": 32, "ln_final": 48, "lb": 56, "s5_d": 72, "gnorm": 80}
        NVEC = 81
        NORMS = [(COL["ln_ffn1"], 0), (COL["ln_mix"], 1), (COL["ln_ffn2"], 2), (COL["ln_ffn1"] + NK, 3),
                 (COL["ln_mix"] + NK, None), (COL["ln_ffn2"] + NK, 4), (COL["ln_final"], None)]
        MAKES = {("down", ("ffn1_0", 1)): 1, ("hgrn_out", ("hgrn", 0)): 2, ("down", ("ffn2_0", 1)): 3,
                 ("down", ("ffn1_1", 1)): 4, ("glu", ("s5", 0)): 5, ("down", ("ffn2_1", 1)): 6}
        READS = {("up", ("ffn1_0", 0)): 0, ("hgrn_in", ("hgrn", 0)): 1, ("up", ("ffn2_0", 0)): 2,
                 ("up", ("ffn1_1", 0)): 3, ("up", ("ffn2_1", 0)): 5}

        Y_BANK = [6, 0, 2, 4, 6]

        def cols(t, i, n=1):
            flat = t[:].rearrange("p a b -> p (a b)")
            w = t.shape[2]
            return flat[:, bass.ds(i * w, n * w)]

        def halves(ap):
            return ap.rearrange("p (h t) -> p h t", h=2)

        def pair(s):
            return ps[:, 2 * s:2 * s + 2, 0:HALF]

        def f32(ap):
            return ap.bitcast(F32)

        def lifted(ap):
            return ap.rearrange("p (n t) -> p t n", t=LIFT)

        block = ctx.enter_context(nc.Block())

        @block.sync
        def _(sp):
            def load_rows(dst, src):
                sp.dma_start(dst, src).then_inc(vec_in, 16)

            at = 0
            for v, n in ((ln_ffn1, 16), (ln_mix, 16), (ln_ffn2, 16), (ln_final, 8), (hgrn_lb_logits, 16), (s5_d, 8)):
                flat = v.rearrange("l d -> (l d)") if len(v.shape) == 2 else v
                load_rows(vec_rows[at:at + n, :], flat.rearrange("(k c) -> k c", c=P))
                at += n
            load_rows(vec_rows[at:at + 1, :], hgrn_gnorm)
            assert at + 1 == NVEC

            def w_source(ph, j, i):
                kind, (name, g) = ph.kind, ph.name
                if kind in ("up", "down"):
                    layer = int(name[-1])
                    w_in, w_out = (ffn1_w_in, ffn1_w_out) if name[:4] == "ffn1" else (ffn2_w_in, ffn2_w_out)
                    f0 = g * F_GROUPS[0]
                if kind == "up":
                    v = w_in[layer].rearrange("(k p) (a f c) -> p k a f c", p=P, a=2, c=P)
                    return [v[:, :, a, i * 2 + (f0 + j), :] for a in range(2)]
                if kind == "down":
                    v = w_out[layer, f0 * P:(f0 + ph.kt) * P].rearrange("(k p) (m c) -> p k m c", p=P, c=P)
                    return [v[:, :, i * 2 + j, :]]
                if kind == "hgrn_in":
                    v = hgrn_w_in[0].rearrange("(k p) (r h c) -> p k r h c", p=P, r=4, c=P)
                    return [v[:, :, 2 * j + a, i, :] for a in range(2)]
                if kind == "hgrn_out":
                    return [hgrn_w_out[0].rearrange("(k p) (m c) -> p k m c", p=P, c=P)[:, :, i * 2 + j, :]]
                v = s5_w_glu[0].rearrange("(k p) (a m c) -> p k a m c", p=P, a=2, c=P)
                return [v[:, :, a, i * 2 + j, :] for a in range(2)]

            def load_pair(ph, i):
                for j in range(2):
                    sp.wait_ge(w_ready[j], i + ph.pair0)
                    sp.wait_ge(begun, 1)
                    dst = w_raw[j][:, 0:ph.size].rearrange("p (a k c) -> p a k c", a=ph.cols, c=P)
                    src = w_source(ph, j, i)
                    if ph.cols == 2:
                        for a in range(2):
                            sp.dma_start(dst[:, a], src[a]).then_inc(w_dma[j], 16)
                    else:
                        for r in range(2):
                            k0, k1 = r * ph.kt // 2, (r + 1) * ph.kt // 2
                            sp.dma_start(dst[:, 0, k0:k1], src[0][:, k0:k1]).then_inc(w_dma[j], 16)

            def load_piece(ct):
                sp.wait_ge(bpart_done, ct)
                sp.wait_ge(ct_full, ct)
                sp.wait_ge(begun, 1)
                for r, (b_d, c_d) in enumerate(((s5_b_re, s5_c_re), (s5_b_im, s5_c_im))):
                    b_v = b_d[0].rearrange("g p c -> (g p) c").rearrange("(a s q) c -> a q s c", s=ST_CT, q=P)
                    sp.dma_start(b_in[:, r], b_v[ct]).then_inc(pin, 16)
                    c_v = c_d[0].rearrange("g c p -> (g c) p").rearrange("(a q) p -> a q p", q=P)
                    for d in range(2):
                        sp.dma_start(c_in[:, r, d], c_v[ct]).then_inc(pin, 16)

            def matrices_stored():
                sp.wait_ge(wb_st_done, 16 * NK)
                sp.wait_ge(wc_st_done, 16 * NK)
                sp.wait_ge(kz_st_done, 32 * NK)

            def spread_taps(ct):
                for t in range(LIFT):
                    at = (LIFT - 1 - t) * GROUP_CH
                    for g in range(2):
                        dst = wi_d[ct, t * GROUP_CH:(t + 1) * GROUP_CH].rearrange("c (s g) q -> g c s q", g=2)[g]
                        sp.dma_start(dst, kz_d[ct, g, :, :, at:at + P]).then_inc(wi_st_done, 16)

            def load_y_matrices(ct):
                b = ct % 2
                sp.dma_start(wi[b][:], wi_d[ct]).then_inc(wy_ld[b], 16)
                for g in range(2):
                    rows = wc_d[ct, STATE * g:STATE * (g + 1)]
                    for half in range(2):
                        dst = wc[b][STATE * half:STATE * (half + 1)].rearrange("p (s g) q -> p g s q", g=2)[:, g]
                        sp.dma_start(dst, rows[:, half ^ g]).then_inc(wy_ld[b], 16)

            def s_load(h, b):
                sp.dma_start(s_in[b][:], state_hgrn[0, :, h].rearrange("b k v -> k b v")).then_inc(s_ld[b], 16)

            def s_store(h, b):
                sp.wait_ge(s_out_done, h + 1)
                sp.wait_ge(begun, 1)
                sp.dma_start(hgrn_s[0, :, h].rearrange("b k v -> k b v"), s_out[b][:]).then_inc(s_st[b], 16)
                sp.wait_ge(chain_done, h + 1)
                sp.wait_ge(begun, 1)
                sp.dma_start(hgrn_p[0, 0, h], s_end[b][:]).then_inc(s_st[b], 16)

            sp.wait_ge(begun, 1)
            for ph in PH:
                makes_s5 = ph.kind == "down" and ph.name[0] == "ffn1_0"
                if ph.kind == "hgrn_in":
                    for i in range(2):
                        load_pair(ph, i)
                        if i == 0:
                            sp.wait_ge(h_ready, 2 * NK)
                            matrices_stored()
                        s_load(i, i)
                    with sp.Fori(1, HEADS // 2) as i:
                        for b in range(2):
                            load_pair(ph, i * 2 + b)
                            s_store(i * 2 + (b - 2), b)
                            sp.wait_ge(o_full, i * 2 + (b - 1))
                            sp.wait_ge(begun, 1)
                            s_load(i * 2 + b, b)
                elif makes_s5:
                    for i in range(ph.pairs):
                        ct = i + ph.name[1] * (NK // 2)
                        load_pair(ph, i)
                        load_piece(ct)
                elif ph.kind == "glu":
                    load_pair(ph, 0)
                    sp.wait_ge(ssq_done, 5 * NK)
                    for r, s in enumerate((state_s5_re, state_s5_im)):
                        v = s[0].rearrange("b g p -> b (g p)").rearrange("b (s q) -> (b s) q", q=P)
                        sp.dma_start(st_rows[:, r], v.rearrange("(h r) q -> r h q", h=2)).then_inc(rows_ld, 16)
                    sp.wait_ge(wi_st_done, 256 * NK)
                    for ct in range(2):
                        sp.dma_start(wb[ct][:], wb_d[ct]).then_inc(wb_ld[ct], 16)
                    for ct in range(2):
                        load_y_matrices(ct)
                    for ct in range(2, NK):
                        sp.wait_ge(v_full, ct - 1)
                        sp.dma_start(wb[ct % 2][:], wb_d[ct]).then_inc(wb_ld[ct % 2], 16)
                    for ct in range(2, NK):
                        sp.wait_ge(y_full, ct - 1)
                        load_y_matrices(ct)
                    sp.wait_ge(f_done, 2)
                    for r, s in enumerate((re_p, im_p)):
                        v = s[0, 0].rearrange("g p -> (g p)").rearrange("(s q) -> s q", q=P)
                        sp.dma_start(v, fp_rows[:, r]).then_inc(f_st, 16)
                    for r, s in enumerate((re_s, im_s)):
                        v = s[0].rearrange("b g p -> b (g p)").rearrange("b (s q) -> (b s) q", q=P)
                        sp.dma_start(v.rearrange("(h r) q -> r h q", h=2), fs_rows[:, r]).then_inc(f_st, 16)
                    with sp.Fori(1, ph.pairs) as i:
                        load_pair(ph, i)
                elif ph.kind == "up" and ph.name[0] == "ffn2_0":
                    with sp.Fori(0, NK // 2) as i:
                        load_pair(ph, i)
                        spread_taps(i + ph.name[1] * (NK // 2))
                    with sp.Fori(NK // 2, ph.pairs) as i:
                        load_pair(ph, i)
                else:
                    if ph is PH[0]:
                        load_pair(ph, 0)
                    with sp.Fori(int(ph is PH[0]), ph.pairs) as i:
                        load_pair(ph, i)
                    if ph.kind == "hgrn_out":
                        for h in (HEADS - 2, HEADS - 1):
                            s_store(h, h % 2)
            for c in range(CHUNKS + 1):
                sp.wait_ge(y_low, c + 1)
                sp.wait_ge(y_high, c + 1)
                if c < CHUNKS:
                    sp.dma_start(y_prompt[0, c * P:(c + 1) * P, :], y_rows[:, c, :]).then_inc(y_st, 16)
                else:
                    sp.dma_start(y_sample.rearrange("b t d -> (b t) d"), y_rows[0:SAMPLE, c, :]).then_inc(y_st, 16)
            sp.wait_ge(y_st, 16 * (CHUNKS + 1))
            sp.wait_ge(f_st, 64)
            matrices_stored()
            sp.wait_ge(wi_st_done, 256 * NK)
            for b in range(2):
                sp.wait_ge(s_st[b], 32 * HEADS // 2 + 1)

        @block.gpsimd
        def _(pool):
            nc.gpsimd.memset(ident[:], 0.0).then_inc(begun, 1)
            nc.gpsimd.memset(ones[:], 1.0).then_inc(consts, 1)
            nc.gpsimd.memset(eps_t[:], EPS).then_inc(consts, 1)
            pool.wait_ge(begun, 1)
            nc.gpsimd.affine_select(out=ident[:], in_=ident[:], compare_op=ALU.not_equal, fill=1.0, base=0,
                                    pattern=[[-1, P]], channel_multiplier=1).then_inc(consts, 1)
            nc.gpsimd.iota(m_i[0][:], pattern=[[1, P]], base=0, channel_multiplier=0).then_inc(consts, 1)
            nc.gpsimd.iota(m_i[1][:], pattern=[[0, P]], base=0, channel_multiplier=1).then_inc(consts, 1)
            nc.gpsimd.memset(kz[:], 0.0).then_inc(s_st[0], 1)
            nc.gpsimd.memset(b_blk[:], 0.0).then_inc(s_st[1], 1)
            nc.gpsimd.memset(own_seq[:], 1.0).then_inc(consts, 1)
            pool.wait_ge(consts, 6)
            nc.gpsimd.affine_select(out=own_seq[:], in_=own_seq[:], compare_op=ALU.is_ge, fill=0.0, base=0,
                                    pattern=[[-DEC_SEQ, DEC_BATCH]], channel_multiplier=1).then_inc(consts, 1)
            pool.wait_ge(consts, 7)
            nc.gpsimd.affine_select(out=own_seq[:], in_=own_seq[:], compare_op=ALU.is_ge, fill=0.0, base=DEC_SEQ - 1,
                                    pattern=[[DEC_SEQ, DEC_BATCH]], channel_multiplier=-1).then_inc(consts, 1)

            def rest(ph, j, i):
                pool.wait_ge(w_hi_done[j], i + (ph.pair0 + 1))
                n = ph.size
                nc.gpsimd.tensor_tensor(w_lo[j][:, 0:n], w_raw[j][:, 0:n], f32(w_hi[j][:, 0:n]), ALU.subtract)\
                    .then_inc(w_ready[j], 1)

            def states(m, b, turn):
                pool.wait_ge(s_ld[b], turn * 16 + 16)
                pool.wait_ge(s_st[b], turn * 32 + 1)
                if not isinstance(m, int) or m:
                    pool.wait_ge(kvs_full, m)
                pool.wait_ge(vtok_done, m + 1)
                nc.gpsimd.tensor_tensor(
                    v_seq[:], v_tok[0:SAMPLE, CHUNKS, :].unsqueeze(1).to_broadcast([SAMPLE, DEC_BATCH, P]),
                    own_seq[:].unsqueeze(2).to_broadcast([SAMPLE, DEC_BATCH, P]), ALU.mult).then_inc(vseq_done, 1)
                pool.wait_ge(qk_done, m * LEVELS + SAMPLE_LEVELS)
                nc.gpsimd.tensor_tensor(
                    s_out[b][:], s_in[b][:],
                    e_t[:, 432 + PROMPT_BLOCKS:432 + BLOCKS].unsqueeze(2).to_broadcast([P, DEC_BATCH, P]),
                    ALU.mult).then_inc(decay_done, 1)

            def sampled_states(half):
                tiles = slice(half * ST // 2, (half + 1) * ST // 2)
                shape = [P, 2, DEC_BATCH, ST // 2]
                t1, t2 = (t[:, 0:ST * DEC_BATCH].rearrange("p (r b s) -> p r b s", r=2, b=DEC_BATCH) for t in z_t)
                before = s5_s[:, :, tiles, PROMPT_BLOCKS:].rearrange("p r s b -> p r b s")
                adds = s5_v[:, :, tiles, PROMPT_BLOCKS:].rearrange("p r s b -> p r b s")
                by = [lam8[:, q, :, tiles].unsqueeze(2).to_broadcast(shape) for q in range(2)]
                pool.wait_ge(sin_done, 1)
                pool.wait_ge(v_read, (half + 1) * NK // 2)
                pool.wait_ge(fs_done, half)
                nc.gpsimd.tensor_tensor(t1, before, by[0], ALU.mult).then_inc(fs_link, 1)
                nc.gpsimd.tensor_tensor(t2[:, ::-1], before, by[1], ALU.mult).then_inc(fs_link, 1)
                pool.wait_ge(fs_link, half * 3 + 2)
                nc.gpsimd.tensor_tensor(t1, t1, adds, ALU.add).then_inc(fs_link, 1)
                pool.wait_ge(fs_link, half * 3 + 3)
                nc.gpsimd.tensor_tensor(s5_fs[:, :, :, tiles], t1, t2, ALU.add).then_inc(fs_done, 1)

            for n, ph in enumerate(PH):
                if ph.kind == "glu":
                    rest(ph, 0, 0)
                    sampled_states(0)
                    sampled_states(1)
                    rest(ph, 1, 0)
                    with pool.Fori(1, ph.pairs) as i:
                        for j in range(2):
                            rest(ph, j, i)
                elif ph.kind == "hgrn_in":
                    rest(ph, 0, 0)
                    rest(ph, 1, 0)
                    rest(ph, 0, 1)
                    rest(ph, 1, 1)
                    states(0, 0, 0)
                    with pool.Fori(0, HEADS // 2 - 1) as i:
                        rest(ph, 0, i * 2 + 2)
                        rest(ph, 1, i * 2 + 2)
                        states(i * 2 + 1, 1, i)
                        rest(ph, 0, i * 2 + 3)
                        rest(ph, 1, i * 2 + 3)
                        states(i * 2 + 2, 0, i + 1)
                    rest(PH[n + 1], 0, 0)
                    rest(PH[n + 1], 1, 0)
                    states(HEADS - 1, 1, HEADS // 2 - 1)
                else:
                    with pool.Fori(int(ph.kind == "hgrn_out"), ph.pairs) as i:
                        for j in range(2):
                            rest(ph, j, i)

        @block.scalar
        def _(act):
            act.dma_start(x_rows[:, 0:CHUNKS, :], x_prompt[0].rearrange("(c p) d -> p c d", p=P)).then_inc(x_in, 16)
            act.dma_start(x_rows[0:SAMPLE, CHUNKS, :], x_sample.rearrange("b t d -> (b t) d")).then_inc(x_in, 16)
            lam_rows = s5_a_re[0].rearrange("g p -> (g p)").rearrange("(s q) -> s q", q=P)
            act.dma_start(lam_in[0:ST, :], lam_rows).then_inc(lam_ld, 16)
            lam_rows = s5_a_im[0].rearrange("g p -> (g p)").rearrange("(s q) -> s q", q=P)
            act.dma_start(lam_in[ST:2 * ST, :], lam_rows).then_inc(lam_ld, 16)
            act.dma_start(dt_in[2 * ST:3 * ST, :], s5_log_dt[0].rearrange("(s g) -> s g", g=2)).then_inc(lam_ld, 16)

            def split(ph, j, i, prev, i_prev):
                if prev is not None:
                    if i_prev is None:
                        s, n = prev.last_use(j)
                        act.wait_ge(full[s], n)
                    elif prev.kind == "glu":
                        for s in range(2):
                            act.wait_ge(full[s], i_prev * 2 + (prev.tile0 + j + 1))
                    elif prev.cols == 2:
                        act.wait_ge(full[1], i_prev * 2 + (prev.tile0 + j + 1))
                    else:
                        act.wait_ge(full[j], i_prev + (prev.tile0 + 1))
                act.wait_ge(w_dma[j], i * 32 + (ph.pair0 * 32 + 32))
                nc.scalar.activation(w_hi[j][:, 0:ph.size], w_raw[j][:, 0:ph.size], ACT.Copy).then_inc(w_hi_done[j], 1)

            def split_next(n, ph, j, i, last):
                if j == 0:
                    if isinstance(i, int) and i == 0:
                        if n and ph.kind != "hgrn_out":
                            split(ph, 1, 0, PH[n - 1], None)
                    else:
                        split(ph, 1, i, ph, i - 1)
                elif not last:
                    split(ph, 0, i + 1, ph, i)
                elif n + 1 < len(PH) and (ph.kind, ph.name) not in MAKES:
                    split(PH[n + 1], 0, 0, ph, None)

            def split_ahead(n, ph, j, last):
                if last and j == 0 and n + 1 < len(PH) and (ph.kind, ph.name) in MAKES:
                    split(PH[n + 1], 0, 0, ph, None)

            def norm_tile(r, m, taken):
                gain, fill = NORMS[r]
                act.wait_ge(*taken)
                act.wait_ge(ssq_done, m + r * NK)
                act.wait_ge(begun, 1)
                if r == len(NORMS) - 1:
                    nc.scalar.activation(cols(y_n, m), cols(x, m), ACT.Copy, scale=vec[:, bass.ds(m + gain, 1)])\
                        .then_inc(yn_done, 1)
                elif fill is not None:
                    nc.scalar.activation(cols(h_hi, m), cols(x, m), ACT.Copy, scale=vec[:, bass.ds(m + gain, 1)])\
                        .then_inc(h_hi_done, 1)
                nc.scalar.activation(sq[:], cols(x, m), ACT.Square).then_inc(sq_done, 1)

            def root(r):
                act.wait_ge(norm_full, r + 1)
                nc.scalar.activation(halves(sq[:]), ps[:, 4:6, 0:HALF], ACT.Sqrt, scale=1.0 / D_MODEL, bias=eps_t[:])\
                    .then_inc(sd_done, 1)

            act.wait_ge(vec_full, 1)
            nc.scalar.activation(vec[:, 0:NVEC], ps[:, 0, 0:NVEC], ACT.Copy).then_inc(vec_done, 1)
            act.wait_ge(vec_done, 1)
            for m in range(NK):
                if m == 2:
                    split(PH[0], 0, 0, None, None)
                if m == 5:
                    split(PH[0], 1, 0, None, None)
                norm_tile(0, m, (x_read, m + 1))

            def ffn_up(n, ph):
                base = up_at[ph.name]

                def unit(i, j, last=False):
                    u = i * 2 + (base + j)
                    t = i * 2 + (ph.tile0 + j)
                    split_next(n, ph, j, i, last)
                    if ph.name[1] == 0 and j == 0 and isinstance(i, int) and i == 0:
                        root(READS[(ph.kind, ph.name)])
                    act.wait_ge(free[0], t + 1)
                    act.wait_ge(g_full, u)
                    nc.scalar.activation(t_s[:], t_a[:], ACT.Silu).then_inc(silu_done, 1)
                    act.wait_ge(g_full, u + 1)
                    act.wait_ge(begun, 1)
                    nc.scalar.activation(cols(g_hi, i * 2 + j), t_g[:], ACT.Copy).then_inc(g_hi_done, 1)

                for j in range(2):
                    unit(0, j)
                with act.Fori(1, ph.pairs - 1) as i:
                    for j in range(2):
                        unit(i, j)
                for j in range(2):
                    unit(ph.pairs - 1, j, last=True)

            def ffn_down(n, ph):
                r = MAKES.get((ph.kind, ph.name))
                pieces = ph.kind == "down" and ph.name[0] == "ffn1_0"

                def unit(i, j, last=False):
                    split_next(n, ph, j, i, last)
                    if pieces:
                        ct = i + ph.name[1] * (NK // 2)
                        if j == 0:
                            act.wait_ge(ct_full, ct + 1)
                            act.wait_ge(cpart_done, ct)
                            v = ps[:, 7, 0:2 * P].rearrange("p (q g c) -> p q g c", g=2, c=GROUP_CH)
                            o = c_t[:].rearrange("p r s c -> p (r s) c")
                            nc.scalar.activation(o[0:STATE], v[0:STATE, :, 0], ACT.Copy)
                            nc.scalar.activation(o[STATE:P], v[STATE:P, :, 1], ACT.Copy).then_inc(ct_done, 1)
                            act.wait_ge(bl_full, ct + 1)
                            act.wait_ge(wb_st_done, ct * 16)
                            for q in range(2):
                                ins = nc.scalar.activation(wb_st[:, q].rearrange("p s q -> p (s q)"), ps[:, 4 + q, :],
                                                           ACT.Copy)
                            ins.then_inc(wbst_done, 1)
                            act.wait_ge(wbst_done, ct + 1)
                            act.wait_ge(begun, 1)
                            act.dma_start(wb_d[ct], wb_st[:]).then_inc(wb_st_done, 16)
                        else:
                            act.wait_ge(cpart_done, ct + 1)
                            act.wait_ge(begun, 1)
                            act.dma_start(wc_d[ct].rearrange("p r s q -> p (r s) q"),
                                          c_pow[:, :, :, GROUP_CH:].rearrange("p r s q -> p (r s) q"))\
                               .then_inc(wc_st_done, 16)
                    split_ahead(n, ph, j, last)
                    if r is not None:
                        norm_tile(r, i * 2 + j, (free[j], i + (ph.tile0 + 1)))
                    if pieces and j == 1:
                        act.wait_ge(tap_full, ct + 1)
                        act.wait_ge(kz_st_done, ct * 32)
                        nc.scalar.activation(kz[:, :, P - GROUP_CH:],
                                             ps[0:2 * GROUP_CH, 6, :].rearrange("p (s q) -> p s q", q=P), ACT.Copy)\
                            .then_inc(kz_done, 1)
                        act.wait_ge(kz_done, ct + 1)
                        act.wait_ge(begun, 1)
                        for g in range(2):
                            act.dma_start(kz_d[ct, g], kz[GROUP_CH * g:GROUP_CH * (g + 1)]).then_inc(kz_st_done, 16)

                for j in range(2):
                    unit(0, j)
                with act.Fori(1, ph.pairs - 1) as i:
                    for j in range(2):
                        unit(i, j)
                for j in range(2):
                    unit(ph.pairs - 1, j, last=True)

            def hgrn(n_ph, ph):
                def project_f(n, b):
                    act.wait_ge(free[1], n * 2 + (ph.tile0 + 1))
                    nc.scalar.activation(k_t[b][:], pre[:], ACT.Sigmoid, scale=-1.0).then_inc(sig_done, 1)
                    if not isinstance(n, int) or n:
                        act.wait_ge(qk_done, n * LEVELS - (LEVELS - 2))
                    nc.scalar.activation(f_t[:], pre[:], ACT.Sigmoid).then_inc(sig_done, 1)

                def project_g(n, b):
                    act.wait_ge(free[1], n * 2 + (ph.tile0 + 2))
                    nc.scalar.activation(s_g[b][:], pre[:], ACT.Silu).then_inc(silu_g, 1)

                def take_turned(m, bank_done, dst, done):
                    act.wait_ge(bank_done, m + 1)
                    if not isinstance(m, int) or m:
                        act.wait_ge(o_full, m)
                    nc.scalar.activation(dst[:, 0:CHUNKS, :].rearrange("p c q -> p (c q)"), ps[:, 6, :], ACT.Copy)
                    nc.scalar.activation(dst[0:SAMPLE, CHUNKS, :], ps[0:SAMPLE, 7, 0:P], ACT.Copy).then_inc(done, 1)

                def tail(m):
                    act.wait_ge(o_full, m + 1)
                    if not isinstance(m, int) or m:
                        act.wait_ge(og_done, m)
                    nc.scalar.activation(sq[:, 0:SEQ], ps[:, 5, :], ACT.Square)
                    nc.scalar.activation(sq[:, SEQ:T], ps[:, 4, 0:SAMPLE], ACT.Square).then_inc(osq_done, 1)
                    act.wait_ge(r_full, m + 1)
                    nc.scalar.activation(halves(sq[:]), ps[:, 6:8, 0:HALF], ACT.Sqrt, scale=1.0 / P, bias=eps_t[:])\
                        .then_inc(osd_done, 1)

                def o_high(head):
                    if head is not None:
                        act.wait_ge(og_done, head + 1)
                        act.wait_ge(begun, 1)
                        nc.scalar.activation(cols(o_hi, head), ssq[:], ACT.Copy).then_inc(o_hi_done, 1)

                def step(n, b, m, before, last=False):
                    if n is not None:
                        if isinstance(n, int) and n == 0:
                            split(ph, 1, 0, PH[n_ph - 1], None)
                            root(READS[(ph.kind, ph.name)])
                        else:
                            split(ph, 1, n, ph, n - 1)
                        project_f(n, b)
                    elif m is not None:
                        split(PH[n_ph + 1], 1, 0, ph, None)
                    if m is not None:
                        act.wait_ge(wb_st_done, 16 * NK)
                        act.wait_ge(wc_st_done, 16 * NK)
                        act.wait_ge(kz_st_done, 32 * NK)
                        take_turned(m, vt_full, v_tok, vtok_done)
                    if n is not None:
                        if last:
                            split(PH[n_ph + 1], 0, 0, ph, None)
                        else:
                            split(ph, 0, n + 1, ph, n)
                    if m is not None:
                        take_turned(m, kt_full, k_tok, ktok_done)
                    o_high(before)
                    if n is not None:
                        project_g(n, b)
                    if m is not None:
                        tail(m)

                step(0, 0, None, None)
                step(1, 1, 0, None)
                with act.Fori(0, HEADS // 2 - 2) as i:
                    step(i * 2 + 2, 0, i * 2 + 1, i * 2)
                    step(i * 2 + 3, 1, i * 2 + 2, i * 2 + 1)
                step(HEADS - 2, 0, HEADS - 3, HEADS - 4)
                step(HEADS - 1, 1, HEADS - 2, HEADS - 3, last=True)
                step(None, 0, HEADS - 1, HEADS - 2)
                step(None, 0, None, HEADS - 1)

            def s5(n, ph):
                root(4)
                act.wait_ge(sin_full, 1)
                for q in range(2):
                    v = ps[:, 6, 2 * P * q:2 * P * (q + 1)].rearrange("p (b s) -> p b s", s=ST)
                    ins = nc.scalar.activation(s5_s[:, q, :, PROMPT_BLOCKS:].rearrange("p s b -> p b s"), v, ACT.Copy)
                ins.then_inc(sin_done, 1)
                def take_v(ct):
                    act.wait_ge(v_full, ct + 1)
                    b = 4 + 2 * (ct % 2)
                    o = s5_v[:, :, ST_CT * ct:ST_CT * (ct + 1), :].rearrange("p r s n -> p r (s n)")
                    nc.scalar.activation(o, ps[:, b:b + 2, 0:HALF], ACT.Copy).then_inc(v_read, 1)

                for at in range(NK + 2):
                    if at < NK:
                        act.wait_ge(t1_full, at + 1)
                        if at >= 2:
                            act.wait_ge(t2_full, at - 1)
                        o = turned[at % 2][:].rearrange("n (g t c) -> n t g c", g=G_CT, t=LIFT)
                        for h in range(2):
                            v = ps[0:BLOCKS, h, :].rearrange("n (t g c) -> n t g c", g=G_CT, c=GROUP_CH)
                            ins = nc.scalar.activation(o[:, 4 * h:4 * h + 4], v, ACT.Copy)
                        ins.then_inc(t1_read, 1)
                    if at >= 2:
                        take_v(at - 2)
                    if 1 <= at <= NK:
                        ct = at - 1
                        act.wait_ge(t2_full, ct + 1)
                        o = u_lift[:, G_CT * ct:G_CT * (ct + 1), :].rearrange("p g n -> p (g n)")
                        nc.scalar.activation(halves(o), pair(1), ACT.Copy).then_inc(t2_read, 1)

                def take_y(ct):
                    act.wait_ge(y_full, ct + 1)
                    if ct >= 4:
                        act.wait_ge(t3_full, ct - 3)
                    o = turned[ct % 4][:].rearrange("n (t s g c) -> n g s t c", t=LIFT, g=2, c=GROUP_CH)
                    for g in range(2):
                        v = ps[0:BLOCKS, 4 + 2 * (ct % 2) + g, :].rearrange("n (s t c) -> n s t c", t=LIFT, c=GROUP_CH)
                        ins = nc.scalar.activation(o[:, g], v, ACT.Copy)
                    ins.then_inc(y_read, 1)

                def gelu(ct):
                    act.wait_ge(yy_done, ct + 1)
                    if ct >= 2:
                        act.wait_ge(z_ready, ct - 1)
                    nc.scalar.activation(z_t[ct % 2][:], y_f[ct % 2][:], ACT.Gelu_apprx_tanh).then_inc(gelu_done, 1)
                    act.wait_ge(gelu_done, ct + 1)
                    nc.scalar.activation(lifted(z_hi[:, ct]), z_t[ct % 2][:].rearrange("p (t n) -> p t n", t=LIFT),
                                         ACT.Copy).then_inc(z_hi_done, 1)

                def stack(ct):
                    half = ct // (NK // 2)
                    act.wait_ge(scan_done, half + 1)
                    act.wait_ge(fs_done, half + 1)
                    tiles = slice(ST_CT * ct, ST_CT * (ct + 1))
                    for g in range(2):
                        for up in range(2):
                            ins = nc.scalar.activation(stacked(ct)[STATE * up:STATE * (up + 1), :, g],
                                                       s5_s[STATE * g:STATE * (g + 1), up ^ g, tiles], ACT.Copy)
                    ins.then_inc(stacked_done, 1)

                stack(0)
                for ct in range(4):
                    if ct < 3:
                        stack(ct + 1)
                    take_y(ct)
                stack(4)
                stack(5)
                take_y(4)
                act.wait_ge(f_full, 1)
                nc.scalar.activation(fp_rows[:].rearrange("p r q -> p (r q)"), ps[0:ST, 0, 0:2 * P], ACT.Copy)\
                    .then_inc(f_done, 1)
                act.wait_ge(f_full, 2)
                nc.scalar.activation(fs_rows[:].rearrange("p r h q -> p (r h q)"), ps[:, 1, :], ACT.Copy)\
                    .then_inc(f_done, 1)
                gelu(0)
                gelu(1)
                for ct in range(5, NK):
                    if ct < NK - 1:
                        stack(ct + 1)
                    take_y(ct)
                    gelu(2 * (ct - 4))
                    gelu(2 * (ct - 4) + 1)

                def unit(i, j, last=False):
                    split_next(n, ph, j, i, last)
                    t = i * 2 + (ph.tile0 + j)
                    act.wait_ge(full[1], t + 1)
                    act.wait_ge(gs_done, i * 2 + j)
                    nc.scalar.activation(halves(t_s[:]), pair(1), ACT.Sigmoid).then_inc(free[1], 1)
                    split_ahead(n, ph, j, last)
                    norm_tile(5, i * 2 + j, (gs_done, i * 2 + (j + 1)))

                for j in range(2):
                    unit(0, j)
                with act.Fori(1, ph.pairs - 1) as i:
                    for j in range(2):
                        unit(i, j)
                for j in range(2):
                    unit(ph.pairs - 1, j, last=True)

            for n, ph in enumerate(PH):
                {"up": ffn_up, "down": ffn_down, "hgrn_in": hgrn, "hgrn_out": ffn_down, "glu": s5}[ph.kind](n, ph)
            act.wait_ge(rms_full, 1)
            nc.scalar.activation(y_rs[:, 0:CHUNKS], ps[:, 4, 0:CHUNKS], ACT.Sqrt, scale=1.0 / D_MODEL, bias=eps_t[:])
            nc.scalar.activation(y_rs[0:SAMPLE, CHUNKS:CHUNKS + 1], ps[0:SAMPLE, 4, CHUNKS:CHUNKS + 1], ACT.Sqrt,
                                 scale=1.0 / D_MODEL, bias=eps_t[0:SAMPLE]).then_inc(rms_root, 1)
            act.wait_ge(rms_done, 1)
            for c in range(CHUNKS + 1):
                n = P if c < CHUNKS else SAMPLE
                act.wait_ge(yt_full, c + 1)
                nc.scalar.activation(y_rows[0:n, c, 0:BANK], ps[0:n, Y_BANK[c], :], ACT.Copy, scale=y_rs[0:n, c:c + 1])\
                    .then_inc(y_low, 1)


        @block.vector
        def _(dve):
            link = Chain(dve, dve_link)
            V = nc.vector

            def norm_tile(r, m):
                gain, fill = NORMS[r]
                if fill is not None:
                    dve.wait_ge(h_hi_done, m + (fill * NK + 1))
                    V.scalar_tensor_tensor(out=cols(h_lo, m), in0=cols(x, m), scalar=vec[:, bass.ds(m + gain, 1)],
                                           in1=f32(cols(h_hi, m)), op0=ALU.mult, op1=ALU.subtract).then_inc(h_ready, 1)
                dve.wait_ge(ssq_done, m + r * NK)
                dve.wait_ge(sq_done, m + (r * NK + 1))
                V.tensor_tensor(ssq[:], ssq[:], sq[:], ALU.add).then_inc(ssq_done, 1)

            def clear_ssq(r):
                if r:
                    dve.wait_ge(norm_full, r)
                V.memset(ssq[:], 0.0).then_inc(ssq_zero, 1)
                dve.wait_ge(ssq_zero, r + 1)

            def reciprocal(r):
                dve.wait_ge(sd_done, r + 1)
                V.reciprocal(rstd[:], sq[:]).then_inc(rstd_done, 1)
                dve.wait_ge(rstd_done, r + 1)

            def scaled(dst, s):
                return V.tensor_tensor(halves(dst), pair(s), halves(rstd[:]), ALU.mult)

            clear_ssq(0)
            for m in range(NK + 1):
                if m < NK:
                    b = 4 + 2 * (m % 2)
                    dve.wait_ge(x_full, m + 1)
                    V.tensor_copy(x[:, m, 0:SEQ], ps[:, b, :])
                    V.tensor_copy(x[:, m, SEQ:T], ps[:, b + 1, 0:SAMPLE]).then_inc(x_read, 1)
                if m:
                    norm_tile(0, m - 1)
            dve.wait_ge(lam_ld, 48)
            V.tensor_copy(lam_in[2 * ST:3 * ST].rearrange("s (g p) -> s g p", g=2),
                          dt_in[2 * ST:3 * ST].unsqueeze(2).to_broadcast([ST, 2, STATE])).then_inc(dt_done, 1)

            def bounds():
                a0, a1 = vec[:, COL["lb"]:COL["lb"] + NK], vec[:, COL["lb"] + NK:COL["lb"] + 2 * NK]
                dve.wait_ge(vec_done, 1)
                link(V.tensor_tensor(lb_t[:, 0], a0, a1, ALU.max))
                link(V.tensor_tensor(lb_t[:, 1], a0, lb_t[:, 0], ALU.subtract))
                link(V.tensor_tensor(lb_t[:, 2], a1, lb_t[:, 0], ALU.subtract))
                link(exp_of(lb_t[:, 1:3, :].rearrange("p a b -> p (a b)"), 2 * NK))
                link(V.tensor_tensor(lb_t[:, 0], lb_t[:, 1], lb_t[:, 2], ALU.add))
                link(V.reciprocal(lb_t[:, 0], lb_t[:, 0]))
                link(V.tensor_tensor(lb_t[:, 1], lb_t[:, 1], lb_t[:, 0], ALU.mult))
                link(V.tensor_tensor(lb_t[:, 2], lb_t[:, 1], lb_t[:, 1], ALU.subtract))
                link(V.tensor_scalar(lb[:], lb_t[:, 2], 0.0, 1.0 - 1e-4, ALU.max, ALU.min))
                link(V.tensor_scalar(lb_c[:], lb[:], -1.0, 1.0, ALU.mult, ALU.add))

            def exp_of(v, w):
                n, r, y = (lam_sc[:, k, 0:w] for k in (20, 21, 22))
                n_i = lam_sc[:, 23, 0:w].bitcast(I32)
                round_ = 1.5 * 2.0 ** 23
                link(V.tensor_scalar(v, v, -87.0, 88.0, ALU.max, ALU.min))
                link(V.tensor_scalar(n, v, 1.4426950408889634, round_, ALU.mult, ALU.add))
                link(V.tensor_scalar(n, n, -round_, None, ALU.add))
                link(V.scalar_tensor_tensor(out=r, in0=n, scalar=-0.693359375, in1=v, op0=ALU.mult, op1=ALU.add))
                link(V.scalar_tensor_tensor(out=r, in0=n, scalar=2.12194440e-4, in1=r, op0=ALU.mult, op1=ALU.add))
                link(V.tensor_scalar(y, r, 1.0 / 5040, None, ALU.mult))
                for c in (1.0 / 720, 1.0 / 120, 1.0 / 24, 1.0 / 6, 0.5, 1.0):
                    link(V.scalar_tensor_tensor(out=y, in0=y, scalar=c, in1=r, op0=ALU.add, op1=ALU.mult))
                link(V.tensor_scalar(y, y, 1.0, None, ALU.add))
                link(V.tensor_scalar(n_i, n, 127.0, 2.0 ** 23, ALU.add, ALU.mult))
                return V.tensor_tensor(v, y, n_i.bitcast(F32), ALU.mult)

            def make_masks():
                dve.wait_ge(consts, 5)
                query, key, differ, v = m_i[0][:], m_i[1][:], m_i[2][:], m_f[0][:]
                link(V.tensor_tensor(differ, query, key, ALU.bitwise_xor))
                link(V.tensor_tensor(m_f[1][:], query, key, ALU.is_gt))
                link(V.tensor_tensor(v, differ, m_f[1][:], ALU.mult))
                link(V.tensor_tensor(masks[:, 0, :], query, key, ALU.is_equal))
                link(V.tensor_copy(masks_s[:, 0, :], masks[0:SAMPLE, 0, 0:SAMPLE]))
                link(V.tensor_scalar(m_f[2][:], v, float(DEC_SEQ), None, ALU.is_lt))
                for n, half in enumerate(HALVINGS):
                    link(V.tensor_scalar(m_f[3][:], v, float(half), None, ALU.is_ge))
                    link(V.tensor_copy(masks[:, n + 1, :], m_f[3][:]))
                    if n + 1 < SAMPLE_LEVELS:
                        link(V.tensor_tensor(masks_s[:, n + 1, :], m_f[3][0:SAMPLE, 0:SAMPLE],
                                             m_f[2][0:SAMPLE, 0:SAMPLE], ALU.mult))

            def row(k):
                return lam_sc[:, k, :]

            a_re, a_im, dt = (lam_c[:, k, :] for k in range(3))

            def step_sizes():
                dve.wait_ge(vec_full, 2)
                link(V.tensor_copy(lam_c[:].rearrange("p k s -> p (k s)"), ps[:, 7, 0:3 * ST]))
                link(exp_of(dt, ST))
                link(V.tensor_tensor(row(0), a_re, dt, ALU.mult))
                link(V.tensor_tensor(row(1), a_im, dt, ALU.mult))
                link(exp_of(row(0), ST))

            def lambda_bar():
                round_ = 1.5 * 2.0 ** 23
                link(V.tensor_scalar(row(2), row(1), 0.15915494309189535, round_, ALU.mult, ALU.add))
                link(V.tensor_scalar(row(2), row(2), -round_, None, ALU.add))
                for part in (-6.28125, -1.9353071795864769e-3):
                    link(V.scalar_tensor_tensor(out=row(1), in0=row(2), scalar=part, in1=row(1), op0=ALU.mult, op1=ALU.add))
                link(V.tensor_scalar(row(1), row(1), 3.1415925, -3.1415925, ALU.min, ALU.max))
                link(V.tensor_scalar(row(3), row(1), 0.5, None, ALU.mult))
                link(V.tensor_tensor(row(4), row(3), row(3), ALU.mult))
                link(V.tensor_scalar(row(5), row(4), 1.0 / 6227020800, None, ALU.mult))
                for c in (-1.0 / 39916800, 1.0 / 362880, -1.0 / 5040, 1.0 / 120, -1.0 / 6):
                    link(V.scalar_tensor_tensor(out=row(5), in0=row(5), scalar=c, in1=row(4), op0=ALU.add, op1=ALU.mult))
                link(V.scalar_tensor_tensor(out=row(5), in0=row(5), scalar=1.0, in1=row(3), op0=ALU.add, op1=ALU.mult))
                link(V.tensor_scalar(row(6), row(4), 1.0 / 479001600, None, ALU.mult))
                for c in (-1.0 / 3628800, 1.0 / 40320, -1.0 / 720, 1.0 / 24, -0.5):
                    link(V.scalar_tensor_tensor(out=row(6), in0=row(6), scalar=c, in1=row(4), op0=ALU.add, op1=ALU.mult))
                link(V.tensor_scalar(row(6), row(6), 1.0, 2.0, ALU.add, ALU.mult))
                link(V.tensor_tensor(row(6), row(6), row(5), ALU.mult))
                link(V.tensor_tensor(row(7), row(5), row(5), ALU.mult))
                link(V.tensor_scalar(row(7), row(7), -2.0, None, ALU.mult))
                link(V.tensor_tensor(row(11), row(0), row(6), ALU.mult))
                link(V.tensor_tensor(row(10), row(0), row(7), ALU.mult))
                link(V.tensor_scalar(row(12), row(0), -1.0, None, ALU.add))
                link(V.tensor_tensor(row(10), row(10), row(12), ALU.add))

            def b_factor():
                link(V.tensor_tensor(row(12), a_re, a_re, ALU.mult))
                link(V.tensor_tensor(row(13), a_im, a_im, ALU.mult))
                link(V.tensor_tensor(row(12), row(12), row(13), ALU.add))
                link(V.reciprocal(row(12), row(12)))
                link(V.tensor_tensor(row(13), row(10), a_re, ALU.mult))
                link(V.tensor_tensor(row(14), row(11), a_im, ALU.mult))
                link(V.tensor_tensor(row(13), row(13), row(14), ALU.add))
                link(V.tensor_tensor(row(8), row(13), row(12), ALU.mult))
                link(V.tensor_tensor(row(13), row(11), a_re, ALU.mult))
                link(V.tensor_tensor(row(14), row(10), a_im, ALU.mult))
                link(V.tensor_tensor(row(13), row(13), row(14), ALU.subtract))
                link(V.tensor_tensor(row(9), row(13), row(12), ALU.mult))

            def powers():
                link(V.memset(lam_p[:, 0, :, 0:1], 1.0))
                link(V.memset(lam_p[:, 1, :, 0:1], 0.0))
                link(V.tensor_scalar(lam_p[:, 0, :, 1], row(10), 1.0, None, ALU.add))
                link(V.tensor_copy(lam_p[:, 1, :, 1], row(11)))
                for n in (1, 2, 4):
                    a_r, a_i = (lam_p[:, q, :, 1:n + 1] for q in range(2))
                    b_r, b_i = (lam_p[:, q, :, n:n + 1].to_broadcast([P, ST, n]) for q in range(2))
                    o_r, o_i = (lam_p[:, q, :, n + 1:2 * n + 1] for q in range(2))
                    t = p_t1[:, 0:ST * n].rearrange("p (s n) -> p s n", n=n)
                    link(V.tensor_tensor(o_r, a_r, b_r, ALU.mult))
                    link(V.tensor_tensor(t, a_i, b_i, ALU.mult))
                    link(V.tensor_tensor(o_r, o_r, t, ALU.subtract))
                    link(V.tensor_tensor(o_i, a_r, b_i, ALU.mult))
                    link(V.tensor_tensor(t, a_i, b_r, ALU.mult))
                    link(V.tensor_tensor(o_i, o_i, t, ALU.add))
                for q in range(2):
                    link(V.tensor_copy(lam_r[:, q], lam_p[:, q, :, 0:LIFT][:, :, ::-1]))
                link(V.tensor_copy(lam8[:, 0, 0], lam_p[:, 0, :, LIFT]))
                link(V.tensor_copy(lam8[:, 0, 1], lam_p[:, 0, :, LIFT]))
                link(V.tensor_copy(lam8[:, 1, 0], lam_p[:, 1, :, LIFT]))
                link(V.tensor_scalar(lam8[:, 1, 1], lam_p[:, 1, :, LIFT], -1.0, None, ALU.mult))
                link(V.tensor_copy(row(12), lam_p[:, 0, :, LIFT]))
                link(V.tensor_copy(row(13), lam_p[:, 1, :, LIFT]))
                for _ in range(3):
                    link(V.tensor_tensor(row(14), row(12), row(12), ALU.mult))
                    link(V.tensor_tensor(row(15), row(13), row(13), ALU.mult))
                    link(V.scalar_tensor_tensor(out=row(13), in0=row(12), scalar=2.0, in1=row(13), op0=ALU.mult, op1=ALU.mult))
                    link(V.tensor_tensor(row(12), row(14), row(15), ALU.subtract))
                link(V.tensor_copy(lam64[:, 0, 0], row(12)))
                link(V.tensor_copy(lam64[:, 0, 1], row(12)))
                link(V.tensor_copy(lam64[:, 1, 0], row(13)))
                link(V.tensor_scalar(lam64[:, 1, 1], row(13), -1.0, None, ALU.mult))

            def complex_mult(out_r, out_i, a, b, t1, t2, done, negate_i=False):
                (a_r, a_i), (b_r, b_i) = a, b
                link(V.tensor_tensor(t1, a_r, b_r, ALU.mult))
                link(V.tensor_tensor(t2, a_i, b_i, ALU.mult))
                link(V.tensor_tensor(out_r, t1, t2, ALU.subtract))
                link(V.tensor_tensor(t1, a_r, b_i, ALU.mult))
                link(V.tensor_tensor(t2, a_i, b_r, ALU.mult))
                if negate_i:
                    done(V.scalar_tensor_tensor(out=out_i, in0=t1, scalar=-1.0, in1=t2, op0=ALU.mult, op1=ALU.subtract))
                else:
                    done(V.tensor_tensor(out_i, t1, t2, ALU.add))

            def of_ct(row, ct):
                return lam_sc[:, row, bass.ds(ct * ST_CT, ST_CT)].unsqueeze(2).to_broadcast([P, ST_CT, GROUP_CH])

            def b_part(ct):
                dve.wait_ge(pin, ct * 96 + 96)
                dve.wait_ge(bl_full, ct)
                dve.wait_ge(tap_full, ct)
                t1, t2 = (t[:, 0:ST_CT * GROUP_CH].rearrange("p (s c) -> p s c", s=ST_CT) for t in (p_t1, p_t2))
                complex_mult(b_bar[:, 0], b_bar[:, 1], (b_in[:, 0], b_in[:, 1]), (of_ct(8, ct), of_ct(9, ct)), t1, t2,
                             link)
                for g in range(2):
                    rows = slice(STATE * g, STATE * (g + 1))
                    link(V.tensor_copy(
                        b_blk[rows, :, :, GROUP_CH * g:GROUP_CH * (g + 1)].rearrange("p r s c -> p (r s) c"),
                        b_bar[rows].rearrange("p r s c -> p (r s) c")))
                shape = [P, ST_CT, LIFT, GROUP_CH]
                t1, t2 = (t[:, 0:ST_CT * P].rearrange("p (s t c) -> p s t c", s=ST_CT, t=LIFT) for t in (p_t1, p_t2))
                power = [lam_r[:, q, bass.ds(ct * ST_CT, ST_CT), :].unsqueeze(3).to_broadcast(shape)
                         for q in range(2)]
                bar = [b_bar[:, q].unsqueeze(2).to_broadcast(shape) for q in range(2)]
                out = [b_pow[:, q].rearrange("p s (t c) -> p s t c", t=LIFT) for q in range(2)]
                complex_mult(out[0], out[1], power, bar, t1, t2, lambda ins: ins.then_inc(bpart_done, 1))

            def c_part(ct):
                dve.wait_ge(ct_done, ct + 1)
                dve.wait_ge(bpart_done, ct + 1)
                dve.wait_ge(wc_st_done, ct * 16)
                shape = [P, ST_CT, LIFT + 1, GROUP_CH]
                t1, t2 = (t[:].rearrange("p (s t c) -> p s t c", s=ST_CT, c=GROUP_CH) for t in (p_t1, p_t2))
                power = [lam_p[:, q, bass.ds(ct * ST_CT, ST_CT), :].unsqueeze(3).to_broadcast(shape) for q in range(2)]
                c = [c_t[:, q].unsqueeze(2).to_broadcast(shape) for q in range(2)]
                out = [c_pow[:, q].rearrange("p s (t c) -> p s t c", c=GROUP_CH) for q in range(2)]
                complex_mult(out[0], out[1], c, power, t1, t2, lambda ins: ins.then_inc(cpart_done, 1), negate_i=True)

            def ffn_up(ph):
                base = up_at[ph.name]
                if (ph.kind, ph.name) in READS:
                    reciprocal(READS[(ph.kind, ph.name)])

                def unit(i, j):
                    u = i * 2 + (base + j)
                    t = i * 2 + (ph.tile0 + j)
                    dve.wait_ge(full[0], t + 1)
                    scaled(t_a[:], 0).then_inc(free[0], 1)
                    dve.wait_ge(full[1], t + 1)
                    scaled(t_b[:], 1).then_inc(free[1], 1)
                    dve.wait_ge(g_ready, u)
                    dve.wait_ge(free[1], t + 1)
                    dve.wait_ge(silu_done, u + 1)
                    V.tensor_tensor(t_g[:], t_b[:], t_s[:], ALU.mult).then_inc(g_full, 1)
                    dve.wait_ge(g_hi_done, u + 1)
                    V.tensor_tensor(cols(g_lo, i * 2 + j), t_g[:], f32(cols(g_hi, i * 2 + j)), ALU.subtract)\
                        .then_inc(g_ready, 1)

                first = 0
                if ph is PH[0]:
                    unit(0, 0)
                    unit(0, 1)
                    make_masks()
                    unit(1, 0)
                    bounds()
                    unit(1, 1)
                    step_sizes()
                    unit(2, 0)
                    lambda_bar()
                    unit(2, 1)
                    b_factor()
                    unit(3, 0)
                    powers()
                    unit(3, 1)
                    first = 4
                with dve.Fori(first, ph.pairs) as i:
                    for j in range(2):
                        unit(i, j)

            def down(ph):
                r = MAKES.get((ph.kind, ph.name))
                pieces = ph.kind == "down" and ph.name[0] == "ffn1_0"
                if r is not None:
                    if ph.kind == "hgrn_out":
                        dve.wait_ge(o_ready, HEADS)
                    clear_ssq(r)
                scale = 1.0 if ph.kind == "hgrn_out" else 0.5

                def unit(i, j):
                    if pieces and j == 0:
                        b_part(i + ph.name[1] * (NK // 2))
                        c_part(i + ph.name[1] * (NK // 2))
                    m = i * 2 + j
                    dve.wait_ge(full[j], i + (ph.tile0 + 1))
                    V.scalar_tensor_tensor(out=halves(cols(x, m)), in0=pair(j), scalar=scale, in1=halves(cols(x, m)),
                                           op0=ALU.mult, op1=ALU.add).then_inc(free[j], 1)
                    if r is not None:
                        norm_tile(r, m)

                link.settle()
                at, per = link.base, 6 + 2 + 5 + 5 if pieces else 0
                if pieces:
                    for j in range(2):
                        unit(0, j)
                    assert link.n == per
                    link.n = 0
                with dve.Fori(int(pieces), ph.pairs) as i:
                    link.base = i * per + at
                    for j in range(2):
                        unit(i, j)
                    assert link.n == per
                    link.n = 0
                link.base = at + ph.pairs * per

            def hgrn(ph):
                reciprocal(1)
                link(V.memset(score[:], 0.0))

                def level(m, b, n):
                    dve.wait_ge(sc_full, m * LEVELS + (n + 1))
                    q, k = q_t[b], k_t[b]
                    if n == 0:
                        V.tensor_tensor(q[:], q[:], f_t[:], ALU.mult).then_inc(qk_done, 1)
                    else:
                        if n == 3 and (not isinstance(m, int) or m):
                            dve.wait_ge(decay_done, m)
                        half = HALVINGS[n - 1]
                        span = T if half < DEC_SEQ else SEQ
                        blocks = span // (2 * half)
                        at = {1: None, 2: 0, 4: 288, 8: 432, 16: 504, 32: 536, 64: 552, 128: 560}
                        e = f_t[:, 0:span] if half == 1 else e_t[:, at[half]:at[half] + span // half]
                        e = e.rearrange("p (n h) -> p n h", h=2)
                        out = e_t[:, at[2 * half]:at[2 * half] + blocks]
                        qv = q[:, 0:span].rearrange("p (n h l) -> p n h l", h=2, l=half)
                        kv = k[:, 0:span].rearrange("p (n h l) -> p n h l", h=2, l=half)
                        shape = [P, blocks, half]
                        dve.wait_ge(qk_done, m * LEVELS + n)
                        V.tensor_tensor(qv[:, :, 1], qv[:, :, 1], e[:, :, 0:1].to_broadcast(shape), ALU.mult)
                        V.tensor_tensor(kv[:, :, 0], kv[:, :, 0], e[:, :, 1:2].to_broadcast(shape), ALU.mult)
                        V.tensor_tensor(out, e[:, :, 0], e[:, :, 1], ALU.mult).then_inc(qk_done, 1)
                    dve.wait_ge(begun, 1)
                    if n == 0 and (not isinstance(m, int) or m):
                        dve.wait_ge(o_full, m)
                    dve.wait_ge(sc_read, m * LEVELS + n)
                    shape = [P, CHUNKS, P]
                    ins = V.copy_predicated(score[:, 0:SEQ].rearrange("p (c q) -> p c q", q=P),
                                            masks[:, n, :].unsqueeze(1).to_broadcast(shape),
                                            ps[:, 4 + n % 2, :].rearrange("p (c q) -> p c q", q=P))
                    if n < SAMPLE_LEVELS:
                        ins = V.copy_predicated(score[0:SAMPLE, SEQ:T], masks_s[:, n, :], ps[0:SAMPLE, 6 + n % 2, 0:SAMPLE])
                    ins.then_inc(sc_read, 1)

                def take(dst, s, n, k):
                    dve.wait_ge(full[s], n * 2 + (ph.tile0 + k + 1))
                    scaled(dst, s).then_inc(free[s], 1)

                def gates(n, b):
                    dve.wait_ge(sig_done, n * 2 + 2)
                    link(V.tensor_scalar(f_t[:], f_t[:], lb_c[:, bass.ds(n, 1)], lb[:, bass.ds(n, 1)], ALU.mult, ALU.add))
                    V.tensor_scalar(f_t[:], f_t[:], GATE_FLOOR, None, ALU.max)
                    V.tensor_scalar(k_t[b][:], k_t[b][:], lb_c[:, bass.ds(n, 1)], None, ALU.mult).then_inc(gates_done, 1)

                def chain(m, b, turn):
                    kv = lambda c: ps[:, 4, c * P:(c + 1) * P]
                    dve.wait_ge(kvp_full, m + 1)
                    link(V.tensor_copy(s_chunk[:, 0, :], kv(0)))
                    for c in range(1, CHUNKS):
                        decay = e_t[:, 560 + c:561 + c]
                        out = s_chunk[:, c, :] if c < CHUNKS - 1 else s_end[b][:]
                        if c == CHUNKS - 1:
                            dve.wait_ge(s_st[b], turn * 32 + 1)
                        ins = V.scalar_tensor_tensor(out=out, in0=s_chunk[:, c - 1, :], scalar=decay, in1=kv(c),
                                                     op0=ALU.mult, op1=ALU.add)
                        if c < CHUNKS - 1:
                            link(ins)
                    ins.then_inc(chain_done, 1)

                def tail(m, b):
                    dve.wait_ge(kvs_full, m + 1)
                    dve.wait_ge(decay_done, m + 1)
                    sv = s_out[b][:].rearrange("p b v -> p (b v)").rearrange("p (h w) -> p h w", h=2)
                    V.tensor_tensor(sv, sv, ps[:, 6:8, :], ALU.add).then_inc(s_out_done, 1)
                    dve.wait_ge(silu_g, m + 1)
                    dve.wait_ge(o_ready, m)
                    dve.wait_ge(osq_done, m + 1)
                    gn = vec[:, COL["gnorm"]:COL["gnorm"] + 1]
                    V.scalar_tensor_tensor(out=ssq[:, 0:SEQ], in0=ps[:, 5, :], scalar=gn, in1=s_g[b][:, 0:SEQ],
                                           op0=ALU.mult, op1=ALU.mult)
                    V.scalar_tensor_tensor(out=ssq[:, SEQ:T], in0=ps[:, 4, 0:SAMPLE], scalar=gn,
                                           in1=s_g[b][:, SEQ:T], op0=ALU.mult, op1=ALU.mult).then_inc(on_done, 1)

                def invert(head, quarter):
                    if head is not None:
                        dve.wait_ge(osd_done, head + 1)
                        at = slice(quarter * T // 4, (quarter + 1) * T // 4)
                        V.reciprocal(o_rs[:, at], sq[:, at]).then_inc(inv_done, 1)

                def normalise(head):
                    if head is not None:
                        dve.wait_ge(on_done, head + 1)
                        dve.wait_ge(inv_done, head * 4 + 4)
                        V.tensor_tensor(ssq[:], ssq[:], o_rs[:], ALU.mult).then_inc(og_done, 1)

                def o_rest(head):
                    if head is not None:
                        dve.wait_ge(o_hi_done, head + 1)
                        V.tensor_tensor(cols(o_lo, head), ssq[:], f32(cols(o_hi, head)), ALU.subtract).then_inc(o_ready, 1)

                def step(n, b, m, turn, before):
                    links = int(n is not None) + (CHUNKS - 1 if m is not None else 0)
                    mb = 1 - b
                    if m is not None:
                        level(m, mb, 0)
                        level(m, mb, 1)
                    if n is not None:
                        take(q_t[b][:], 0, n, 0)
                    invert(before, 0)
                    if m is not None:
                        level(m, mb, 2)
                        level(m, mb, 3)
                    if n is not None:
                        if not isinstance(n, int) or n:
                            dve.wait_ge(silu_g, n)
                        take(pre[:], 1, n, 0)
                    if m is not None:
                        level(m, mb, 4)
                    invert(before, 1)
                    if m is not None:
                        level(m, mb, 5)
                    if n is not None:
                        gates(n, b)
                    if m is not None:
                        level(m, mb, 6)
                    if n is not None:
                        if not isinstance(n, int) or n:
                            dve.wait_ge(vt_full, n)
                        take(v_t[:], 0, n, 1)
                    if m is not None:
                        level(m, mb, 7)
                    invert(before, 2)
                    invert(before, 3)
                    normalise(before)
                    if m is not None:
                        chain(m, mb, turn)
                    o_rest(before)
                    if n is not None:
                        take(pre[:], 1, n, 1)
                    if m is not None:
                        tail(m, mb)
                    assert link.n == links, (link.n, links)

                link.settle()
                step(0, 0, None, None, None)
                link.settle()
                step(1, 1, 0, 0, None)
                link.settle()
                at = link.base
                one = 1 + CHUNKS - 1
                with dve.Fori(0, HEADS // 2 - 1) as i:
                    link.base = i * (2 * one) + at
                    step(i * 2 + 2, 0, i * 2 + 1, i, i * 2)
                    link.settle()
                    step(i * 2 + 3, 1, i * 2 + 2, i + 1, i * 2 + 1)
                    link.n = 0
                link.base = at + (HEADS // 2 - 1) * 2 * one
                step(None, 0, HEADS - 1, HEADS // 2 - 1, HEADS - 2)
                link.settle()
                step(None, 0, None, None, HEADS - 1)

            def s5(ph):
                reciprocal(4)
                for ct in range(NK):
                    V.scalar_tensor_tensor(out=u_t[:, ct].rearrange("p (t n) -> p t n", t=LIFT), in0=lifted(x[:, ct]),
                                           scalar=vec[:, NORMS[4][0] + ct:NORMS[4][0] + ct + 1], in1=lifted(rstd[:]),
                                           op0=ALU.mult, op1=ALU.mult).then_inc(u_done, 1)
                link.settle()
                dve.wait_ge(norm_full, 5)
                half_st = ST // 2

                def advance(out, before, adds, lam, done):
                    w = 2 * half_st * (SUPER if len(out.shape) == 4 else 1)
                    t1, t2 = (t[:, 0:w].rearrange("p (r s) -> p r s", r=2) for t in (sq, ssq))
                    if len(out.shape) == 4:
                        t1, t2 = (t.rearrange("p r (s b) -> p r s b", b=SUPER) for t in (t1, t2))
                    first = link.begin(V.tensor_tensor(t1, before, lam[0], ALU.mult))
                    link.begin(V.tensor_tensor(t2[:, ::-1], before, lam[1], ALU.mult))
                    dve.wait_ge(dve_link, first)
                    link(V.tensor_tensor(t1, t1, adds, ALU.add))
                    done(V.tensor_tensor(out, t1, t2, ALU.add))

                def scan(half):
                    tiles = slice(half * half_st, (half + 1) * half_st)
                    dve.wait_ge(v_read, (half + 1) * NK // 2)
                    shape = [P, 2, half_st, SUPER]
                    by8 = [lam8[:, q, :, tiles].unsqueeze(3).to_broadcast(shape) for q in range(2)]
                    by64 = [lam64[:, q, :, tiles] for q in range(2)]
                    v = s5_v[:, :, tiles, 0:PROMPT_BLOCKS].rearrange("p r s (b j) -> p r s b j", j=STEPS)
                    s = s5_s[:, :, tiles, 0:PROMPT_BLOCKS].rearrange("p r s (b j) -> p r s b j", j=STEPS)
                    e, edge = s5_e[:, :, tiles], s5_b[:, :, tiles]
                    link(V.tensor_scalar(e, v[:, :, :, :, 0], 1.0, None, ALU.mult))
                    for j in range(1, STEPS):
                        advance(e, e, v[:, :, :, :, j], by8, link)
                    link(V.memset(edge[:, :, :, 0:1], 0.0))
                    for b in range(SUPER):
                        advance(edge[:, :, :, b + 1], edge[:, :, :, b], e[:, :, :, b], by64, link)
                    link(V.tensor_scalar(s[:, :, :, :, 0], edge[:, :, :, 0:SUPER], 1.0, None, ALU.mult))
                    for j in range(1, STEPS - 1):
                        advance(s[:, :, :, :, j], s[:, :, :, :, j - 1], v[:, :, :, :, j - 1], by8, link)
                    j = STEPS - 1
                    advance(s[:, :, :, :, j], s[:, :, :, :, j - 1], v[:, :, :, :, j - 1], by8,
                            lambda ins: ins.then_inc(scan_done, 1))
                    dve.wait_ge(scan_done, half + 1)

                scan(0)
                scan(1)

                def z_rest(ct):
                    dve.wait_ge(z_hi_done, ct + 1)
                    V.tensor_tensor(lifted(z_lo[:, ct]), z_t[ct % 2][:].rearrange("p (t n) -> p t n", t=LIFT),
                                    f32(lifted(z_hi[:, ct])), ALU.subtract).then_inc(z_ready, 1)

                for ct in range(NK):
                    dve.wait_ge(t3_full, ct + 1)
                    if ct >= 2:
                        dve.wait_ge(gelu_done, ct - 1)
                    V.scalar_tensor_tensor(out=halves(y_f[ct % 2][:]), in0=halves(u_t[:, ct]),
                                           scalar=vec[:, COL["s5_d"] + ct:COL["s5_d"] + ct + 1],
                                           in1=pair(1), op0=ALU.mult, op1=ALU.add).then_inc(yy_done, 1)
                    if ct:
                        z_rest(ct - 1)
                z_rest(NK - 1)
                link.settle()
                clear_ssq(5)

                def unit(i, j):
                    t = i * 2 + (ph.tile0 + j)
                    m = i * 2 + j
                    dve.wait_ge(full[0], t + 1)
                    dve.wait_ge(free[1], t + 1)
                    V.tensor_tensor(halves(t_a[:]), pair(0), halves(t_s[:]), ALU.mult).then_inc(free[0], 1)
                    dve.wait_ge(free[0], t + 1)
                    V.tensor_tensor(cols(x, m), cols(x, m), t_a[:], ALU.add).then_inc(gs_done, 1)
                    norm_tile(5, m)

                with dve.Fori(0, ph.pairs) as i:
                    for j in range(2):
                        unit(i, j)

            for ph in PH:
                {"up": ffn_up, "down": down, "hgrn_in": hgrn, "hgrn_out": down, "glu": s5}[ph.kind](ph)
            dve.wait_ge(rms_root, 1)
            V.reciprocal(y_rs[:, 0:CHUNKS], y_rs[:, 0:CHUNKS])
            V.reciprocal(y_rs[0:SAMPLE, CHUNKS:CHUNKS + 1], y_rs[0:SAMPLE, CHUNKS:CHUNKS + 1]).then_inc(rms_done, 1)
            dve.wait_ge(rms_done, 1)
            for c in range(CHUNKS + 1):
                n = P if c < CHUNKS else SAMPLE
                dve.wait_ge(yt_full, c + 1)
                V.tensor_scalar(y_rows[0:n, c, BANK:], ps[0:n, Y_BANK[c] + 1, :], y_rs[0:n, c:c + 1], None, ALU.mult)\
                    .then_inc(y_high, 1)

        @block.tensor
        def _(pe):
            M = nc.tensor

            def turn(out, t, n=P, w=P):
                return M.transpose(out, t, ident[0:n, 0:n])

            def sum_tokens(r):
                pe.wait_ge(ssq_done, NK * (r + 1))
                pe.wait_ge(consts, 3)
                if r:
                    pe.wait_ge(sd_done, r)
                if r == 2:
                    pe.wait_ge(og_done, HEADS)
                if r == 5:
                    pe.wait_ge(y_read, NK)
                for h in range(2):
                    ins = M.matmul(ps[:, 4 + h, 0:HALF], ones[:], ssq[:, h * HALF:(h + 1) * HALF], start=True, stop=True)
                ins.then_inc(norm_full, 1)

            def product(ph, j, a, i, hi, lo, before=None, part=None):
                k0, k1 = part or (0, ph.kt)
                s, t = (a, i * 2 + (ph.tile0 + j)) if ph.cols == 2 else (j, i + ph.tile0)
                if k0 == 0:
                    pe.wait_ge(w_ready[j], i + (ph.pair0 + 1))
                    pe.wait_ge(free[s], t)
                for k in range(k0, k1):
                    if before is not None:
                        before(k)
                    at = (a * ph.kt + k) * P
                    for n, (w, v) in enumerate(((w_hi, hi), (w_hi, lo), (w_lo, hi))):
                        for h in range(2):
                            ins = M.matmul(ps[:, 2 * s + h, 0:HALF], w[j][:, at:at + P], v[:, k, h * HALF:(h + 1) * HALF],
                                           start=k == 0 and n == 0, stop=k == ph.kt - 1 and n == 2)
                if k1 == ph.kt:
                    ins.then_inc(full[s], 1)

            def tokens(m):
                b = 4 + 2 * (m % 2)
                if m >= 2:
                    pe.wait_ge(x_read, m - 1)
                for c in range(CHUNKS):
                    turn(ps[:, b, c * P:(c + 1) * P], x_rows[:, c, m * P:(m + 1) * P])
                turn(ps[:, b + 1, 0:SAMPLE], x_rows[0:SAMPLE, CHUNKS, m * P:(m + 1) * P], SAMPLE).then_inc(x_full, 1)

            pe.wait_ge(consts, 3)
            pe.wait_ge(vec_in, 7 * 16)
            turn(ps[:, 0, 0:NVEC], vec_rows[0:NVEC, :], NVEC).then_inc(vec_full, 1)
            pe.wait_ge(x_in, 32)
            for m in range(NK - 2):
                tokens(m)
            pe.wait_ge(vec_done, 1)
            for m in range(NK):
                if m < 2:
                    tokens(NK - 2 + m)
                for a in range(2):
                    product(PH[0], 0, a, 0, h_hi, h_lo, lambda k: pe.wait_ge(h_ready, k + 1), (m, m + 1))
                if m == NK - 2:
                    sum_tokens(0)
            pe.wait_ge(lam_ld, 48)
            pe.wait_ge(dt_done, 1)
            turn(ps[:, 7, 0:3 * ST], lam_in[0:3 * ST, :], 3 * ST).then_inc(vec_full, 1)

            def reads_norm(ph):
                r = READS[(ph.kind, ph.name)]
                fill = NORMS[r][1]

                def before(k):
                    pe.wait_ge(h_ready, fill * NK + k + 1)
                    if k == NK - 1:
                        sum_tokens(r)
                return before

            def ffn_up(ph):
                first = reads_norm(ph) if (ph.kind, ph.name) in READS else None
                for j in range(int(ph is PH[0]), 2):
                    for a in range(2):
                        product(ph, j, a, 0, h_hi, h_lo, first if (j, a) == (0, 0) else None)
                with pe.Fori(1, ph.pairs) as i:
                    for j in range(2):
                        for a in range(2):
                            product(ph, j, a, i, h_hi, h_lo)

            def c_turned(ct):
                pe.wait_ge(pin, ct * 96 + 96)
                pe.wait_ge(ct_done, ct)
                for r in range(2):
                    ins = turn(ps[:, 7, r * P:(r + 1) * P], c_in[:, r].rearrange("p d q -> p (d q)"))
                ins.then_inc(ct_full, 1)

            def b_turned(ct):
                pe.wait_ge(bpart_done, ct + 1)
                pe.wait_ge(wbst_done, ct)
                for r in range(2):
                    for st in range(ST_CT):
                        ins = turn(ps[:, 4 + r, st * P:(st + 1) * P], b_pow[:, r, st])
                ins.then_inc(bl_full, 1)

            def taps(ct):
                pe.wait_ge(cpart_done, ct + 1)
                pe.wait_ge(kz_done, ct)
                for st in range(ST_CT):
                    for r in range(2):
                        ins = M.matmul(ps[0:2 * GROUP_CH, 6, st * P:(st + 1) * P], b_blk[:, r, st], c_pow[:, r, st, 0:P],
                                       start=r == 0, stop=r == 1)
                ins.then_inc(tap_full, 1)

            def down(ph):
                pieces = ph.name[0] == "ffn1_0"
                made = up_at.get(ph.name, 0)

                def before(k):
                    if ph.kind == "hgrn_out":
                        pe.wait_ge(o_ready, k + 1)
                    elif k == 0:
                        pe.wait_ge(g_ready, made + ph.kt - 1)
                    elif k == ph.kt - 1:
                        pe.wait_ge(g_ready, made + ph.kt)

                hi, lo = (o_hi, o_lo) if ph.kind == "hgrn_out" else (g_hi, g_lo)
                ct0 = ph.name[1] * (NK // 2)

                def pair_of(i, first=None):
                    if pieces:
                        c_turned(i + ct0)
                    begun_at = None
                    if first is not None and ph.kind == "hgrn_out":
                        begun_at = HEADS - 2
                        product(ph, 0, 0, i, hi, lo, first, (begun_at, HEADS - 1))
                        product(ph, 1, 0, i, hi, lo, None, (begun_at, HEADS - 1))
                        product(ph, 0, 0, i, hi, lo, first, (HEADS - 1, HEADS))
                    else:
                        product(ph, 0, 0, i, hi, lo, first)
                    if pieces:
                        b_turned(i + ct0)
                    product(ph, 1, 0, i, hi, lo, None, (HEADS - 1, HEADS) if begun_at else None)
                    if pieces:
                        taps(i + ct0)

                if pieces:
                    pe.wait_ge(sd_done, 1)
                pair_of(0, before)
                with pe.Fori(1, ph.pairs) as i:
                    pair_of(i)

            def hgrn(ph):
                out_ph = PH[PH.index(ph) + 1]

                def level(m, b, n):
                    if n == 0:
                        if not isinstance(m, int) or m:
                            pe.wait_ge(on_done, m)
                            pe.wait_ge(osd_done, m)
                        pe.wait_ge(gates_done, m + 1)
                    else:
                        pe.wait_ge(qk_done, m * LEVELS + n)
                    if n >= 2:
                        pe.wait_ge(sc_read, m * LEVELS + (n - 1))
                    for c in range(CHUNKS):
                        at = slice(c * P, (c + 1) * P)
                        ins = M.matmul(ps[:, 4 + n % 2, at], k_t[b][:, at], q_t[b][:, at], start=True, stop=True)
                    if n < SAMPLE_LEVELS:
                        ins = M.matmul(ps[0:SAMPLE, 6 + n % 2, 0:SAMPLE], k_t[b][:, SEQ:T], q_t[b][:, SEQ:T],
                                       start=True, stop=True)
                    ins.then_inc(sc_full, 1)

                def turned(t, done):
                    for c in range(CHUNKS):
                        turn(ps[:, 6, c * P:(c + 1) * P], t[:, c * P:(c + 1) * P])
                    turn(ps[0:SAMPLE, 7, 0:P], t[:, SEQ:T]).then_inc(done, 1)

                def v_turned(m):
                    pe.wait_ge(free[0], m * 2 + (ph.tile0 + 2))
                    pe.wait_ge(sc_read, m * LEVELS + SAMPLE_LEVELS)
                    turned(v_t, vt_full)

                def k_turned(m, b):
                    pe.wait_ge(qk_done, m * LEVELS + LEVELS)
                    pe.wait_ge(vtok_done, m + 1)
                    turned(k_t[b], kt_full)

                def chunk_adds(m):
                    pe.wait_ge(ktok_done, m + 1)
                    pe.wait_ge(sc_read, m * LEVELS + (LEVELS - 1))
                    for c in range(CHUNKS):
                        ins = M.matmul(ps[:, 4, c * P:(c + 1) * P], k_tok[:, c, :], v_tok[:, c, :], start=True, stop=True)
                    ins.then_inc(kvp_full, 1)

                def tail(m, b):
                    pe.wait_ge(vseq_done, m + 1)
                    for h in range(2):
                        v = v_seq[:, 4 * h:4 * h + 4, :].rearrange("p b v -> p (b v)")
                        ins = M.matmul(ps[:, 6 + h, :], k_tok[0:SAMPLE, CHUNKS, :], v, start=True, stop=True)
                    ins.then_inc(kvs_full, 1)
                    pe.wait_ge(sc_read, m * LEVELS + LEVELS)
                    pe.wait_ge(chain_done, m + 1)
                    for c in range(CHUNKS):
                        at = slice(c * P, (c + 1) * P)
                        M.matmul(ps[:, 5, at], v_tok[:, c, :], score[:, at], start=True, stop=c == 0)
                        if c:
                            M.matmul(ps[:, 5, at], s_chunk[:, c - 1, :], q_t[b][:, at], start=False, stop=True)
                    pe.wait_ge(decay_done, m + 1)
                    M.matmul(ps[:, 4, 0:SAMPLE], v_tok[0:SAMPLE, CHUNKS, :], score[0:SAMPLE, SEQ:T], start=True, stop=False)
                    for n in range(DEC_BATCH):
                        at = SEQ + n * DEC_SEQ
                        ins = M.matmul(ps[:, 4, n * DEC_SEQ:(n + 1) * DEC_SEQ], s_in[b][:, n, :],
                                       q_t[b][:, at:at + DEC_SEQ], start=False, stop=n == DEC_BATCH - 1)
                    ins.then_inc(o_full, 1)
                    pe.wait_ge(osq_done, m + 1)
                    pe.wait_ge(s_out_done, m + 1)
                    for h in range(2):
                        ins = M.matmul(ps[:, 6 + h, 0:HALF], ones[:], sq[:, h * HALF:(h + 1) * HALF], start=True, stop=True)
                    ins.then_inc(r_full, 1)

                def step(n, b, m):
                    first = reads_norm(ph) if isinstance(n, int) and n == 0 else None
                    cuts = (3, 6, 9, 13, 16, 19, 22, 25, 28, 30, 32)
                    done = 0
                    for at, cut in enumerate(cuts):
                        while n is not None and done < cut:
                            tile, k0 = divmod(done, NK)
                            k1 = min(NK, k0 + cut - done)
                            product(ph, tile // 2, tile % 2, n, h_hi, h_lo, first if tile == 0 else None, (k0, k1))
                            done += k1 - k0
                        if n is None and at < HEADS - 2:
                            j, k = divmod(2 * at, HEADS - 2)
                            product(out_ph, j, 0, 0, o_hi, o_lo, lambda k: pe.wait_ge(o_ready, k + 1), (k, k + 2))
                        if m is not None:
                            if at < LEVELS:
                                level(m, 1 - b, at)
                            if at == SAMPLE_LEVELS:
                                v_turned(m)
                            if at == LEVELS:
                                k_turned(m, 1 - b)
                            if at == LEVELS + 1:
                                chunk_adds(m)
                    if m is not None:
                        tail(m, 1 - b)

                pe.wait_ge(wbst_done, NK)
                pe.wait_ge(kz_done, NK)
                step(0, 0, None)
                step(1, 1, 0)
                with pe.Fori(0, HEADS // 2 - 1) as i:
                    step(i * 2 + 2, 0, i * 2 + 1)
                    step(i * 2 + 3, 1, i * 2 + 2)
                step(None, 0, HEADS - 1)

            def s5(ph):
                sum_tokens(4)
                pe.wait_ge(rows_ld, 32)
                for q in range(2):
                    for h in range(2):
                        at = (2 * q + h) * P
                        ins = turn(ps[:, 6, at:at + P], st_rows[:, q, h])
                ins.then_inc(sin_full, 1)
                pe.wait_ge(sd_done, 5)

                def blocks_first(ct):
                    pe.wait_ge(u_done, ct + 1)
                    if ct:
                        pe.wait_ge(t1_read, ct)
                    for t in range(LIFT):
                        ins = turn(ps[0:BLOCKS, t // 4, (t % 4) * P:(t % 4 + 1) * P], u_t[:, ct, t * BLOCKS:(t + 1) * BLOCKS])
                    ins.then_inc(t1_full, 1)

                def places_first(ct):
                    pe.wait_ge(t1_read, ct + 1)
                    if ct:
                        pe.wait_ge(t2_read, ct)
                    for g in range(G_CT):
                        ins = turn(ps[:, 2 + g // 4, (g % 4) * BLOCKS:(g % 4 + 1) * BLOCKS],
                                   turned[ct % 2][:, g * P:(g + 1) * P], BLOCKS)
                    ins.then_inc(t2_full, 1)

                def block_adds(ct):
                    pe.wait_ge(t2_read, ct + 1)
                    pe.wait_ge(wb_ld[ct % 2], 16 * (ct // 2 + 1))
                    if ct == 1:
                        pe.wait_ge(sin_done, 1)
                    if ct >= 2:
                        pe.wait_ge(v_read, ct - 1)
                    for r in range(2):
                        for g in range(2):
                            for st in range(ST_CT):
                                ins = M.matmul(
                                    ps[STATE * g:STATE * (g + 1), 4 + 2 * (ct % 2) + r, st * BLOCKS:(st + 1) * BLOCKS],
                                    wb[ct % 2][:, r, st, STATE * g:STATE * (g + 1)], u_lift[:, G_CT * ct + 2 * st + g, :],
                                    start=True, stop=True)
                    ins.then_inc(v_full, 1)

                for at in range(NK + 2):
                    if at < NK:
                        blocks_first(at)
                    if at >= 2:
                        block_adds(at - 2)
                    if 1 <= at <= NK:
                        places_first(at - 1)

                def outputs(ct):
                    pe.wait_ge(wy_ld[ct % 2], 80 * (ct // 2 + 1))
                    pe.wait_ge(stacked_done, ct + 1)
                    if ct < 2:
                        pe.wait_ge(v_read, NK)
                    else:
                        pe.wait_ge(y_read, ct - 1)
                    for g in range(G_CT):
                        st, g2 = g // 2, g % 2
                        out = ps[0:BLOCKS, 4 + 2 * (ct % 2) + g2, st * P:(st + 1) * P]
                        M.matmul(out, u_lift[:, G_CT * ct + g, :], wi[ct % 2][:, g], start=True, stop=False)
                        ins = M.matmul(out, stacked(ct)[:, st, g2], wc[ct % 2][:, g], start=False, stop=True)
                    ins.then_inc(y_full, 1)

                def channels_first(ct):
                    pe.wait_ge(y_read, ct + 1)
                    if ct:
                        pe.wait_ge(yy_done, ct)
                    for t in range(LIFT):
                        ins = turn(ps[:, 2 + t // 4, (t % 4) * BLOCKS:(t % 4 + 1) * BLOCKS],
                                   turned[ct % 4][:, t * P:(t + 1) * P], BLOCKS)
                    ins.then_inc(t3_full, 1)

                def last_states():
                    pe.wait_ge(t1_read, NK)
                    pe.wait_ge(scan_done, 2)
                    for q in range(2):
                        ins = turn(ps[0:ST, 0, q * P:(q + 1) * P], s5_b[:, q, :, SUPER])
                    ins.then_inc(f_full, 1)
                    pe.wait_ge(fs_done, 2)
                    for q in range(2):
                        for h in range(2):
                            at = (2 * q + h) * P
                            ins = turn(ps[:, 1, at:at + P], s5_fs[:, q, 4 * h:4 * h + 4].rearrange("p b s -> p (b s)"))
                    ins.then_inc(f_full, 1)

                def glu_part(k0, k1):
                    if k0 == 0:
                        pe.wait_ge(f_done, 2)
                    product(ph, 0, 0, 0, z_hi, z_lo, lambda k: pe.wait_ge(z_ready, k + 1), (k0, k1))

                for ct in range(5):
                    outputs(ct)
                channels_first(0)
                last_states()
                channels_first(1)
                outputs(5)
                channels_first(2)
                glu_part(0, 1)
                channels_first(3)
                glu_part(1, 2)
                outputs(6)
                channels_first(4)
                glu_part(2, 3)
                channels_first(5)
                glu_part(3, 4)
                outputs(7)
                channels_first(6)
                glu_part(4, 6)
                channels_first(7)
                glu_part(6, 8)
                pe.wait_ge(yy_done, NK)
                product(ph, 0, 1, 0, z_hi, z_lo)
                for a in (1, 0):
                    product(ph, 1, a, 0, z_hi, z_lo)
                with pe.Fori(1, ph.pairs) as i:
                    for j in range(2):
                        for a in (1, 0):
                            product(ph, j, a, i, z_hi, z_lo)

            for ph in PH:
                {"up": ffn_up, "down": down, "hgrn_in": hgrn, "hgrn_out": down, "glu": s5}[ph.kind](ph)

            pe.wait_ge(yn_done, NK)
            for c in range(CHUNKS + 1):
                n = P if c < CHUNKS else SAMPLE
                if c == 1:
                    pe.wait_ge(ssq_done, len(NORMS) * NK)
                    for d in range(CHUNKS):
                        M.matmul(ps[:, 4, d:d + 1], ssq[:, d * P:(d + 1) * P], ones[:, 0:1], start=True, stop=True)
                    M.matmul(ps[0:SAMPLE, 4, CHUNKS:CHUNKS + 1], ssq[:, SEQ:T], ones[:, 0:1], start=True, stop=True)\
                     .then_inc(rms_full, 1)
                if c == 3:
                    pe.wait_ge(rms_root, 1)
                if c == 4:
                    pe.wait_ge(y_low, 1)
                    pe.wait_ge(y_high, 1)
                for k in range(NK):
                    ins = turn(ps[0:n, Y_BANK[c] + k // 4, (k % 4) * P:(k % 4 + 1) * P], y_n[:, k, c * P:c * P + n])
                ins.then_inc(yt_full, 1)


_INS = ["x_prompt", "x_sample", "state_hgrn", "state_s5_re", "state_s5_im", "ln_ffn1", "ffn1_w_in", "ffn1_w_out",
        "ln_mix", "ln_ffn2", "ffn2_w_in", "ffn2_w_out", "hgrn_lb_logits", "hgrn_w_in", "hgrn_gnorm", "hgrn_w_out",
        "s5_a_re", "s5_a_im", "s5_log_dt", "s5_b_re", "s5_b_im", "s5_c_re", "s5_c_im", "s5_d", "s5_w_glu", "ln_final"]
_OUTS = [(1, SEQ, D_MODEL), (DEC_BATCH, DEC_SEQ, D_MODEL), (1, 1, HEADS, P, P), (1, 1, GROUPS, STATE),
         (1, 1, GROUPS, STATE), (1, DEC_BATCH, HEADS, P, P), (1, DEC_BATCH, GROUPS, STATE),
         (1, DEC_BATCH, GROUPS, STATE)]


def kernel(**inputs):
    import numpy as _np
    import concourse.bacc as _bacc
    from concourse import mybir as _mybir
    from concourse.bass_utils import run_bass_kernel_spmd as _run

    nc = _bacc.Bacc("TRN2", target_bir_lowering=False, num_devices=1)
    arrays, args = {}, []
    for name in _INS:
        a = _np.ascontiguousarray(inputs[name])
        arrays[f"in_{name}_dram"] = a
        args.append(nc.dram_tensor(f"in_{name}_dram", a.shape, _mybir.dt.from_np(a.dtype), kind="ExternalInput").ap())
    for i, shape in enumerate(_OUTS):
        args.append(nc.dram_tensor(f"out_{i}_dram", shape, F32, kind="ExternalOutput").ap())
    build_trunk(nc, *args)
    r = _run(nc, [arrays], core_ids=[0])
    return tuple(r.results[0][f"out_{i}_dram"] for i in range(len(_OUTS)))
```
